# Optimizing a Trainium2 kernel written in Bass

```python
import math
import jax
import jax.numpy as jnp
from jax import lax
import numpy as np

D_MODEL = 2048
BATCH = 1
SEQ = 128
DEPTH = 1
DEC_BATCH = 1
DEC_SEQ = 256
PAST_LEN = 128

GRID_W = 64
EPS = 1e-6
F32 = jnp.float32

SSD_HEADS = 16
SSD_HEADDIM = 64
SSD_INNER = SSD_HEADS * SSD_HEADDIM
SSD_GROUPS = 4
D_STATE = 64
CONV_W = 5
CHUNK = 128
XBC_DIM = SSD_INNER + 2 * SSD_GROUPS * D_STATE

N_HEADS = 16
KV_HEADS = 4
HEAD_DIM = 64
ATTN_INNER = N_HEADS * HEAD_DIM
KV_INNER = KV_HEADS * HEAD_DIM
Q_BLOCK = 128
ROPE_THETA = 10000.0

POOL_GROUPS = 4
POOL_INNER = 1024
POOL_GROUP_DIM = POOL_INNER // POOL_GROUPS
POOL_WINDOWS = (2, 4, 8, 16)

N_BRANCHES = 3

N_EXPERTS = 16
N_EXPERT_GROUPS = 4
EXPERTS_PER_GROUP = N_EXPERTS // N_EXPERT_GROUPS
TOP_K = 2
D_FF = 512

IN_SPLITS = (SSD_INNER, XBC_DIM, SSD_HEADS, SSD_HEADS, ATTN_INNER, KV_INNER, KV_INNER, POOL_INNER)
D_IN = SSD_INNER + XBC_DIM + 2 * SSD_HEADS + ATTN_INNER + 2 * KV_INNER + POOL_INNER + N_BRANCHES * D_MODEL

kernel_name = 'hybrid_dit_prefix_step'

def rms_norm(x, g):
    xf = x.astype(F32)
    y = xf * lax.rsqrt(jnp.mean(xf * xf, axis=-1, keepdims=True) + EPS)
    return (y * g).astype(x.dtype)

def modulate(x, gain, shift, scale):
    return rms_norm(x, gain) * (1 + scale[:, None, :]) + shift[:, None, :]

def axial_rope(n_tokens):
    rows = n_tokens // GRID_W
    row = jnp.repeat(jnp.arange(rows, dtype=F32), GRID_W)
    col = jnp.tile(jnp.arange(GRID_W, dtype=F32), rows)
    n_freq = HEAD_DIM // 4
    inv = ROPE_THETA ** (-jnp.arange(n_freq, dtype=F32) / n_freq)
    ang = jnp.concatenate([row[:, None] * inv, col[:, None] * inv], axis=-1)
    return jnp.cos(ang), jnp.sin(ang)

def apply_rope(x, cos, sin):
    xf = x.astype(F32).reshape(x.shape[:-1] + (HEAD_DIM // 2, 2))
    x1, x2 = xf[..., 0], xf[..., 1]
    c, s = cos[None, :, None, :], sin[None, :, None, :]
    out = jnp.stack([x1 * c - x2 * s, x1 * s + x2 * c], axis=-1)
    return out.reshape(x.shape).astype(x.dtype)

def gqa_attend(q, k, v):
    b, tq = q.shape[:2]
    nb = tq // Q_BLOCK
    qb = q.reshape(b, nb, Q_BLOCK, KV_HEADS, N_HEADS // KV_HEADS, HEAD_DIM).transpose(1, 0, 2, 3, 4, 5)
    scale = HEAD_DIM ** -0.5

    def block(qi):
        s = jnp.einsum('bqkgd,bskd->bkgqs', qi, k, preferred_element_type=F32) * scale
        p = jax.nn.softmax(s, axis=-1)
        return jnp.einsum('bkgqs,bskd->bqkgd', p.astype(v.dtype), v)

    o = lax.map(block, qb)
    return o.transpose(1, 0, 2, 3, 4, 5).reshape(b, tq, ATTN_INNER)

def centred_dwconv(x, w, bias):
    pad = CONV_W // 2
    y = lax.conv_general_dilated(x, w[:, None, :], window_strides=(1,), padding=((pad, pad),),
                                 dimension_numbers=('NWC', 'WIO', 'NWC'), feature_group_count=x.shape[-1])
    return y + bias

def segsum(a):
    t = a.shape[-1]
    x = jnp.broadcast_to(a[..., None], a.shape + (t,))
    x = jnp.where(jnp.tril(jnp.ones((t, t), bool), -1), x, 0)
    ss = jnp.cumsum(x, axis=-2)
    return jnp.where(jnp.tril(jnp.ones((t, t), bool)), ss, -jnp.inf)

def ssd_scan(x, dt, a_head, bm, cm, h0):
    b, L = x.shape[:2]
    nc = L // CHUNK
    xd = (x * dt[..., None]).reshape(b, nc, CHUNK, SSD_HEADS, SSD_HEADDIM)
    a = (dt * a_head).reshape(b, nc, CHUNK, SSD_HEADS).transpose(0, 3, 1, 2)
    bc = bm.reshape(b, nc, CHUNK, SSD_HEADS, D_STATE)
    cc = cm.reshape(b, nc, CHUNK, SSD_HEADS, D_STATE)
    a_cs = jnp.cumsum(a, axis=-1)
    lmat = jnp.exp(segsum(a))
    y_diag = jnp.einsum('bclhn,bcshn,bhcls,bcshp->bclhp', cc, bc, lmat, xd)
    decay_states = jnp.exp(a_cs[..., -1:] - a_cs)
    states = jnp.einsum('bclhn,bhcl,bclhp->bchpn', bc, decay_states, xd)
    states = jnp.concatenate([h0[:, None], states], axis=1)
    chunk_decay = jnp.exp(segsum(jnp.pad(a_cs[..., -1], ((0, 0), (0, 0), (1, 0)))))
    states = jnp.einsum('bhzc,bchpn->bzhpn', chunk_decay, states)
    y_off = jnp.einsum('bclhn,bchpn,bhcl->bclhp', cc, states[:, :-1], jnp.exp(a_cs))
    y = (y_diag + y_off).reshape(b, L, SSD_HEADS, SSD_HEADDIM)
    return y, states[:, -1]

def ssd_mixer(z, xbc, dt_f, dt_b, lp, h0_f, h0_b):
    b, L, _ = xbc.shape
    xbc = jax.nn.silu(centred_dwconv(xbc, lp['conv_w'], lp['conv_b']))
    xs, bg, cg = jnp.split(xbc, [SSD_INNER, SSD_INNER + SSD_GROUPS * D_STATE], axis=-1)
    xs = xs.reshape(b, L, SSD_HEADS, SSD_HEADDIM)
    rep = SSD_HEADS // SSD_GROUPS
    bh = jnp.repeat(bg.reshape(b, L, SSD_GROUPS, D_STATE), rep, axis=2)
    ch = jnp.repeat(cg.reshape(b, L, SSD_GROUPS, D_STATE), rep, axis=2)
    a_heads = -jnp.exp(lp['a_log'])
    dtf = jax.nn.softplus(dt_f + lp['dt_bias'][0])
    dtb = jax.nn.softplus(dt_b + lp['dt_bias'][1])
    y_f, hf = ssd_scan(xs, dtf, a_heads[0], bh, ch, h0_f)
    y_b, hb = ssd_scan(jnp.flip(xs, 1), jnp.flip(dtb, 1), a_heads[1], jnp.flip(bh, 1), jnp.flip(ch, 1), h0_b)
    y = y_f + jnp.flip(y_b, 1) + lp['d_skip'][:, None] * xs
    y = y.reshape(b, L, SSD_INNER) * jax.nn.silu(z)
    return rms_norm(y, lp['ssd_norm']), hf, hb

def multiscale_pool(p, w_grp, scale):
    b, L, _ = p.shape
    pg = p.reshape(b, L, POOL_GROUPS, POOL_GROUP_DIM)
    cs = jnp.cumsum(jnp.pad(pg.astype(F32), ((0, 0), (1, 0), (0, 0), (0, 0))), axis=1)
    t = jnp.arange(L)
    outs = []
    for g, w in enumerate(POOL_WINDOWS):
        lo = jnp.clip(t - w // 2, 0, L)
        hi = jnp.clip(t + (w - w // 2), 0, L)
        cnt = (hi - lo).astype(F32)
        outs.append((cs[:, hi, g] - cs[:, lo, g]) / cnt[None, :, None])
    pooled = jnp.stack(outs, axis=2).astype(p.dtype)
    y = jnp.einsum('blgd,gde->blge', pooled - pg, w_grp).reshape(b, L, POOL_INNER)
    return y * scale

def mixers(h, lp, h0_f, h0_b, rope, ctx_k, ctx_v):
    b, L, _ = h.shape
    offsets = [int(o) for o in np.cumsum(IN_SPLITS)]
    z, xbc, dt_f, dt_b, q, k, v, pin, gate_logits = jnp.split(h @ lp['w_in'], offsets, axis=-1)
    y_ssd, hf, hb = ssd_mixer(z, xbc, dt_f, dt_b, lp, h0_f, h0_b)
    q = rms_norm(q.reshape(b, L, N_HEADS, HEAD_DIM), lp['q_norm'])
    k = rms_norm(k.reshape(b, L, KV_HEADS, HEAD_DIM), lp['k_norm'])
    v = v.reshape(b, L, KV_HEADS, HEAD_DIM)
    if rope is None:
        k_all, v_all = k, v
    else:
        q = apply_rope(q, rope[0], rope[1])
        k = apply_rope(k, rope[0], rope[1])
        k_all = jnp.concatenate([k, ctx_k], axis=1)
        v_all = jnp.concatenate([v, ctx_v], axis=1)
    o_attn = gqa_attend(q, k_all, v_all)
    o_pool = multiscale_pool(pin, lp['pool_w'], lp['pool_scale'])
    g = jax.nn.sigmoid(gate_logits.reshape(b, L, N_BRANCHES, D_MODEL))
    merged = (g[:, :, 0] * (y_ssd @ lp['w_ssd_out'])
              + g[:, :, 1] * (o_attn @ lp['w_attn_out'])
              + g[:, :, 2] * (o_pool @ lp['w_pool_out']))
    return merged @ lp['w_out'], k, v, hf, hb

def moe_ffn(h, w_router, b_router, w_gate, w_up, w_down):
    b, L, _ = h.shape
    scores = jax.nn.sigmoid(jnp.einsum('bld,de->ble', h, w_router, preferred_element_type=F32))
    biased = scores + b_router.astype(F32)
    grouped = biased.reshape(b, L, N_EXPERT_GROUPS, EXPERTS_PER_GROUP)
    group_score = jnp.sum(lax.top_k(grouped, TOP_K)[0], axis=-1)
    best = jnp.argmax(group_score, axis=-1)
    in_group = (jnp.arange(N_EXPERTS) // EXPERTS_PER_GROUP)[None, None, :] == best[..., None]
    _, idx = lax.top_k(jnp.where(in_group, biased, -jnp.inf), TOP_K)
    sel = jnp.take_along_axis(scores, idx, axis=-1)
    wts = sel / jnp.sum(sel, axis=-1, keepdims=True)
    gate = jnp.sum(jax.nn.one_hot(idx, N_EXPERTS, dtype=F32) * wts[..., None], axis=-2).astype(h.dtype)
    a = jnp.einsum('bld,edf->blef', h, w_gate)
    u = jnp.einsum('bld,edf->blef', h, w_up)
    act = jax.nn.silu(a) * u * gate[..., None]
    return jnp.einsum('blef,efd->bld', act, w_down)

def setup_inputs(seed: int = 0) -> dict:
    key = jax.random.key(seed)
    ks = iter(jax.random.split(key, 40))

    def nrm(shape, scale):
        return jax.random.normal(next(ks), shape, F32) * scale

    def gain(shape):
        return 1.0 + nrm(shape, 0.02)

    dt0 = jnp.exp(jax.random.uniform(next(ks), (DEPTH, 2, SSD_HEADS), F32, math.log(1e-3), math.log(1e-1)))
    dt_bias = dt0 + jnp.log(-jnp.expm1(-dt0))
    a_log = jnp.log(jax.random.uniform(next(ks), (DEPTH, 2, SSD_HEADS), F32, 1.0, 16.0))
    return {
        'x_prompt': nrm((BATCH, SEQ, D_MODEL), 1.0),
        'x_sample': nrm((DEC_BATCH, DEC_SEQ, D_MODEL), 1.0),
        'cache_k': nrm((DEC_BATCH, DEPTH, PAST_LEN, KV_HEADS, HEAD_DIM), 1.0),
        'cache_v': nrm((DEC_BATCH, DEPTH, PAST_LEN, KV_HEADS, HEAD_DIM), 1.0),
        'state_ssd_fwd': nrm((DEC_BATCH, DEPTH, SSD_HEADS, SSD_HEADDIM, D_STATE), 0.1),
        'state_ssd_bwd': nrm((DEC_BATCH, DEPTH, SSD_HEADS, SSD_HEADDIM, D_STATE), 0.1),
        'c': nrm((DEC_BATCH, D_MODEL), 1.0),
        'c_ctx': nrm((D_MODEL,), 1.0),
        'w_ada': nrm((DEPTH, D_MODEL, 6 * D_MODEL), 0.5 * D_MODEL ** -0.5),
        'b_ada': nrm((DEPTH, 6 * D_MODEL), 0.02),
        'norm_mix': gain((DEPTH, D_MODEL)),
        'norm_ffn': gain((DEPTH, D_MODEL)),
        'w_in': nrm((DEPTH, D_MODEL, D_IN), D_MODEL ** -0.5),
        'conv_w': nrm((DEPTH, CONV_W, XBC_DIM), CONV_W ** -0.5),
        'conv_b': nrm((DEPTH, XBC_DIM), 0.01),
        'a_log': a_log,
        'dt_bias': dt_bias,
        'd_skip': 1.0 + nrm((DEPTH, SSD_HEADS), 0.1),
        'ssd_norm': gain((DEPTH, SSD_INNER)),
        'q_norm': gain((DEPTH, HEAD_DIM)),
        'k_norm': gain((DEPTH, HEAD_DIM)),
        'pool_w': nrm((DEPTH, POOL_GROUPS, POOL_GROUP_DIM, POOL_GROUP_DIM), POOL_GROUP_DIM ** -0.5),
        'pool_scale': gain((DEPTH, POOL_INNER)),
        'w_ssd_out': nrm((DEPTH, SSD_INNER, D_MODEL), SSD_INNER ** -0.5),
        'w_attn_out': nrm((DEPTH, ATTN_INNER, D_MODEL), ATTN_INNER ** -0.5),
        'w_pool_out': nrm((DEPTH, POOL_INNER, D_MODEL), POOL_INNER ** -0.5),
        'w_out': nrm((DEPTH, D_MODEL, D_MODEL), D_MODEL ** -0.5),
        'w_router': nrm((D_MODEL, N_EXPERTS), D_MODEL ** -0.5),
        'b_router': nrm((N_EXPERTS,), 0.01),
        'w_gate_ff': nrm((DEPTH, N_EXPERTS, D_MODEL, D_FF), D_MODEL ** -0.5),
        'w_up_ff': nrm((DEPTH, N_EXPERTS, D_MODEL, D_FF), D_MODEL ** -0.5),
        'w_down_ff': nrm((DEPTH, N_EXPERTS, D_FF, D_MODEL), D_FF ** -0.5),
        'norm_final': gain((D_MODEL,)),
    }

def reference(x_prompt, x_sample, cache_k, cache_v, state_ssd_fwd, state_ssd_bwd, c, c_ctx,
              w_ada, b_ada, norm_mix, norm_ffn, w_in, conv_w, conv_b, a_log, dt_bias, d_skip, ssd_norm,
              q_norm, k_norm, pool_w, pool_scale, w_ssd_out, w_attn_out, w_pool_out, w_out,
              w_router, b_router, w_gate_ff, w_up_ff, w_down_ff, norm_final):
    bp = x_prompt.shape[0]
    ls = x_sample.shape[1]
    rope = axial_rope(ls)
    zero_state = jnp.zeros((bp, SSD_HEADS, SSD_HEADDIM, D_STATE), x_prompt.dtype)
    cond_ctx = jax.nn.silu(c_ctx)[None]
    cond_lat = jax.nn.silu(c)
    xc, xl = x_prompt, x_sample
    ks, vs, hfs, hbs = [], [], [], []
    for l in range(DEPTH):
        lp = {'w_in': w_in[l], 'conv_w': conv_w[l], 'conv_b': conv_b[l], 'a_log': a_log[l],
              'dt_bias': dt_bias[l], 'd_skip': d_skip[l], 'ssd_norm': ssd_norm[l], 'q_norm': q_norm[l],
              'k_norm': k_norm[l], 'pool_w': pool_w[l], 'pool_scale': pool_scale[l],
              'w_ssd_out': w_ssd_out[l], 'w_attn_out': w_attn_out[l], 'w_pool_out': w_pool_out[l],
              'w_out': w_out[l]}
        mc = jnp.split(cond_ctx @ w_ada[l] + b_ada[l], 6, axis=-1)
        ml = jnp.split(cond_lat @ w_ada[l] + b_ada[l], 6, axis=-1)
        mix, k_c, v_c, hf, hb = mixers(modulate(xc, norm_mix[l], mc[0], mc[1]), lp, zero_state, zero_state,
                                       None, None, None)
        xc = xc + mc[2][:, None] * mix
        xc = xc + mc[5][:, None] * moe_ffn(modulate(xc, norm_ffn[l], mc[3], mc[4]), w_router, b_router,
                                           w_gate_ff[l], w_up_ff[l], w_down_ff[l])
        ks.append(k_c)
        vs.append(v_c)
        hfs.append(hf)
        hbs.append(hb)
        mix, _, _, _, _ = mixers(modulate(xl, norm_mix[l], ml[0], ml[1]), lp, state_ssd_fwd[:, l],
                                 state_ssd_bwd[:, l], rope, cache_k[:, l], cache_v[:, l])
        xl = xl + ml[2][:, None] * mix
        xl = xl + ml[5][:, None] * moe_ffn(modulate(xl, norm_ffn[l], ml[3], ml[4]), w_router, b_router,
                                           w_gate_ff[l], w_up_ff[l], w_down_ff[l])
    y_prompt = rms_norm(xc, norm_final)
    y_sample = rms_norm(xl, norm_final)
    new_cache_k = jnp.stack(ks, axis=1)
    new_cache_v = jnp.stack(vs, axis=1)
    new_state_ssd_fwd = jnp.stack(hfs, axis=1)
    new_state_ssd_bwd = jnp.stack(hbs, axis=1)
    return (y_prompt, y_sample, new_cache_k, new_cache_v, new_state_ssd_fwd, new_state_ssd_bwd)


_drawn_inputs = setup_inputs


def setup_inputs(seed=0):
    import zlib

    import numpy as np

    out = dict(_drawn_inputs(seed))
    spreads = {}
    factors = {'cache_k': 26.784,
     'cache_v': 29.104,
     'conv_b': 3.257,
     'ssd_norm': 18.862,
     'q_norm': 8.0,
     'k_norm': 8.633,
     'pool_scale': 19.007,
     'norm_final': 20.046,
     'norm_ffn': 4.246}
    for name, (base, spread) in spreads.items():
        noise = np.random.default_rng([zlib.crc32(name.encode()), seed]).standard_normal(out[name].shape)
        drawn = base * np.exp(spread * noise) if base else spread * noise
        out[name] = jnp.asarray(drawn.astype(out[name].dtype))
    for name, factor in factors.items():
        out[name] = (out[name] * factor).astype(out[name].dtype)
    return out
```

```python
import contextlib

import concourse.bass as bass
from concourse import mybir
from concourse.bass import ds
import numpy as np

F32 = mybir.dt.float32
F32R = mybir.dt.float32r
I32 = mybir.dt.int32
ACT = mybir.ActivationFunctionType
ALU = mybir.AluOpType
AX = mybir.AxisListType.X

P = 128
D = 2048
KB = D // P
T_CTX, T_LAT, T_PAST = 128, 256, 128
T = T_CTX + T_LAT
SEG = ((0, T_CTX), (T_CTX, T))
EPS = 1e-6
GRID_W = 64
HEADS, KV, HD = 16, 4, 64
SSD_H, SSD_G = 16, 4
NCH = T // P
POOL_WINDOWS = (2, 4, 8, 16)
NE, NG = 16, 4
DFF = 512

TILE = 1024
R = 4
LEAD = 2
ADA_BODY = KB // 2
ADA_FIRST, ADA_CHUNKS = 2 * D // 512, 6 * D // 512
SSD_BLOCKS, ATT_BLOCKS, POOL_BLOCKS = 20, 12, 8
MERGE_TILES = 3 * KB

Q_HEADS = [h for j in range(8) for h in (8 * (j // 4) + j % 4, 8 * (j // 4) + 4 + j % 4)]


class Steps:

    def __init__(self, eng, sem):
        self.eng, self.sem, self.n, self.i, self.per = eng, sem, 0, None, 0

    def did(self, ins):
        ins.then_inc(self.sem, 1)
        self.n += 1

    def wait(self):
        self.eng.wait_ge(self.sem, self.n if self.i is None else self.i * self.per + self.n)

    def chain(self, ins):
        self.did(ins)
        self.wait()

    def enter(self, i, per):
        self.i, self.per, self.start = i, per, self.n

    def leave(self, iters):
        assert self.n - self.start == self.per, (self.sem, self.n - self.start)
        self.n, self.i = self.start + self.per * iters, None


def rsqrt_steps(dve, nc, st, v, y, t):
    st.chain(nc.vector.tensor_scalar(y.bitcast(I32), v.bitcast(I32), 1, None, ALU.logical_shift_right))
    st.chain(nc.vector.tensor_scalar(y.bitcast(I32), y.bitcast(I32), -1.0, float(0x5F3759DF), ALU.mult, ALU.add))
    for _ in range(4):
        st.chain(nc.vector.tensor_tensor(t, y, y, ALU.mult))
        st.chain(nc.vector.scalar_tensor_tensor(out=t, in0=t, scalar=-0.5, in1=v, op0=ALU.mult, op1=ALU.mult))
        st.chain(nc.vector.scalar_tensor_tensor(out=y, in0=t, scalar=1.5, in1=y, op0=ALU.add, op1=ALU.mult))


class Net:

    def __init__(self, nc, io):
        self.nc, self.io = nc, io
        self.at = (nc.sbuf_base + 63) // 32 * 32
        sb = self.keep
        self.ident = sb("ident", [P, P], F32)
        self.ones = sb("ones", [P, P], F32)
        self.mods = sb("mods", [P, 96, 2], F32)
        self.gains = sb("gains", [P, 4, KB], F32)
        self.mod_a = sb("mod_a", [P, KB, 2], F32)
        self.half_gate = sb("half_gate", [P, KB, 2], F32)
        self.rstd = sb("rstd", [P, T], F32)
        self.rs_v = sb("rs_v", [P, T], F32)
        self.rs_t = sb("rs_t", [P, T], F32)
        self.hhi = sb("hhi", [P, KB, T], F32R)
        self.hlo = sb("hlo", [P, KB, T], F32R)
        self.merged = sb("merged", [P, KB, T], F32)
        self.raw = sb("raw", [P, R, TILE], F32)
        self.whi = sb("whi", [P, R, TILE], F32R)
        self.wlo = sb("wlo", [P, R, TILE], F32R)
        self.arena = self.at
        self.bank = [nc.alloc_psum_tensor(f"bank{i}", [P, 512], F32) for i in range(8)]
        self.landed = [nc.alloc_semaphore(f"tile_landed{i}") for i in range(R)]
        self.hi_done = nc.alloc_semaphore("tile_hi_done")
        self.lo_done = nc.alloc_semaphore("tile_lo_done")
        self.dve_steps = Steps(None, nc.alloc_semaphore("dve_steps"))
        self.used = nc.alloc_semaphore("tile_used")
        self.tile0 = 0
        self.src, self.src0 = io.dense, 0

    def keep(self, name, shape, dt):
        t = self.nc.alloc_sbuf_tensor_at(name, shape, dt, offset=self.at)
        self.at += (int(np.prod(shape[1:])) * 4 + 31) // 32 * 32
        assert self.at <= self.nc.sbuf_usable_end, (name, self.at - self.nc.sbuf_usable_end)
        return t

    def steps(self, dve):
        self.dve_steps.eng = dve
        return self.dve_steps

    def sem(self, name):
        return self.nc.alloc_semaphore(name)

    def sp_start(self, sp):
        for t in range(R):
            sp.dma_start(self.raw[:, t, :], self.src[t]).then_inc(self.landed[t], 16)

    def sp_tile(self, sp, i, body, t):
        n = i * body + (self.tile0 + t)
        sp.wait_ge(self.lo_done, n + 1)
        sp.dma_start(self.raw[:, t % R, :], self.src[ds(n + (R - self.src0), 1)].rearrange("a p c -> p (a c)"))\
            .then_inc(self.landed[t % R], 16)

    def sp_tiles(self, sp, iters, body):
        with sp.Fori(0, iters) as i:
            for t in range(body):
                self.sp_tile(sp, i, body, t)

    def act_hi(self, act, i, body, t):
        s, n = (t + LEAD) % R, i * body + (self.tile0 + t + LEAD)
        act.wait_ge(self.landed[s], i * (16 * body // R) + 16 * (self.tile0 // R + (t + LEAD) // R + 1))
        act.wait_ge(self.used, n + 1)
        self.nc.scalar.activation(self.whi[:, s, :], self.raw[:, s, :], ACT.Copy).then_inc(self.hi_done, 1)

    def dve_lo(self, dve, i, body, t):
        s, n = (t + LEAD) % R, i * body + (self.tile0 + t + LEAD)
        dve.wait_ge(self.hi_done, n + 1)
        self.nc.vector.tensor_tensor(self.wlo[:, s, :], self.raw[:, s, :], self.whi[:, s, :].bitcast(F32),
                                     ALU.subtract).then_inc(self.lo_done, 1)

    def pe_tile(self, pe, i, body, t, out, xhi, xlo, k0, blocks):
        s = t % R
        pe.wait_ge(self.lo_done, i * body + (self.tile0 + t + 1))
        for kk in range(8):
            k, c = k0 + kk, slice(kk * P, kk * P + P)
            self.nc.tensor.matmul(out, self.whi[:, s, c], xhi[:, k, :], start=(k == 0), stop=False)
            self.nc.tensor.matmul(out, self.whi[:, s, c], xlo[:, k, :], start=False, stop=False)
            last = self.nc.tensor.matmul(out, self.wlo[:, s, c], xhi[:, k, :], start=False, stop=(k == blocks - 1))
        last.then_inc(self.used, 1)

    def tiles_done(self, i, body, t):
        return i * body + (self.tile0 + t + 1 + R)


def ada_phase(N):
    nc, io, body, chunks = N.nc, N.io, ADA_BODY, ADA_FIRST
    N.at = N.arena
    xt = N.keep("x_mix", [P, KB, T], F32)
    N.xt = xt
    cond = N.keep("cond", [P, KB, 2], F32)
    ctanh = N.keep("cond_tanh", [P, KB, 2], F32)
    csilu = N.keep("cond_silu", [P, KB, 2], F32)
    cst = N.keep("cond_parts", [P, KB, P], F32R)
    rows = N.keep("ada_rows", [P, 2, 512], F32)
    four = N.keep("ada_four", [P, 2, 4, 4], F32)
    bada = N.keep("b_ada_sb", [P, 96], F32)
    sq = N.keep("x_squares", [P, 2, 4, T], F32)
    sem = N.sem
    loaded, s_tanh, s_silu, s_chi, s_clo, s_zero = [sem("ada_" + n) for n in ("loaded", "tanh", "silu", "chi", "clo", "zero")]
    consts_in, x_in = sem("consts_in"), sem("x_in")
    s_sq, s_sqsum, s_row, s_tr, s_four, s_add = [
        sem("ada_" + n) for n in ("squares", "sqsum", "row", "tr", "four", "add")]
    N.ada_sems = loaded, s_zero, s_tanh, s_silu, s_chi, s_clo, s_row, s_tr, s_four, s_add
    with nc.Block() as block:
        @block.sync
        def _(sp):
            sp.dma_start(cond[:, :, :], io.cond).then_inc(loaded, 16)
            sp.dma_start(N.ident[:, :], io.ident).then_inc(consts_in, 16)
            sp.dma_start(N.gains[:, :, :], io.gains).then_inc(consts_in, 16)
            sp.dma_start(bada[:, :], io.b_ada).then_inc(consts_in, 16)
            N.sp_start(sp)
            sp.dma_start(xt[:, :, :], io.x).then_inc(x_in, 16)
            N.sp_tiles(sp, chunks, body)

        @block.gpsimd
        def _(pool):
            nc.gpsimd.memset(cst[:, :, :].bitcast(F32), 0.0).then_inc(s_zero, 1)
            nc.gpsimd.memset(N.ones[:, :], 1.0).then_inc(s_zero, 1)

        @block.scalar
        def _(act):
            nc.scalar.sem_inc(s_four, 1)
            act.wait_ge(loaded, 16)
            nc.scalar.activation(ctanh[:, :, :], cond[:, :, :], ACT.Tanh, scale=0.5).then_inc(s_tanh, 1)
            for t in range(-LEAD, 0):
                N.act_hi(act, 0, body, t)
            act.wait_ge(s_silu, 1)
            act.wait_ge(s_zero, 1)
            nc.scalar.activation(cst[:, :, 0:2], csilu[:, :, :], ACT.Copy).then_inc(s_chi, 1)
            act.wait_ge(x_in, 16)
            for b in range(4):
                if b >= 2:
                    act.wait_ge(s_sqsum, b - 1)
                nc.scalar.activation(sq[:, b % 2], xt[:, 4 * b:4 * b + 4, :], ACT.Square).then_inc(s_sq, 1)

            def chunk(i, first):
                for t in range(body):
                    N.act_hi(act, i, body, t)
                    if t == 1 and not first:
                        act.wait_ge(s_tr, i)
                        nc.scalar.activation(four[:, 0], N.bank[6][:, :].rearrange("p (a b) -> p a b", a=4)[:, :, 0:4],
                                             ACT.Copy).then_inc(s_four, 1)
                act.wait_ge(N.used, N.tiles_done(i, body, body - 1))
                nc.scalar.activation(rows[:, 0, :], N.bank[0][:, :], ACT.Copy).then_inc(s_row, 1)
            chunk(0, True)
            with act.Fori(1, chunks) as i:
                chunk(i, False)
            act.wait_ge(s_tr, chunks)
            nc.scalar.activation(four[:, 0], N.bank[6][:, :].rearrange("p (a b) -> p a b", a=4)[:, :, 0:4],
                                 ACT.Copy).then_inc(s_four, 1)

        @block.vector
        def _(dve):
            st = N.steps(dve)
            dve.wait_ge(s_tanh, 1)
            st.chain(nc.vector.scalar_tensor_tensor(out=csilu[:, :, :], in0=ctanh[:, :, :], scalar=1.0, in1=cond[:, :, :],
                                                    op0=ALU.add, op1=ALU.mult))
            nc.vector.tensor_scalar(csilu[:, :, :], csilu[:, :, :], 0.5, None, ALU.mult).then_inc(s_silu, 1)
            for t in range(-LEAD, 0):
                N.dve_lo(dve, 0, body, t)
            dve.wait_ge(s_silu, 1)
            dve.wait_ge(s_chi, 1)
            nc.vector.tensor_tensor(cst[:, :, 2:4], csilu[:, :, :], cst[:, :, 0:2].bitcast(F32), ALU.subtract)\
                .then_inc(s_clo, 1)

            def chunk(i, first):
                for t in range(body):
                    N.dve_lo(dve, i, body, t)
                    if t == 3 and not first:
                        dve.wait_ge(s_four, i + 1)
                        nc.vector.tensor_tensor(N.mods[:, ds(i * 4 - 4, 4), :], four[:, 0, :, 0:2], four[:, 0, :, 2:4],
                                                ALU.add).then_inc(s_add, 1)
            chunk(0, True)
            dve.wait_ge(s_sqsum, 4)
            st.chain(nc.vector.tensor_scalar(N.rs_v[:, :], N.bank[7][:, 0:T], 1.0 / D, EPS, ALU.mult, ALU.add))
            rsqrt_steps(dve, nc, st, N.rs_v[:, :], N.rstd[:, :], N.rs_t[:, :])
            with dve.Fori(1, chunks) as i:
                chunk(i, False)
            dve.wait_ge(s_four, chunks + 1)
            dve.wait_ge(consts_in, 48)
            nc.vector.tensor_tensor(N.mods[:, 4 * chunks - 4:4 * chunks, :], four[:, 0, :, 0:2], four[:, 0, :, 2:4], ALU.add).then_inc(s_add, 1)
            dve.wait_ge(s_add, chunks)
            done = slice(0, 4 * chunks)
            st.chain(nc.vector.tensor_tensor(N.mods[:, done, :], N.mods[:, done, :],
                                             bada[:, done].unsqueeze(2).to_broadcast([P, 4 * chunks, 2]), ALU.add))

        @block.tensor
        def _(pe):
            nc.tensor.sem_inc(N.used, R)
            pe.wait_ge(s_zero, 2)
            for b in range(4):
                pe.wait_ge(s_sq, b + 1)
                for k in range(4):
                    last = nc.tensor.matmul(N.bank[7][:, 0:T], N.ones[:, :], sq[:, b % 2, k, :],
                                            start=(b + k == 0), stop=(b * 4 + k == KB - 1))
                last.then_inc(s_sqsum, 1)
            pe.wait_ge(s_clo, 1)
            pe.wait_ge(consts_in, 48)

            def transposes(i):
                pe.wait_ge(s_row, i)
                pe.wait_ge(s_four, i)
                for q in range(4):
                    last = nc.tensor.transpose(N.bank[6][:, q * P:q * P + P], rows[:, 0, q * P:q * P + P], N.ident[:, :])
                last.then_inc(s_tr, 1)

            def chunk(i, first):
                for t in range(body):
                    pe.wait_ge(N.lo_done, i * body + (N.tile0 + t + 1))
                    if t == 0 and not first:
                        pe.wait_ge(s_row, i)
                    for kk in range(2):
                        k, c = 2 * t + kk, slice(kk * 512, kk * 512 + 512)
                        nc.tensor.matmul(N.bank[0][:, :], cst[:, k, :], N.whi[:, t % R, c], start=(k == 0), stop=False)
                        last = nc.tensor.matmul(N.bank[0][:, :], cst[:, k, :], N.wlo[:, t % R, c],
                                                start=False, stop=(k == KB - 1))
                    last.then_inc(N.used, 1)
                    if t == 1 and not first:
                        transposes(i)
            chunk(0, True)
            with pe.Fori(1, chunks) as i:
                chunk(i, False)
            transposes(chunks)
    N.tile0 += chunks * body


def modulate_phase(N, part, gain, name):
    nc = N.nc
    tmp = N.keep("mod_tmp" + name, [P, 4, T], F32)
    s_a, s_t, s_hi, s_lo = [N.sem(name + n) for n in ("_a", "_t", "_hi", "_lo")]
    with nc.Block() as block:
        @block.vector
        def _(dve):
            st = N.steps(dve)
            scale = N.mods[:, (part + 1) * KB:(part + 2) * KB, :]
            st.chain(nc.vector.scalar_tensor_tensor(
                out=N.mod_a[:, :, :], in0=scale, scalar=1.0,
                in1=N.gains[:, gain, :].unsqueeze(2).to_broadcast([P, KB, 2]), op0=ALU.add, op1=ALU.mult))

            def low(k):
                dve.wait_ge(s_hi, 2 * k + 2)
                for g, (a, b) in enumerate(SEG):
                    nc.vector.scalar_tensor_tensor(
                        out=N.hlo[:, k, a:b], in0=tmp[:, k % 4, a:b], scalar=N.mods[:, part * KB + k, g:g + 1],
                        in1=N.hhi[:, k, a:b].bitcast(F32), op0=ALU.add, op1=ALU.subtract).then_inc(s_lo, 1)
            for k in range(KB):
                if k >= 4:
                    dve.wait_ge(s_lo, 2 * k - 6)
                for g, (a, b) in enumerate(SEG):
                    nc.vector.scalar_tensor_tensor(
                        out=tmp[:, k % 4, a:b], in0=N.xt[:, k, a:b], scalar=N.mod_a[:, k, g:g + 1],
                        in1=N.rstd[:, a:b], op0=ALU.mult, op1=ALU.mult).then_inc(s_t, 1)
                if k >= 2:
                    low(k - 2)
            low(KB - 2)
            low(KB - 1)

        @block.scalar
        def _(act):
            for k in range(KB):
                act.wait_ge(s_t, 2 * k + 2)
                for g, (a, b) in enumerate(SEG):
                    nc.scalar.activation(N.hhi[:, k, a:b], tmp[:, k % 4, a:b], ACT.Identity,
                                         bias=N.mods[:, part * KB + k, g:g + 1], scale=1.0).then_inc(s_hi, 1)


def start_credits(N):
    N.evac, N.blk0 = N.sem("block_evacuated"), 0
    N.gate_read, N.out_read, N.m0 = N.sem("gate_bank_read"), N.sem("out_bank_read"), 0
    with N.nc.Block() as block:
        @block.scalar
        def _(act):
            N.nc.scalar.sem_inc(N.evac, 2)
            N.nc.scalar.sem_inc(N.gate_read, 2)

        @block.vector
        def _(dve):
            N.nc.vector.sem_inc(N.out_read, 2)


def pe_blocks(N, pe, iters):
    with pe.Fori(0, iters) as i:
        for t in range(4):
            if t % 2 == 0:
                pe.wait_ge(N.evac, i * 2 + (N.blk0 + t // 2 + 1))
            N.pe_tile(pe, i, 4, t, N.bank[t // 2][:, 0:T], N.hhi, N.hlo, 8 * (t % 2), KB)


def ssd_in_phase(N):
    nc, io = N.nc, N.io
    N.at = N.arena
    S = N.S = {}
    S["z"] = z = N.keep("ssd_z", [P, 8, T], F32)
    S["xs_at"] = N.at
    S["xs"] = xs = N.keep("ssd_xbc", [P, 12, T], F32)
    S["d"] = dskip = N.keep("d_skip_sb", [P, 8], F32)
    S["end1"] = N.at
    PADW = T + 8
    pad = N.keep("xbc_padded", [P, 2, PADW], F32)
    acc = N.keep("conv_sums", [P, 2, PADW - 4], F32)
    th = N.keep("conv_tanh", [P, 2, PADW - 4], F32)
    cw = N.keep("conv_weights", [P, 12, 6], F32)
    wdt = N.keep("w_dt_raw", [P, KB, 32], F32)
    wdh = N.keep("w_dt_hi", [P, KB, P], F32R)
    wdl = N.keep("w_dt_lo", [P, KB, P], F32R)
    sem = N.sem
    s_ld, s_zero, s_dhi, s_dlo, s_dt = [sem("sin_" + n) for n in ("loads", "zero", "dthi", "dtlo", "dt")]
    s_conv, s_fin, s_tanh, s_z, s_zt = [sem("sin_" + n) for n in ("conv", "xs", "tanh", "z", "ztanh")]
    t0 = N.tile0
    with nc.Block() as block:
        @block.sync
        def _(sp):
            sp.dma_start(wdt[:, :, :], io.w_dt).then_inc(s_ld, 16)
            sp.dma_start(cw[:, :, :], io.conv).then_inc(s_ld, 16)
            sp.dma_start(dskip[:, :], io.d_skip).then_inc(s_ld, 16)
            N.sp_tiles(sp, 6, 4)
            N.tile0 += 24
            N.sp_tiles(sp, 4, 4)
            N.tile0 = t0
            sp.wait_ge(s_ld, 48)

        @block.gpsimd
        def _(pool):
            nc.gpsimd.memset(wdh[:, :, :].bitcast(F32), 0.0).then_inc(s_zero, 1)
            nc.gpsimd.memset(wdl[:, :, :].bitcast(F32), 0.0).then_inc(s_zero, 1)
            nc.gpsimd.memset(pad[:, :, :], 0.0).then_inc(s_zero, 1)

        @block.scalar
        def _(act):
            act.wait_ge(s_ld, 48)
            act.wait_ge(s_zero, 3)
            nc.scalar.activation(wdh[:, :, 0:32], wdt[:, :, :], ACT.Copy).then_inc(s_dhi, 1)
            with act.Fori(0, 6) as i:
                for t in range(4):
                    N.act_hi(act, i, 4, t)
                    if t % 2 == 1:
                        b = t // 2
                        act.wait_ge(s_conv, i * 2 + (b + 1))
                        act.wait_ge(N.used, N.tiles_done(i, 4, t))
                        nc.scalar.activation(pad[:, b, 2:2 + T_CTX], N.bank[b][:, 0:T_CTX], ACT.Copy)
                        nc.scalar.activation(pad[:, b, 6 + T_CTX:6 + T], N.bank[b][:, T_CTX:T], ACT.Copy)\
                            .then_inc(N.evac, 1)
                    if t >= 2:
                        b = t - 2
                        act.wait_ge(s_conv, i * 2 + (b + 3))
                        nc.scalar.activation(th[:, b, :], acc[:, b, :], ACT.Tanh, scale=0.5).then_inc(s_tanh, 1)
            N.tile0 += 24
            act.wait_ge(s_fin, 4 + 24)
            with act.Fori(0, 4) as i:
                for t in range(4):
                    N.act_hi(act, i, 4, t)
                    if t % 2 == 1:
                        b = t // 2
                        act.wait_ge(s_z, i * 2 + (b + 1))
                        act.wait_ge(N.used, N.tiles_done(i, 4, t))
                        nc.scalar.activation(th[:, b, 0:T], N.bank[b][:, 0:T], ACT.Tanh, scale=0.5).then_inc(s_zt, 1)
                        nc.scalar.activation(z[:, ds(i * 2 + b, 1), :].rearrange("p a c -> p (a c)"), N.bank[b][:, 0:T],
                                             ACT.Copy).then_inc(N.evac, 1)
            N.tile0 = t0

        @block.vector
        def _(dve):
            nc.vector.sem_inc(s_conv, 2)
            nc.vector.sem_inc(s_z, 2)
            nc.vector.sem_inc(s_fin, 4)
            dve.wait_ge(s_dhi, 1)
            nc.vector.tensor_tensor(wdl[:, :, 0:32], wdt[:, :, :], wdh[:, :, 0:32].bitcast(F32), ALU.subtract)\
                .then_inc(s_dlo, 1)
            st = N.steps(dve)
            with dve.Fori(0, 6) as i:
                st.enter(i, 10)
                for t in range(4):
                    N.dve_lo(dve, i, 4, t)
                    if t % 2 == 1:
                        b = t // 2
                        dve.wait_ge(N.evac, i * 2 + (N.blk0 + b + 3))
                        dve.wait_ge(s_fin, i * 4 + (2 * b + 2))
                        w = lambda k: cw[:, ds(i * 2 + b, 1), k:k + 1].rearrange("p a c -> p (a c)")
                        st.chain(nc.vector.tensor_scalar(acc[:, b, :], pad[:, b, 0:T + 4], w(0), w(5), ALU.mult, ALU.add))
                        for k in range(1, 5):
                            ins = nc.vector.scalar_tensor_tensor(out=acc[:, b, :], in0=pad[:, b, k:k + T + 4], scalar=w(k),
                                                                 in1=acc[:, b, :], op0=ALU.mult, op1=ALU.add)
                            if k < 4:
                                st.chain(ins)
                            else:
                                ins.then_inc(s_conv, 1)
                    if t >= 2:
                        b = t - 2
                        dve.wait_ge(s_tanh, i * 2 + (b + 1))
                        st.chain(nc.vector.tensor_scalar(th[:, b, :], th[:, b, :], 0.5, 0.5, ALU.mult, ALU.add))
                        for (o, (lo, hi)) in zip((0, 4), SEG):
                            nc.vector.tensor_tensor(
                                xs[:, ds(i * 2 + b, 1), lo:hi].rearrange("p a c -> p (a c)"),
                                acc[:, b, lo + o:hi + o], th[:, b, lo + o:hi + o], ALU.mult).then_inc(s_fin, 1)
                st.leave(6)
            N.tile0 += 24
            with dve.Fori(0, 4) as i:
                for t in range(4):
                    N.dve_lo(dve, i, 4, t)
                    if t % 2 == 1:
                        b = t // 2
                        dve.wait_ge(N.evac, i * 2 + (N.blk0 + 12 + b + 3))
                        zb = z[:, ds(i * 2 + b, 1), :].rearrange("p a c -> p (a c)")
                        nc.vector.scalar_tensor_tensor(out=zb, in0=th[:, b, 0:T], scalar=1.0, in1=zb,
                                                       op0=ALU.add, op1=ALU.mult).then_inc(s_z, 1)
            N.tile0 = t0

        @block.tensor
        def _(pe):
            pe.wait_ge(s_dlo, 1)
            for k in range(KB):
                nc.tensor.matmul(N.bank[7][:, 0:T], wdh[:, k, :], N.hhi[:, k, :], start=(k == 0), stop=False)
                nc.tensor.matmul(N.bank[7][:, 0:T], wdh[:, k, :], N.hlo[:, k, :], start=False, stop=False)
                last = nc.tensor.matmul(N.bank[7][:, 0:T], wdl[:, k, :], N.hhi[:, k, :], start=False, stop=(k == KB - 1))
            last.then_inc(s_dt, 1)
            pe_blocks(N, pe, 6)
            N.tile0, N.blk0 = N.tile0 + 24, N.blk0 + 12
            pe_blocks(N, pe, 4)
            N.tile0, N.blk0 = t0, N.blk0 - 12
            pe.wait_ge(s_dt, 1)
    N.tile0 += 40
    N.blk0 += 20


def ssd_scan_phase(N):
    nc, io, S = N.nc, N.io, N.S
    z, xs, dskip = S["z"], S["xs"], S["d"]
    N.at = S["end1"]
    sem = N.sem
    xtok = N.keep("x_tok", [P, NCH, 1024], F32)
    btok = N.keep("B_tok", [P, NCH, 256], F32)
    h0 = N.keep("h0", [P, 2, 2, 256], F32)
    s1 = N.keep("mid_state", [P, 256], F32)
    cbm = N.keep("CB_masked", [P, 2, T], F32)
    stout = N.keep("ctx_states", [P, 2, 2, 256], F32)
    tri = N.keep("tri", [P, 2, P], F32)
    wt = N.keep("decay_w", [P, 4, 2], F32)
    dttok = N.keep("dt_tok", [P, NCH, 32], F32)
    cstok = N.keep("cs_tok", [P, NCH, 32], F32)
    aexp = N.keep("a_exp", [P, 32], F32)
    dbias = N.keep("dt_bias_sb", [32, 1], F32)
    ec = N.keep("C_decayed", [P, 4, T_LAT], F32)
    xd = N.keep("x_dt", [P, NCH, 256], F32)
    xdd = N.keep("x_dt_decay", [P, 2, 256], F32)
    csb_at = N.at
    csb = N.keep("cs_rows_bc", [P, 2, 4, T], F32)
    N.at = csb_at
    dv, du, ds_, dq, dp, dr, dsp = [N.keep("dt_" + n, [32, T], F32) for n in ("v", "u", "s", "q", "p", "r", "sp")]
    rows_f, rows_b = N.rs_t, N.rs_v
    N.at = S["xs_at"]
    S["hi"] = ohi = N.keep("ssd_out_hi", [P, 8, T], F32R)
    S["lo"] = olo = N.keep("ssd_out_lo", [P, 8, T], F32R)
    (s_ld, s_v, s_abs, s_exp, s_dtr, s_tp, s_dttok, s_aexp, s_atok, s_cs, s_cstok, s_rows, s_rowst, s_x2t, s_xtok) = [
        sem("sc_" + n) for n in ("loads", "v", "abs", "exp", "dtr", "dtT", "dttok", "aexp", "atok", "cs", "cstok",
                                 "rows", "rows_stored", "xT", "xtok")]
    s_csb = [sem("sc_csb0"), sem("sc_csb1")]
    (s_cb, s_cbm, s_ec, s_wsub, s_wexp, s_xd, s_xdd, s_st, s_s1, s_stout, s_cd, s_d, s_dexp, s_m, s_y, s_gated, s_sq, s_sqs,
     s_norm, s_ohi, s_olo, s_sto) = [
        sem("sc_" + n) for n in ("cb", "cbm", "ec", "wsub", "wexp", "xd", "xdd", "st", "s1", "stout", "cd", "d", "dexp", "m",
                                 "y", "gated", "sq", "sqs", "norm", "ohi", "olo", "states_out")]
    B = N.bank
    steps = [(g, dr_) for g in range(SSD_G) for dr_ in range(2)]
    MID, END, NEXT = (1, 2), (127, 128), (2, 1)

    def ybank(g, pp):
        return B[2 + 2 * (g % 2) + pp]

    with nc.Block() as block:
        @block.sync
        def _(sp):
            sp.dma_start(dbias[:, :], io.dt_bias).then_inc(s_ld, 16)
            sp.dma_start(aexp[:, :], io.a_log.partition_broadcast(P)).then_inc(s_ld, 16)
            sp.dma_start(tri[:, :, :], io.tri).then_inc(s_ld, 16)
            sp.dma_start(h0[:, :, :, :], io.h0).then_inc(s_ld, 16)
            sp.wait_ge(s_rows, 2)
            sp.dma_start(io.scratch[0:16, :], rows_f[0:16, :]).then_inc(s_rowst, 16)
            sp.dma_start(io.scratch[16:32, :], rows_b[16:32, :]).then_inc(s_rowst, 16)
            sp.wait_ge(s_rowst, 32)
            for n, (g, d) in enumerate(steps):
                if n >= 2:
                    sp.wait_ge(s_y, n - 1)
                r0 = 16 * d + 4 * g
                sp.dma_start(csb[:, n % 2].rearrange("p a c -> p (a c)"),
                             io.scratch[r0:r0 + 4, :].rearrange("a c -> (a c)").partition_broadcast(P))\
                    .then_inc(s_csb[n % 2], 16)
            sp.wait_ge(s_stout, 8)
            sp.dma_start(io.states, stout[:, :, :, :]).then_inc(s_sto, 16)
            sp.wait_ge(s_sto, 16)
            sp.wait_ge(s_ld, 64)

        @block.tensor
        def _(pe):
            for f in range(6):
                for q in range(4):
                    last = nc.tensor.transpose(B[f][:, q * P:q * P + P], xs[:, 4 * (f % 2) + q, (f // 2) * P:(f // 2 + 1) * P],
                                               N.ident[:, :])
                last.then_inc(s_x2t, 1)
            for f in range(2):
                pe.wait_ge(s_xtok, f + 1)
                for q in range((4, 2)[f]):
                    c, b = (2 * f + q // 2), 8 + q % 2
                    last = nc.tensor.transpose(B[f][:, q * P:q * P + P], xs[:, b, c * P:(c + 1) * P], N.ident[:, :])
                last.then_inc(s_x2t, 1)
            pe.wait_ge(s_dtr, 1)
            for c in range(NCH):
                last = nc.tensor.transpose(B[6][:, c * 32:c * 32 + 32], dsp[:, c * P:(c + 1) * P], N.ident[0:32, 0:32])
            last.then_inc(s_tp, 1)
            pe.wait_ge(s_atok, 1)
            pe.wait_ge(s_ld, 64)
            pe.wait_ge(s_xtok, 8)
            for c in range(NCH):
                for d in range(2):
                    last = nc.tensor.matmul(B[6][:, 128 + c * 32 + 16 * d:128 + c * 32 + 16 * d + 16], tri[:, d, :],
                                            cstok[:, c, 16 * d:16 * d + 16], start=True, stop=True)
            last.then_inc(s_cs, 1)
            for d in range(2):
                for c in range(NCH):
                    last = nc.tensor.matmul(B[4 + d][0:32, c * P:(c + 1) * P], cstok[:, c, :], tri[:, d, :],
                                            start=True, stop=True)
                last.then_inc(s_cs, 1)
            for n, (g, d) in enumerate(steps):
                pb, gg = 64 * (g % 2), g // 2
                rows = slice(pb, pb + 64)
                if d == 0:
                    if g == 0:
                        pe.wait_ge(s_rows, 2)
                    pe.wait_ge(s_cbm, 2 * g)
                    for c in range(NCH):
                        last = nc.tensor.matmul(B[0][:, c * P:(c + 1) * P], xs[rows, 8 + gg, c * P:(c + 1) * P],
                                                xs[rows, 10 + gg, c * P:(c + 1) * P], start=True, stop=True)
                    last.then_inc(s_cb, 1)
                pe.wait_ge(s_xdd, n + 1)
                pe.wait_ge(s_stout, n)
                pe.wait_ge(s_s1, n)
                nc.tensor.matmul(B[1][rows, 0:256], btok[:, 0, g * 64:g * 64 + 64], xdd[:, 0, :], start=True, stop=True)
                nc.tensor.matmul(B[6][rows, 0:256], btok[:, MID[d], g * 64:g * 64 + 64], xdd[:, 1, :], start=True,
                                 stop=True).then_inc(s_st, 1)
                pe.wait_ge(s_gated, 2 * max(g - 1, 0))
                pe.wait_ge(s_m, n + 1)
                for hh in range(4):
                    y = ybank(g, hh // 2)[64 * (hh % 2):64 * (hh % 2) + 64, :]
                    for c in range(NCH):
                        nc.tensor.matmul(y[:, c * P:(c + 1) * P], xd[:, c, hh * 64:hh * 64 + 64],
                                         csb[:, n % 2, hh, c * P:(c + 1) * P], start=(c == 0 and d == 0), stop=(c == 0 and d == 1),
                                         skip_group_check=True)
                pe.wait_ge(s_cd, n + 1)
                for hh in range(4):
                    y = ybank(g, hh // 2)[64 * (hh % 2):64 * (hh % 2) + 64, :]
                    first, nxt = MID[d], NEXT[d]
                    nc.tensor.matmul(y[:, first * P:(first + 1) * P], h0[rows, gg, d, hh * 64:hh * 64 + 64],
                                     ec[rows, hh, (first - 1) * P:first * P], start=False, stop=False, skip_group_check=True)
                    last = nc.tensor.matmul(y[:, nxt * P:(nxt + 1) * P], s1[rows, hh * 64:hh * 64 + 64],
                                            ec[rows, hh, (nxt - 1) * P:nxt * P], start=False, stop=(d == 1),
                                            skip_group_check=True)
                last.then_inc(s_y, 1)
            for b in range(8):
                pe.wait_ge(s_sq, b + 1)
                last = nc.tensor.matmul(B[0][:, 0:T], N.ones[:, :], xs[:, b, :], start=(b == 0), stop=(b == 7))
            last.then_inc(s_sqs, 1)

        @block.scalar
        def _(act):
            A = nc.scalar.activation
            act.wait_ge(s_v, 1)
            A(du[:, :], dv[:, :], ACT.Abs).then_inc(s_abs, 1)
            act.wait_ge(s_abs, 1)
            A(du[:, :], du[:, :], ACT.Exp, scale=-1.0).then_inc(s_exp, 1)
            act.wait_ge(s_ld, 64)
            A(aexp[:, :], aexp[:, :], ACT.Exp).then_inc(s_aexp, 1)
            for f in range(6):
                act.wait_ge(s_x2t, f + 1)
                A(xtok[:, f // 2, 512 * (f % 2):512 * (f % 2) + 512], B[f][:, :], ACT.Copy).then_inc(s_xtok, 1)
            act.wait_ge(s_x2t, 7)
            A(btok[:, 0:2, :], B[0][:, :], ACT.Copy).then_inc(s_xtok, 1)
            act.wait_ge(s_x2t, 8)
            A(btok[:, 2, :], B[1][:, 0:256], ACT.Copy).then_inc(s_xtok, 1)
            act.wait_ge(s_tp, 1)
            A(dttok[:, :, :], B[6][:, 0:96], ACT.Copy).then_inc(s_dttok, 1)
            act.wait_ge(s_cs, 1)
            act.wait_ge(s_cs, 3)
            A(cstok[:, :, :], B[6][:, 128:224], ACT.Copy).then_inc(s_cstok, 1)
            A(rows_f[0:32, :], B[4][0:32, 0:T], ACT.Copy).then_inc(s_rows, 1)
            A(rows_b[0:32, :], B[5][0:32, 0:T], ACT.Copy).then_inc(s_rows, 1)
            for n, (g, d) in enumerate(steps):
                pb, gg = 64 * (g % 2), g // 2
                rows = slice(pb, pb + 64)
                act.wait_ge(s_csb[n % 2], 16 * (n // 2 + 1))
                act.wait_ge(s_y, n)
                A(ec[rows, :, :], csb[rows, n % 2, :, T_CTX:T], ACT.Exp).then_inc(s_ec, 1)
                act.wait_ge(s_wsub, n + 1)
                A(wt[:, :, :], wt[:, :, :], ACT.Exp).then_inc(s_wexp, 1)
                act.wait_ge(s_d, n + 1)
                A(csb[:, n % 2], csb[:, n % 2], ACT.Exp).then_inc(s_dexp, 1)
                act.wait_ge(s_st, n + 1)
                A(stout[rows, gg, d, :], B[1][rows, 0:256], ACT.Copy).then_inc(s_stout, 1)
            for b in range(8):
                act.wait_ge(s_gated, b + 1)
                if b == 0:
                    act.wait_ge(s_gated, 8)
                A(xs[:, b, :], z[:, b, :], ACT.Square).then_inc(s_sq, 1)
            for b in range(8):
                act.wait_ge(s_norm, b + 1)
                A(ohi[:, b, :], z[:, b, :], ACT.Copy, scale=0.5).then_inc(s_ohi, 1)

        @block.vector
        def _(dve):
            V = nc.vector
            st = N.steps(dve)
            dve.wait_ge(s_ld, 64)
            V.tensor_scalar(dv[:, :], B[7][0:32, 0:T], dbias[:, 0:1], None, ALU.add).then_inc(s_v, 1)
            dve.wait_ge(s_exp, 1)
            st.chain(V.tensor_scalar(dr[:, :], du[:, :], 2.0, None, ALU.add))
            st.chain(V.reciprocal(dr[:, :], dr[:, :]))
            st.chain(V.tensor_tensor(ds_[:, :], du[:, :], dr[:, :], ALU.mult))
            st.chain(V.tensor_tensor(dq[:, :], ds_[:, :], ds_[:, :], ALU.mult))
            st.chain(V.tensor_scalar(dp[:, :], dq[:, :], 1.0 / 17.0, None, ALU.mult))
            for k in (15, 13, 11, 9, 7, 5, 3):
                st.chain(V.scalar_tensor_tensor(out=dp[:, :], in0=dp[:, :], scalar=1.0 / k, in1=dq[:, :], op0=ALU.add, op1=ALU.mult))
            st.chain(V.scalar_tensor_tensor(out=dp[:, :], in0=dp[:, :], scalar=1.0, in1=ds_[:, :], op0=ALU.add, op1=ALU.mult))
            dve.wait_ge(s_v, 1)
            st.chain(V.tensor_scalar(dv[:, :], dv[:, :], 0.0, None, ALU.max))
            V.scalar_tensor_tensor(out=dsp[:, :], in0=dp[:, :], scalar=2.0, in1=dv[:, :], op0=ALU.mult, op1=ALU.add)\
                .then_inc(s_dtr, 1)
            dve.wait_ge(s_aexp, 1)
            dve.wait_ge(s_dttok, 1)
            V.scalar_tensor_tensor(out=cstok[:, :, :], in0=dttok[:, :, :], scalar=-1.0,
                                   in1=aexp[:, :].unsqueeze(1).to_broadcast([P, NCH, 32]), op0=ALU.mult, op1=ALU.mult)\
                .then_inc(s_atok, 1)
            dve.wait_ge(s_cstok, 1)
            for n, (g, d) in enumerate(steps):
                pb, gg = 64 * (g % 2), g // 2
                rows = slice(pb, pb + 64)
                hs = slice(16 * d + 4 * g, 16 * d + 4 * g + 4)
                row = csb[:, n % 2]
                ends = row[:, :, 127:T:P] if d == 0 else row[:, :, 0:T:P]
                pick = slice(0, 2) if d == 0 else slice(0, 3, 2)
                if d == 0:
                    dve.wait_ge(s_cb, g + 1)
                    dve.wait_ge(s_y, n)
                    for dd in range(2):
                        V.tensor_tensor(cbm[:, dd, :], B[0][:, 0:T],
                                        tri[:, dd:dd + 1, :].to_broadcast([P, NCH, P]), ALU.mult).then_inc(s_cbm, 1)
                dve.wait_ge(s_csb[n % 2], 16 * (n // 2 + 1))
                st.chain(V.tensor_tensor(wt[:, :, :], ends[:, :, pick], cstok[:, pick, hs].rearrange("p c h -> p h c"),
                                         ALU.subtract))
                V.tensor_scalar(wt[:, :, :], wt[:, :, :], 0.0, None, ALU.min).then_inc(s_wsub, 1)
                dve.wait_ge(s_ec, n + 1)
                dve.wait_ge(s_y, n)
                V.tensor_tensor(xd[:, :, :].rearrange("p c (h q) -> p c h q", h=4),
                                xtok[:, :, g * 256:g * 256 + 256].rearrange("p c (h q) -> p c h q", h=4),
                                dttok[:, :, hs].unsqueeze(3).to_broadcast([P, NCH, 4, HD]), ALU.mult).then_inc(s_xd, 1)
                dve.wait_ge(s_wexp, n + 1)
                dve.wait_ge(s_xd, n + 1)
                V.tensor_tensor(xdd[:, :, :].rearrange("p c (h q) -> p c h q", h=4),
                                xd[:, pick, :].rearrange("p c (h q) -> p c h q", h=4),
                                wt[:, :, :].rearrange("p h c -> p c h").unsqueeze(3).to_broadcast([P, 2, 4, HD]),
                                ALU.mult).then_inc(s_xdd, 1)
                st.chain(V.tensor_tensor(row.rearrange("p h (c l) -> p h c l", c=NCH), row.rearrange("p h (c l) -> p h c l", c=NCH),
                                         cstok[:, :, hs].rearrange("p c h -> p h c").unsqueeze(3).to_broadcast([P, 4, NCH, P]),
                                         ALU.subtract))
                V.tensor_scalar(row, row, 0.0, None, ALU.min).then_inc(s_d, 1)
                st.chain(V.tensor_tensor(s1[rows, :].rearrange("p (h q) -> p h q", h=4),
                                         h0[rows, gg, d, :].rearrange("p (h q) -> p h q", h=4),
                                         ec[rows, :, END[d]:END[d] + 1].to_broadcast([64, 4, HD]), ALU.mult))
                dve.wait_ge(s_st, n + 1)
                V.tensor_tensor(s1[rows, :], s1[rows, :], B[6][rows, 0:256], ALU.add).then_inc(s_s1, 1)
                dve.wait_ge(s_s1, n + 1)
                V.tensor_tensor(ec[rows, :, :], ec[rows, :, :],
                                xs[rows, 10 + gg, T_CTX:T].unsqueeze(1).to_broadcast([64, 4, T_LAT]), ALU.mult).then_inc(s_cd, 1)
                dve.wait_ge(s_dexp, n + 1)
                V.tensor_tensor(row, row, cbm[:, d:d + 1, :].to_broadcast([P, 4, T]), ALU.mult).then_inc(s_m, 1)
                if d == 1:
                    dve.wait_ge(s_y, n + 1)
                    for pp in range(2):
                        b = 2 * g + pp
                        st.chain(V.scalar_tensor_tensor(out=xs[:, b, :], in0=xs[:, b, :], scalar=dskip[:, b:b + 1],
                                                        in1=ybank(g, pp)[:, 0:T], op0=ALU.mult, op1=ALU.add))
                        V.tensor_tensor(z[:, b, :], z[:, b, :], xs[:, b, :], ALU.mult).then_inc(s_gated, 1)
            dve.wait_ge(s_sqs, 1)
            st.chain(V.tensor_scalar(N.rs_v[:, :], B[0][:, 0:T], 1.0 / 4096, EPS, ALU.mult, ALU.add))
            rsqrt_steps(dve, nc, st, N.rs_v[:, :], N.rstd[:, :], N.rs_t[:, :])
            for b in range(8):
                V.scalar_tensor_tensor(out=z[:, b, :], in0=z[:, b, :], scalar=N.gains[:, 3, b:b + 1], in1=N.rstd[:, :],
                                       op0=ALU.mult, op1=ALU.mult).then_inc(s_norm, 1)
            for b in range(8):
                dve.wait_ge(s_ohi, b + 1)
                V.scalar_tensor_tensor(out=olo[:, b, :], in0=z[:, b, :], scalar=0.5, in1=ohi[:, b, :].bitcast(F32),
                                       op0=ALU.mult, op1=ALU.subtract).then_inc(s_olo, 1)


def merge_phase(N, ohi, olo, first, name):
    nc, body = N.nc, 12
    gt = N.keep("gate_tanh_" + name, [P, 2, T], F32)
    mt = N.keep("merge_tmp_" + name, [P, 2, T], F32)
    iters = MERGE_TILES // body
    with nc.Block() as block:
        @block.sync
        def _(sp):
            N.sp_tiles(sp, iters, body)

        @block.scalar
        def _(act):
            with act.Fori(0, iters) as i:
                for t in range(body):
                    N.act_hi(act, i, body, t)
                    if t % 3 == 2:
                        m = t // 3
                        act.wait_ge(N.out_read, i * 4 + (N.m0 + m + 1))
                        act.wait_ge(N.used, N.tiles_done(i, body, t - 1))
                        nc.scalar.activation(gt[:, m % 2, :], N.bank[m % 2][:, 0:T], ACT.Tanh, scale=0.5)\
                            .then_inc(N.gate_read, 1)

        @block.vector
        def _(dve):
            st = N.steps(dve)
            with dve.Fori(0, iters) as i:
                st.enter(i, 0 if first else 4)
                for t in range(body):
                    N.dve_lo(dve, i, body, t)
                    if t % 3 == 2:
                        m = t // 3
                        dve.wait_ge(N.gate_read, i * 4 + (N.m0 + m + 3))
                        dve.wait_ge(N.used, N.tiles_done(i, body, t))
                        acc = N.merged[:, ds(i * 4 + m, 1), :].rearrange("p a c -> p (a c)")
                        out = acc if first else mt[:, m % 2, :]
                        nc.vector.scalar_tensor_tensor(out=out, in0=gt[:, m % 2, :], scalar=1.0, in1=N.bank[2 + m % 2][:, 0:T],
                                                       op0=ALU.add, op1=ALU.mult).then_inc(N.out_read, 1)
                        if not first:
                            dve.wait_ge(N.out_read, i * 4 + (N.m0 + m + 3))
                            st.chain(nc.vector.tensor_tensor(acc, acc, mt[:, m % 2, :], ALU.add))
                st.leave(iters)

        @block.tensor
        def _(pe):
            with pe.Fori(0, iters) as i:
                for t in range(body):
                    m = t // 3
                    if t % 3 == 0:
                        pe.wait_ge(N.gate_read, i * 4 + (N.m0 + m + 1))
                    if t % 3 == 2:
                        pe.wait_ge(N.out_read, i * 4 + (N.m0 + m + 1))
                        N.pe_tile(pe, i, body, t, N.bank[2 + m % 2][:, 0:T], ohi, olo, 0, 8)
                    else:
                        N.pe_tile(pe, i, body, t, N.bank[m % 2][:, 0:T], N.hhi, N.hlo, 8 * (t % 3), KB)
    N.tile0 += MERGE_TILES
    N.m0 += KB


def attn_in_phase(N):
    nc = N.nc
    N.at = N.arena
    S = N.S = {}
    S["hi"] = N.keep("attn_out_hi", [P, 8, T], F32R)
    S["lo"] = N.keep("attn_out_lo", [P, 8, T], F32R)
    S["qkv"] = qkv = N.keep("qkv", [P, ATT_BLOCKS, T], F32)
    block_in_phase(N, qkv, ATT_BLOCKS)


def block_in_phase(N, out, blocks):
    nc, iters = N.nc, blocks // 2
    with nc.Block() as block:
        @block.sync
        def _(sp):
            N.sp_tiles(sp, iters, 4)

        @block.scalar
        def _(act):
            with act.Fori(0, iters) as i:
                for t in range(4):
                    N.act_hi(act, i, 4, t)
                    if t % 2 == 1:
                        b = t // 2
                        act.wait_ge(N.used, N.tiles_done(i, 4, t))
                        nc.scalar.activation(out[:, ds(i * 2 + b, 1), 0:T].rearrange("p a c -> p (a c)"),
                                             N.bank[b][:, 0:T], ACT.Copy).then_inc(N.evac, 1)

        @block.vector
        def _(dve):
            with dve.Fori(0, iters) as i:
                for t in range(4):
                    N.dve_lo(dve, i, 4, t)

        @block.tensor
        def _(pe):
            pe_blocks(N, pe, iters)
    N.tile0 += 2 * blocks
    N.blk0 += blocks


def attn_phase(N):
    nc, io, S = N.nc, N.io, N.S
    qkv, ohi, olo = S["qkv"], S["hi"], S["lo"]
    sem = N.sem
    early = N.at
    sq = N.keep("head_squares", [P, 2, T], F32)
    sel = N.keep("head_sel", [P, 10, 32], F32)
    selt = N.keep("head_sel_t", [32, 10, P], F32)
    late, N.at = N.at, early
    cst = N.keep("cond_parts_again", [P, KB, P], F32R)
    cond = N.keep("cond_again", [P, KB, 2], F32)
    ctanh, csilu = N.keep("cond_tanh_again", [P, KB, 2], F32), N.keep("cond_silu_again", [P, KB, 2], F32)
    bada = N.keep("b_ada_again", [P, 96], F32)
    four = N.keep("ada_four_again", [P, 4, 4], F32)
    assert N.at <= late
    N.at = late
    arow = N.keep("ada_rows_again", [32, 512], F32)
    cos, sin = N.keep("rope_cos", [P, T_LAT], F32), N.keep("rope_sin", [P, T_LAT], F32)
    rot = N.keep("rope_swap", [P, P], F32)
    qkg = N.keep("qk_gain", [P, 2], F32)
    kf = N.keep("k_all", [P, 2, 512], F32)
    vt = N.keep("v_tok", [P, 4, 256], F32)
    pr = N.keep("probs", [P, 4, T], F32)
    ptl = N.keep("probs_t_lat", [P, 2, 3, T_LAT], F32)
    ptc = N.keep("probs_t_ctx", [P, 2, T_CTX], F32)
    mx, nmx, sm, rc = [N.keep("softmax_" + n, [P, 4], F32) for n in ("max", "bias", "sum", "rec")]
    s_ld, s_sq, s_sqs, s_rs, s_bc, s_nrm, s_rot, s_rope, s_vT, s_v, s_out = [
        sem("at_" + n) for n in ("loads", "sq", "sqs", "rs", "bc", "nrm", "rot", "rope", "vT", "v", "out")]
    s_sc, s_mx, s_nmx, s_exp, s_rc, s_p, s_pt, s_pte, s_pv, s_hi, s_lo = [
        sem("at_" + n) for n in ("scores", "max", "bias", "exp", "rec", "probs", "probsT", "probsT_read", "pv", "hi", "lo")]
    s_al, s_az, s_tanh, s_silu, s_chi, s_clo, s_row, s_tr, s_four, s_add = N.ada_sems
    B = N.bank
    units = [(j, a, t) for j in range(8) for a in range(2) for t in range(3)]
    U = len(units)
    ada_tiles = lambda u: range(ADA_BODY // 2 * max(u % 3 - 1, 0), ADA_BODY // 2 * (u % 3))
    assert U == 3 * (ADA_CHUNKS - ADA_FIRST)

    def heads_rows(a):
        return slice(64 * a, 64 * a + 64)

    def attn_hi(act, j):
        act.wait_ge(s_pv, 2 * j + 2)
        nc.scalar.activation(ohi[:, j, :], B[5 + j % 2][:, 0:T], ACT.Copy).then_inc(s_hi, 1)

    with nc.Block() as block:
        @block.sync
        def _(sp):
            for dst, src in ((sel[:, :, :], io.head_sel), (selt[:, :, :], io.head_sel_t), (cos[:, :], io.rope[0]),
                             (sin[:, :], io.rope[1]), (rot[:, :], io.rope_swap), (qkg[:, :], io.qk_gain),
                             (kf[:, :, T:512], io.cache_k), (vt[:, 3, :], io.cache_v)):
                sp.dma_start(dst, src).then_inc(s_ld, 16)
            sp.wait_ge(s_nrm, 20)
            sp.dma_start(io.kout, kf[:, :, 0:T_CTX]).then_inc(s_out, 16)
            sp.wait_ge(s_v, 2)
            sp.dma_start(io.vout, vt[:, 0, :]).then_inc(s_out, 16)
            sp.wait_ge(s_bc, 10)
            sp.dma_start(cond[:, :, :], io.cond).then_inc(s_al, 16)
            sp.dma_start(bada[:, :], io.b_ada).then_inc(s_al, 16)
            N.sp_tiles(sp, ADA_CHUNKS - ADA_FIRST, ADA_BODY)
            sp.wait_ge(s_out, 32)
            sp.wait_ge(s_ld, 128)

        @block.gpsimd
        def _(pool):
            pool.wait_ge(s_bc, 10)
            nc.gpsimd.memset(cst[:, :, :].bitcast(F32), 0.0).then_inc(s_az, 1)

        @block.tensor
        def _(pe):
            def ada_product(q, t):
                if q == 0 and t == 0:
                    pe.wait_ge(s_clo, 2)
                pe.wait_ge(N.lo_done, q * ADA_BODY + N.tile0 + t + 1)
                if t == 0 and q > 0:
                    pe.wait_ge(s_four, ADA_FIRST + q + 1)
                for kk in range(2):
                    k, c = 2 * t + kk, slice(kk * 512, kk * 512 + 512)
                    nc.tensor.matmul(B[7][:, :], cst[:, k, :], N.whi[:, t % R, c], start=(k == 0), stop=False)
                    last = nc.tensor.matmul(B[7][:, :], cst[:, k, :], N.wlo[:, t % R, c], start=False, stop=(k == KB - 1))
                last.then_inc(N.used, 1)

            def ada_transposes(q):
                pe.wait_ge(s_row, ADA_FIRST + q)
                for b in range(4):
                    last = nc.tensor.transpose(B[7][:, 32 * b:32 * b + 32], arow[:, b * P:b * P + P], N.ident[0:32, 0:32])
                last.then_inc(s_tr, 1)
            pe.wait_ge(s_ld, 128)
            for f in range(2):
                for q in range((4, 2)[f]):
                    c = 2 * f + q // 2
                    last = nc.tensor.transpose(B[5 + f][:, q * P:q * P + P], qkv[:, 10 + q % 2, c * P:(c + 1) * P], N.ident[:, :])
                last.then_inc(s_vT, 1)
            for b in range(10):
                pe.wait_ge(s_sq, b + 1)
                nc.tensor.matmul(B[7][0:32, 0:T], sel[:, b, :], sq[:, b % 2, :], start=(b == 0), stop=(b == 9))\
                    .then_inc(s_sqs, 1)
            pe.wait_ge(s_rs, 1)

            def rotate(b):
                pe.wait_ge(s_nrm, 2 * b + 2)
                if b >= 2:
                    pe.wait_ge(s_rope, b - 1)
                x = qkv[:, b, T_CTX:T] if b < 8 else kf[:, b - 8, T_CTX:T]
                nc.tensor.matmul(B[2 + b % 2][:, 0:T_LAT], rot[:, :], x, start=True, stop=True).then_inc(s_rot, 1)
            for b in range(10):
                if b >= 2:
                    pe.wait_ge(s_nrm, 2 * b - 2)
                nc.tensor.matmul(B[b % 2][:, 0:T], selt[:, b, :], N.rstd[0:32, :], start=True, stop=True).then_inc(s_bc, 1)
                if b >= 1:
                    rotate(b - 1)
            rotate(9)
            pe.wait_ge(s_rope, 10)
            pe.wait_ge(s_v, 2)
            for u in range(U + 5):
                if u < U:
                    j, a, t = units[u]
                    kb, r = j // 4, heads_rows(a)
                    if u >= 3:
                        pe.wait_ge(s_exp, u - 2)
                    keys = kf[r, kb, 0:T_CTX] if t == 0 else kf[r, kb, T_CTX:512]
                    nc.tensor.matmul(B[u % 3][:, 0:(T_CTX if t == 0 else T)], qkv[r, j, t * P:(t + 1) * P], keys,
                                     start=True, stop=True).then_inc(s_sc, 1)
                w = u - 2
                if 0 <= w < U:
                    pe.wait_ge(s_p, w + 1)
                    if w >= 2:
                        pe.wait_ge(s_pte, w - 1)
                    for q in range(1 if units[w][2] == 0 else 3):
                        last = nc.tensor.transpose(B[3 + w % 2][:, q * P:q * P + P], pr[:, w % 4, q * P:q * P + P], N.ident[:, :])
                    last.then_inc(s_pt, 1)
                w = u - 4
                if 0 <= w < U and units[w][2] == 2:
                    j, a, _t = units[w]
                    pe.wait_ge(s_pte, w + 1)
                    if j >= 2 and a == 0:
                        pe.wait_ge(s_lo, j - 1)
                    o, vc = B[5 + j % 2][heads_rows(a), :], (j // 4) * P + 64 * a
                    nc.tensor.matmul(o[:, 0:T_CTX], vt[:, 0, vc:vc + 64], ptc[:, a, :], start=True, stop=True)
                    for q in range(3):
                        last = nc.tensor.matmul(o[:, T_CTX:T], vt[:, 1 + q, vc:vc + 64], ptl[:, a, q, :],
                                                start=(q == 0), stop=(q == 2))
                    last.then_inc(s_pv, 1)
                if u % 3 == 0 and 0 < u <= U:
                    ada_transposes(u // 3)
                if u < U:
                    for t in ada_tiles(u):
                        ada_product(u // 3, t)

        @block.scalar
        def _(act):
            A = nc.scalar.activation
            for b in range(10):
                if b >= 2:
                    act.wait_ge(s_sqs, b - 1)
                A(sq[:, b % 2, :], qkv[:, b, :], ACT.Square).then_inc(s_sq, 1)
                if b == 3:
                    act.wait_ge(s_vT, 2)
                    A(vt[:, 0:2, :], B[5][:, :], ACT.Copy).then_inc(s_v, 1)
                    A(vt[:, 2, :], B[6][:, 0:256], ACT.Copy).then_inc(s_v, 1)
            act.wait_ge(s_al, 48)
            A(ctanh[:, :, :], cond[:, :, :], ACT.Tanh, scale=0.5).then_inc(s_tanh, 1)
            act.wait_ge(s_silu, 2)
            act.wait_ge(s_az, 3)
            A(cst[:, :, 0:2], csilu[:, :, :], ACT.Copy).then_inc(s_chi, 1)

            def ada_row(q):
                act.wait_ge(N.used, N.tile0 + q * ADA_BODY + R)
                A(arow[:, :], B[7][0:32, :], ACT.Copy).then_inc(s_row, 1)

            def ada_four(q):
                act.wait_ge(s_tr, ADA_FIRST + q)
                act.wait_ge(s_add, ADA_FIRST + q - 1)
                A(four[:, :, :], B[7][:, 0:128].rearrange("p (a b) -> p a b", a=4)[:, :, 0:4], ACT.Copy).then_inc(s_four, 1)
            for u in range(U + 3):
                if u < U:
                    act.wait_ge(s_nmx, u + 1)
                    if u >= 4:
                        act.wait_ge(s_pt, u - 3)
                    n = T_CTX if units[u][2] == 0 else T
                    A(pr[:, u % 4, 0:n], B[u % 3][:, 0:n], ACT.Exp, bias=nmx[:, u % 4:u % 4 + 1], scale=HD ** -0.5,
                      accum_out=sm[:, u % 4:u % 4 + 1]).then_inc(s_exp, 1)
                w = u - 3
                if 0 <= w < U:
                    j, a, t = units[w]
                    act.wait_ge(s_pt, w + 1)
                    if w // 3 >= 2:
                        act.wait_ge(s_pv, w // 3 - 1)
                    if t == 0:
                        A(ptc[:, a, :], B[3 + w % 2][:, 0:P], ACT.Copy).then_inc(s_pte, 1)
                    else:
                        A(ptl[:, a, :, (t - 1) * P:t * P], B[3 + w % 2][:, 0:T], ACT.Copy).then_inc(s_pte, 1)
                if u % 3 == 0 and 0 < u <= U:
                    ada_row(u // 3)
                if u % 3 == 1 and 1 < u <= U + 1:
                    ada_four(u // 3)
                if u < U:
                    for t in ada_tiles(u):
                        N.act_hi(act, u // 3, ADA_BODY, t)
                w = u - 9
                if w >= 0 and w % 6 == 0 and w // 6 < 7:
                    attn_hi(act, w // 6)
            attn_hi(act, 7)

        @block.vector
        def _(dve):
            V = nc.vector
            st = N.steps(dve)
            dve.wait_ge(s_sqs, 10)
            st.chain(V.tensor_scalar(N.rs_v[0:32, :], B[7][0:32, 0:T], 1.0 / HD, EPS, ALU.mult, ALU.add))
            rsqrt_steps(dve, nc, st, N.rs_v[0:32, :], N.rstd[0:32, :], N.rs_t[0:32, :])
            nc.vector.sem_inc(s_rs, 1)
            dve.wait_ge(s_ld, 128)

            def rope(b):
                x = qkv[:, b, T_CTX:T] if b < 8 else kf[:, b - 8, T_CTX:T]
                dve.wait_ge(s_rot, b + 1)
                st.chain(V.tensor_tensor(N.rs_t[:, 0:T_LAT], B[2 + b % 2][:, 0:T_LAT], sin[:, :], ALU.mult))
                st.chain(V.tensor_tensor(x, x, cos[:, :], ALU.mult))
                V.tensor_tensor(x, x, N.rs_t[:, 0:T_LAT], ALU.add).then_inc(s_rope, 1)
                dve.wait_ge(s_rope, b + 1)
            for b in range(10):
                dve.wait_ge(s_bc, b + 1)
                for (lo, hi) in SEG:
                    x = qkv[:, b, lo:hi] if b < 8 else kf[:, b - 8, lo:hi]
                    V.scalar_tensor_tensor(out=x, in0=qkv[:, b, lo:hi], scalar=qkg[:, b // 8:b // 8 + 1], in1=B[b % 2][:, lo:hi],
                                           op0=ALU.mult, op1=ALU.mult).then_inc(s_nrm, 1)
                if b >= 1:
                    rope(b - 1)
            rope(9)

            dve.wait_ge(s_tanh, 2)
            st.chain(V.scalar_tensor_tensor(out=csilu[:, :, :], in0=ctanh[:, :, :], scalar=1.0, in1=cond[:, :, :],
                                            op0=ALU.add, op1=ALU.mult))
            V.tensor_scalar(csilu[:, :, :], csilu[:, :, :], 0.5, None, ALU.mult).then_inc(s_silu, 1)
            dve.wait_ge(s_silu, 2)
            dve.wait_ge(s_chi, 2)
            V.tensor_tensor(cst[:, :, 2:4], csilu[:, :, :], cst[:, :, 0:2].bitcast(F32), ALU.subtract).then_inc(s_clo, 1)

            def ada_add(q):
                c = 4 * (ADA_FIRST + q) - 4
                m = N.mods[:, c:c + 4, :]
                dve.wait_ge(s_four, ADA_FIRST + q + 1)
                V.tensor_tensor(m, four[:, :, 0:2], four[:, :, 2:4], ALU.add).then_inc(s_add, 1)
                dve.wait_ge(s_add, ADA_FIRST + q)
                st.chain(V.tensor_tensor(m, m, bada[:, c:c + 4].unsqueeze(2).to_broadcast([P, 4, 2]), ALU.add))

            def low(j):
                dve.wait_ge(s_hi, j + 1)
                V.tensor_tensor(olo[:, j, :], B[5 + j % 2][:, 0:T], ohi[:, j, :].bitcast(F32), ALU.subtract).then_inc(s_lo, 1)
            for u in range(U + 1):
                if u < U:
                    n = T_CTX if units[u][2] == 0 else T
                    c = slice(u % 4, u % 4 + 1)
                    dve.wait_ge(s_sc, u + 1)
                    V.reduce_max(mx[:, c], B[u % 3][:, 0:n], AX).then_inc(s_mx, 1)
                    dve.wait_ge(s_mx, u + 1)
                    if u >= 4:
                        dve.wait_ge(s_exp, u - 3)
                    V.tensor_scalar(nmx[:, c], mx[:, c], -(HD ** -0.5), None, ALU.mult).then_inc(s_nmx, 1)
                w = u - 1
                if w >= 0:
                    n = T_CTX if units[w][2] == 0 else T
                    c = slice(w % 4, w % 4 + 1)
                    dve.wait_ge(s_exp, w + 1)
                    V.reciprocal(rc[:, c], sm[:, c]).then_inc(s_rc, 1)
                    dve.wait_ge(s_rc, w + 1)
                    V.tensor_scalar(pr[:, w % 4, 0:n], pr[:, w % 4, 0:n], rc[:, c], None, ALU.mult).then_inc(s_p, 1)
                if u % 3 == 2 and 2 < u:
                    ada_add(u // 3)
                if u < U:
                    for t in ada_tiles(u):
                        N.dve_lo(dve, u // 3, ADA_BODY, t)
                w = u - 10
                if w >= 0 and w % 6 == 0 and w // 6 < 7:
                    low(w // 6)
            low(7)
            ada_add(U // 3)
    N.tile0 += (ADA_CHUNKS - ADA_FIRST) * ADA_BODY
    N.at = early


def pool_phase(N):
    nc, io = N.nc, N.io
    N.at = N.arena
    S = N.S = {}
    S["hi"] = ohi = N.keep("pool_out_hi", [P, 8, T], F32R)
    S["lo"] = olo = N.keep("pool_out_lo", [P, 8, T], F32R)
    W = 8 + T_CTX + 8 + T_LAT + 8
    pin = N.keep("pool_in", [P, 8, T], F32)
    pad = N.keep("pool_padded", [P, 2, W], F32)
    s2 = N.keep("pool_sums", [P, 2, 2, W], F32)
    inv = N.keep("pool_inv_count", [P, 4, T], F32)
    pw = N.keep("pool_w_sb", [P, 8, 256], F32)
    psc = N.keep("pool_scale_sb", [P, 8], F32)
    dif = N.keep("pool_diff", [P, 2, 2, T], F32)
    block_in_phase(N, pin, POOL_BLOCKS)
    sem = N.sem
    s_ld, s_pad, s_dif, s_mm, s_f, s_hi, s_lo, s_zero = [
        sem("po_" + n) for n in ("loads", "pad", "diff", "mm", "scaled", "hi", "lo", "zero")]
    at = (8, 8 + T_CTX + 8)

    def high(g):
        for e in range(2):
            nc.scalar.wait_ge(s_mm, 2 * g + e + 1)
            nc.scalar.activation(ohi[:, 2 * g + e, :], N.bank[2 * (g % 2) + e][:, 0:T], ACT.Copy,
                                 scale=psc[:, 2 * g + e:2 * g + e + 1]).then_inc(s_hi, 1)

    with nc.Block() as block:
        @block.sync
        def _(sp):
            for dst, src in ((inv[:, :, :], io.pool_inv), (pw[:, :, :], io.pool_w), (psc[:, :], io.pool_scale)):
                sp.dma_start(dst, src).then_inc(s_ld, 16)
            sp.wait_ge(s_ld, 48)

        @block.gpsimd
        def _(pool):
            nc.gpsimd.memset(pad[:, :, :], 0.0).then_inc(s_zero, 1)

        @block.scalar
        def _(act):
            act.wait_ge(s_zero, 1)
            for g in range(4):
                if g >= 1:
                    act.wait_ge(s_dif, 2 * g)
                for (lo, hi), o in zip(SEG, at):
                    nc.scalar.activation(pad[:, :, o:o + hi - lo], pin[:, 2 * g:2 * g + 2, lo:hi], ACT.Copy).then_inc(s_pad, 1)
                if g >= 1:
                    high(g - 1)
            high(3)

        @block.vector
        def _(dve):
            V = nc.vector
            st = N.steps(dve)
            dve.wait_ge(s_ld, 48)

            def low(g):
                for e in range(2):
                    b = 2 * g + e
                    dve.wait_ge(s_hi, b + 1)
                    V.scalar_tensor_tensor(out=olo[:, b, :], in0=N.bank[2 * (g % 2) + e][:, 0:T], scalar=psc[:, b:b + 1],
                                           in1=ohi[:, b, :].bitcast(F32), op0=ALU.mult, op1=ALU.subtract).then_inc(s_lo, 1)
            for g, win in enumerate(POOL_WINDOWS):
                dve.wait_ge(s_pad, 2 * g + 2)
                src, n, w = pad[:, :, :], W, 1
                while w < win:
                    dst = s2[:, (w.bit_length() - 1) % 2]
                    n -= w
                    st.chain(V.tensor_tensor(dst[:, :, 0:n], src[:, :, 0:n], src[:, :, w:w + n], ALU.add))
                    src, w = dst, 2 * w
                if g >= 2:
                    dve.wait_ge(s_mm, 2 * g - 2)
                for (lo, hi), o in zip(SEG, at):
                    st.chain(V.tensor_tensor(dif[:, g % 2, :, lo:hi], src[:, :, o - win // 2:o - win // 2 + hi - lo],
                                             inv[:, g:g + 1, lo:hi].to_broadcast([P, 2, hi - lo]), ALU.mult))
                for (lo, hi), o in zip(SEG, at):
                    V.tensor_tensor(dif[:, g % 2, :, lo:hi], dif[:, g % 2, :, lo:hi], pad[:, :, o:o + hi - lo], ALU.subtract)\
                        .then_inc(s_dif, 1)
                if g >= 1:
                    low(g - 1)
            low(3)

        @block.tensor
        def _(pe):
            pe.wait_ge(s_ld, 48)
            for g in range(4):
                pe.wait_ge(s_dif, 2 * g + 2)
                if g >= 2:
                    pe.wait_ge(s_lo, 2 * g - 2)
                for e in range(2):
                    for k in range(2):
                        last = nc.tensor.matmul(N.bank[2 * (g % 2) + e][:, 0:T], pw[:, 2 * g + k, e * P:(e + 1) * P],
                                                dif[:, g % 2, k, :], start=(k == 0), stop=(k == 1))
                    last.then_inc(s_mm, 1)


def split_merged_phase(N):
    nc = N.nc
    s_hi, s_lo, x_in = N.sem("merged_hi"), N.sem("merged_lo"), N.sem("x_again")
    with nc.Block() as block:
        @block.scalar
        def _(act):
            for b in range(4):
                nc.scalar.activation(N.hhi[:, 4 * b:4 * b + 4, :], N.merged[:, 4 * b:4 * b + 4, :], ACT.Copy, scale=0.5)\
                    .then_inc(s_hi, 1)

        @block.vector
        def _(dve):
            for b in range(4):
                q = slice(4 * b, 4 * b + 4)
                dve.wait_ge(s_hi, b + 1)
                nc.vector.scalar_tensor_tensor(out=N.hlo[:, q, :], in0=N.merged[:, q, :], scalar=0.5,
                                               in1=N.hhi[:, q, :].bitcast(F32), op0=ALU.mult, op1=ALU.subtract)\
                    .then_inc(s_lo, 1)

        @block.sync
        def _(sp):
            for b in range(4):
                sp.wait_ge(s_lo, b + 1)
                sp.dma_start(N.merged[:, 4 * b:4 * b + 4, :], N.io.x[:, 4 * b:4 * b + 4, :]).then_inc(x_in, 16)
            sp.wait_ge(x_in, 64)


def w_out_phase(N):
    nc, iters, xt = N.nc, KB // 2, N.merged
    gcol = N.keep("gate1_pair", [P, 2, 2], F32)
    s_x, s_g = N.sem("x_updated"), N.sem("gate1_here")
    with nc.Block() as block:
        @block.sync
        def _(sp):
            N.sp_tiles(sp, iters, 4)

        @block.scalar
        def _(act):
            with act.Fori(0, iters) as i:
                for t in range(4):
                    N.act_hi(act, i, 4, t)

        @block.vector
        def _(dve):
            nc.vector.sem_inc(s_x, 4)

            def step(i):
                for t in range(4):
                    N.dve_lo(dve, i, 4, t)
                    if t % 2 == 1:
                        b = t // 2
                        dve.wait_ge(N.used, N.tiles_done(i, 4, t))
                        for g, (lo, hi) in enumerate(SEG):
                            x = xt[:, ds(i * 2 + b, 1), lo:hi].rearrange("p a c -> p (a c)")
                            nc.vector.scalar_tensor_tensor(out=x, in0=N.bank[b][:, lo:hi], scalar=gcol[:, b, g:g + 1],
                                                           in1=x, op0=ALU.mult, op1=ALU.add).then_inc(s_x, 1)

            def load_gates(i):
                dve.wait_ge(s_x, i * 4 + 4)
                nc.vector.tensor_copy(gcol[:, :, :], N.mods[:, ds(i * 2 + 2 * KB, 2), :]).then_inc(s_g, 1)
                dve.wait_ge(s_g, i + 1)
            with dve.Fori(0, iters) as i:
                load_gates(i)
                step(i)

        @block.tensor
        def _(pe):
            with pe.Fori(0, iters) as i:
                for t in range(4):
                    if t % 2 == 0:
                        pe.wait_ge(s_x, i * 4 + (t + 2))
                    N.pe_tile(pe, i, 4, t, N.bank[t // 2][:, 0:T], N.hhi, N.hlo, 8 * (t % 2), KB)
    N.tile0 += 2 * KB


def norm_phase(N, name):
    nc, xt = N.nc, N.merged
    sq = N.keep("squares_" + name, [P, 2, 4, T], F32)
    s_sq, s_sum = [N.sem(name + n) for n in ("_squares", "_sums")]
    with nc.Block() as block:
        @block.scalar
        def _(act):
            for b in range(4):
                if b >= 2:
                    act.wait_ge(s_sum, b - 1)
                nc.scalar.activation(sq[:, b % 2], xt[:, 4 * b:4 * b + 4, :], ACT.Square).then_inc(s_sq, 1)

        @block.tensor
        def _(pe):
            for b in range(4):
                pe.wait_ge(s_sq, b + 1)
                for k in range(4):
                    last = nc.tensor.matmul(N.bank[7][:, 0:T], N.ones[:, :], sq[:, b % 2, k, :],
                                            start=(b + k == 0), stop=(b * 4 + k == KB - 1))
                last.then_inc(s_sum, 1)

        @block.vector
        def _(dve):
            st = N.steps(dve)
            dve.wait_ge(s_sum, 4)
            st.chain(nc.vector.tensor_scalar(N.rs_v[:, :], N.bank[7][:, 0:T], 1.0 / D, EPS, ALU.mult, ALU.add))
            rsqrt_steps(dve, nc, st, N.rs_v[:, :], N.rstd[:, :], N.rs_t[:, :])


def rank_steps(st, nc, v, ahead, after, before, rank):
    q = v.shape[1]
    shape = [P, q, 4, 4]
    vi, vj = v.unsqueeze(2).to_broadcast(shape), v.unsqueeze(3).to_broadcast(shape)
    st.did(nc.vector.tensor_tensor(ahead, vi, vj, ALU.is_gt))
    st.chain(nc.vector.tensor_tensor(after, vi, vj, ALU.is_ge))
    st.chain(nc.vector.tensor_tensor(after, after, ahead, ALU.subtract))
    st.chain(nc.vector.tensor_tensor(after, after, before.unsqueeze(1).to_broadcast(shape), ALU.mult))
    st.chain(nc.vector.tensor_tensor(ahead, ahead, after, ALU.add))
    st.chain(nc.vector.reduce_sum(rank, ahead, AX))


def router_phase(N):
    nc, io, sem = N.nc, N.io, N.sem
    N.gate_w = N.keep("half_gate_weights", [P, NCH, NE], F32)
    N.slot = N.keep("slot_in_group", [P, NCH, NG], F32)
    N.most = N.keep("most_in_group", [P, 1], I32)
    N.iota = N.keep("slot_numbers", [P, P], F32)
    mark = N.at
    wr = N.keep("w_router_sb", [P, KB, P], F32)
    wrh = N.keep("w_router_hi", [P, KB, P], F32R)
    wrl = N.keep("w_router_lo", [P, KB, P], F32R)
    lt = N.keep("logits_t", [P, T], F32)
    br = N.keep("b_router_sb", [P, NE], F32)
    before = N.keep("index_before", [P, 4, 4], F32)
    tri = N.keep("tri_upto", [P, P], F32)
    ex, sc, bi, wt = [N.keep("router_" + n, [P, NCH * NE], F32) for n in ("exp", "scores", "biased", "weights")]
    ah, af = N.keep("rank_ahead", [P, 12, 4, 4], F32), N.keep("rank_equal", [P, 12, 4, 4], F32)
    rk, sel = N.keep("rank_in_group", [P, 12, 4], F32), N.keep("selected", [P, 12, 4], F32)
    gs, gr, gb = [N.keep("group_" + n, [P, NCH, NG], F32) for n in ("score", "rank", "best")]
    den = N.keep("weight_sum", [P, NCH], F32)
    cm = N.keep("most_f", [P, 1], F32)
    s_ld, s_wh, s_wl, s_lg, s_lt, s_tr, s_ex, s_gb, s_cs = [
        sem("rt_" + n) for n in ("loads", "w_hi", "w_lo", "logits", "logits_sb", "by_token", "exp", "best", "cumsum")]
    s_ht, s_hh, s_hl = sem("h_by_token"), sem("h_by_token_hi"), sem("h_by_token_lo")
    B = N.bank
    with nc.Block() as block:
        @block.sync
        def _(sp):
            for dst, src in ((wr[:, :, :], io.w_router), (br[:, :], io.b_router), (before[:, :, :], io.before),
                             (tri[:, :], io.tri[:, 0, :]), (N.iota[:, :], io.iota)):
                sp.dma_start(dst, src).then_inc(s_ld, 16)
            sp.wait_ge(s_ld, 80)

        @block.scalar
        def _(act):
            act.wait_ge(s_ld, 80)
            nc.scalar.activation(wrh[:, :, :], wr[:, :, :], ACT.Copy).then_inc(s_wh, 1)
            act.wait_ge(s_lg, 1)
            nc.scalar.activation(lt[:, :], B[0][:, 0:T], ACT.Copy).then_inc(s_lt, 1)
            act.wait_ge(s_tr, 1)
            for c in range(NCH):
                nc.scalar.activation(ex[:, c * NE:(c + 1) * NE], B[1][:, c * P:c * P + NE], ACT.Exp, scale=-1.0)\
                    .then_inc(s_ex, 1)
            for k in range(KB):
                act.wait_ge(s_ht, k + 1)
                nc.scalar.activation(N.hhi[:, k, :], B[4 + k % 4][:, 0:T], ACT.Copy).then_inc(s_hh, 1)

        @block.tensor
        def _(pe):
            pe.wait_ge(s_wl, 1)
            for k in range(KB):
                nc.tensor.matmul(B[0][:, 0:T], wrh[:, k, :], N.hhi[:, k, :], start=(k == 0), stop=False)
                nc.tensor.matmul(B[0][:, 0:T], wrh[:, k, :], N.hlo[:, k, :], start=False, stop=False)
                last = nc.tensor.matmul(B[0][:, 0:T], wrl[:, k, :], N.hhi[:, k, :], start=False, stop=(k == KB - 1))
            last.then_inc(s_lg, 1)
            pe.wait_ge(s_lt, 1)
            for c in range(NCH):
                last = nc.tensor.transpose(B[1][:, c * P:(c + 1) * P], lt[:, c * P:(c + 1) * P], N.ident[:, :])
            last.then_inc(s_tr, 1)
            for k in range(KB):
                if k >= 4:
                    pe.wait_ge(s_hl, k - 3)
                for c in range(NCH):
                    o, t = B[4 + k % 4][:, c * P:(c + 1) * P], slice(c * P, (c + 1) * P)
                    nc.tensor.matmul(o, N.hhi[:, k, t].bitcast(F32), N.ident[:, :], start=True, stop=False)
                    last = nc.tensor.matmul(o, N.hlo[:, k, t].bitcast(F32), N.ident[:, :], start=False, stop=True)
                last.then_inc(s_ht, 1)
            pe.wait_ge(s_gb, 1)
            for c in range(NCH):
                for b in range(c + 1):
                    nc.tensor.matmul(B[2][:, c * NG:(c + 1) * NG], (tri if b == c else N.ones)[:, :], gb[:, b, :],
                                     start=(b == 0), stop=(b == c))
            for b in range(NCH):
                last = nc.tensor.matmul(B[3][:, 0:NG], N.ones[:, :], gb[:, b, :], start=(b == 0), stop=(b == NCH - 1))
            last.then_inc(s_cs, 1)

        @block.vector
        def _(dve):
            V = nc.vector
            st = N.steps(dve)
            dve.wait_ge(s_ld, 80)
            dve.wait_ge(s_wh, 1)
            V.tensor_tensor(wrl[:, :, :], wr[:, :, :], wrh[:, :, :].bitcast(F32), ALU.subtract).then_inc(s_wl, 1)

            def lows(k0, k1):
                for k in range(k0, k1):
                    dve.wait_ge(s_hh, k + 1)
                    V.tensor_tensor(N.hlo[:, k, :], B[4 + k % 4][:, 0:T], N.hhi[:, k, :].bitcast(F32), ALU.subtract)\
                        .then_inc(s_hl, 1)
            dve.wait_ge(s_ex, NCH)
            st.chain(V.tensor_scalar(ex[:, :], ex[:, :], 1.0, None, ALU.add))
            st.chain(V.reciprocal(sc[:, :], ex[:, :]))
            lows(0, 2)
            st.chain(V.tensor_tensor(bi[:, :].rearrange("p (c e) -> p c e", c=NCH), sc[:, :].rearrange("p (c e) -> p c e", c=NCH),
                                     br[:, :].unsqueeze(1).to_broadcast([P, NCH, NE]), ALU.add))
            b4 = bi[:, :].rearrange("p (q j) -> p q j", j=4)
            rank_steps(st, nc, b4, ah[:, :, :, :], af[:, :, :, :], before[:, :, :], rk[:, :, :])
            lows(2, 5)
            st.chain(V.tensor_scalar(sel[:, :, :], rk[:, :, :], 1.5, None, ALU.is_lt))
            st.chain(V.tensor_tensor(rk[:, :, :], sel[:, :, :], b4, ALU.mult))
            st.chain(V.reduce_sum(gs[:, :, :].rearrange("p c g -> p (c g)"), rk[:, :, :], AX))
            lows(5, 7)
            rank_steps(st, nc, gs[:, :, :], ah[:, 0:NCH], af[:, 0:NCH], before[:, :, :], gr[:, :, :])
            lows(7, 10)
            V.tensor_scalar(gb[:, :, :], gr[:, :, :], 0.5, None, ALU.is_lt).then_inc(s_gb, 1)
            dve.wait_ge(s_gb, 1)
            st.chain(V.tensor_tensor(sel[:, :, :], sel[:, :, :],
                                     gb[:, :, :].rearrange("p c g -> p (c g)").unsqueeze(2).to_broadcast([P, 12, 4]), ALU.mult))
            lows(10, 12)
            w3 = wt[:, :].rearrange("p (c e) -> p c e", c=NCH)
            st.chain(V.tensor_tensor(wt[:, :], sel[:, :, :].rearrange("p q j -> p (q j)"), sc[:, :], ALU.mult))
            st.chain(V.reduce_sum(den[:, :], w3, AX))
            st.chain(V.reciprocal(den[:, :], den[:, :]))
            st.chain(V.tensor_scalar(den[:, :], den[:, :], 0.5, None, ALU.mult))
            st.chain(V.tensor_tensor(N.gate_w[:, :, :], w3, den[:, :].unsqueeze(2).to_broadcast([P, NCH, NE]), ALU.mult))
            lows(12, KB)
            dve.wait_ge(s_cs, 1)
            st.chain(V.tensor_tensor(N.slot[:, :, :].rearrange("p c g -> p (c g)"), B[2][:, 0:12],
                                     gb[:, :, :].rearrange("p c g -> p (c g)"), ALU.mult))
            st.chain(V.tensor_scalar(N.slot[:, :, :], N.slot[:, :, :], -1.0, None, ALU.add))
            st.chain(V.reduce_max(cm[:, :], B[3][:, 0:NG], AX))
            st.chain(V.tensor_copy(N.most[:, :], cm[:, :]))
    N.at = mark


FF_ORDER = [("gate", 0, u) for u in range(8)]
for _j in range(4):
    FF_ORDER += [("up", _j, u) for u in range(8)]
    if _j < 3:
        FF_ORDER += [("gate", _j + 1, u) for u in range(8)]
    FF_ORDER += [("down", _j, u) for u in range(8)]
GATE_END = [FF_ORDER.index(("gate", j, 7)) for j in range(4)]
UP_END = [FF_ORDER.index(("up", j, 7)) for j in range(4)]
ACT_TR = [min(UP_END[j] + 5, FF_ORDER.index(("down", j, 0))) for j in range(4)]
SCATTER_AT = [2 + m * 13 // 16 for m in range(KB)]
PICKS = [(1, (24, 25), 26), (0, (27, 28), 29), (0, (31, 33), 34), (0, (35, 36), 37),
         (1, (48, 49), 50), (7, (51, 52), 53), (7, (55, 57), 58), (7, (60, 61), 62)]


class Experts:

    def __init__(self, N):
        sb, sem = N.keep, N.sem
        self.pick = sb("pick", [P, NCH, NG + 2, P], F32R)
        self.place = sb("place", [P, NG + 1, T], F32R)
        self.sr = sb("slot_this_round", [P, NCH, NG], F32)
        self.gws = sb("slot_weights", [P, NG, 4], F32)
        self.gcur = sb("slot_weights_now", [P, 4], F32)
        self.xhi = [sb(f"group_hi{h}", [P, KB, P], F32R) for h in range(2)]
        self.xlo = [sb(f"group_lo{h}", [P, KB, P], F32R) for h in range(2)]
        self.th = sb("ff_tanh", [P, 512], F32)
        self.a1 = sb("ff_silu", [P, 512], F32)
        self.act = sb("ff_act", [P, 512], F32)
        self.ahi, self.alo = sb("ff_act_hi", [P, 512], F32R), sb("ff_act_lo", [P, 512], F32R)
        self.yhi, self.ylo = sb("ff_out_hi", [P, D], F32R), sb("ff_out_lo", [P, D], F32R)
        names = ("picked", "place_tr", "place", "weights", "weights_sb", "steps", "gathered", "group_hi", "group_lo", "tanh",
                 "silu", "act", "act_tr", "act_hi", "act_lo", "y_hi", "y_lo", "scattered", "x_added", "gate_now")
        (self.s_pick, self.s_ptr, self.s_pl, self.s_w, self.s_ws, self.st_sem, self.s_ga, self.s_gh, self.s_gl, self.s_th,
         self.s_si, self.s_act, self.s_at, self.s_ah, self.s_al, self.s_yh, self.s_yl, self.s_sc, self.s_x,
         self.s_gc) = [sem("ff_" + n) for n in names]


def in_round(N, eng, r):
    if r == 0:
        return contextlib.nullcontext()
    return eng.If(eng.value_load(N.most[0:1, 0:1], min_val=0, max_val=T) > P * r)


def expert_round(N, E, r):
    nc, B, body = N.nc, N.bank, NG // 2 * len(FF_ORDER)
    A, V = nc.scalar.activation, nc.vector
    with nc.Block() as block:
        @block.vector
        def _(dve):
            with in_round(N, dve, r):
                st = Steps(dve, E.st_sem)
                st.n = r
                st.chain(V.tensor_scalar(E.sr[:, :, :], N.slot[:, :, :], float(-P * r), None, ALU.add))
                for c in range(NCH):
                    for g in range(NG):
                        V.tensor_scalar(E.pick[:, c, g, :], N.iota[:, :], E.sr[:, c, g:g + 1], None, ALU.is_equal)\
                            .then_inc(E.s_pick, 1)
                dve.wait_ge(E.s_w, r + 1)
                for g in range(NG):
                    V.tensor_copy(E.gws[:, g, :], B[4][:, g * NE + 4 * g:g * NE + 4 * g + 4]).then_inc(E.s_ws, 1)

        @block.gpsimd
        def _(pool):
            if r == 0:
                nc.gpsimd.memset(E.pick[:, :, NG:NG + 2, :].bitcast(F32), 0.0)
                nc.gpsimd.memset(E.place[:, 0:1, :].bitcast(F32), 0.0)

        @block.tensor
        def _(pe):
            with in_round(N, pe, r):
                pe.wait_ge(E.s_pick, 12 * (r + 1))
                for g in range(NG):
                    for c in range(NCH):
                        last = nc.tensor.transpose(B[g][:, c * P:(c + 1) * P], E.pick[:, c, g, :].bitcast(F32), N.ident[:, :])
                    last.then_inc(E.s_ptr, 1)
                for g in range(NG):
                    for c in range(NCH):
                        last = nc.tensor.matmul(B[4][:, g * NE:(g + 1) * NE], E.pick[:, c, g, :].bitcast(F32), N.gate_w[:, c, :],
                                                start=(c == 0), stop=(c == NCH - 1))
                last.then_inc(E.s_w, 1)

        @block.scalar
        def _(act):
            with in_round(N, act, r):
                for g in range(NG):
                    act.wait_ge(E.s_ptr, NG * r + g + 1)
                    A(E.place[:, g + 1, :], B[g][:, 0:T], ACT.Copy).then_inc(E.s_pl, 1)

    g0, y0 = NG * r, (NG + 1) * r
    GL = len(FF_ORDER)

    def picked(i, half):
        return (i * 2 + (y0 + half + 1)) * 8

    def scattered(i, half):
        return (i * 2 + (y0 + half)) * KB

    with nc.Block() as block:
        @block.sync
        def _(sp):
            with in_round(N, sp, r):
                N.sp_tiles(sp, 2, body)
                for s in range(R):
                    sp.wait_ge(N.landed[s], 16 * (N.tile0 // R + 2 * body // R + 1))

        @block.scalar
        def _(act):
            with in_round(N, act, r):
                def group_high(n, p, bank, x):
                    act.wait_ge(E.s_ga, n + (p + 1))
                    A(x[:, 2 * p:2 * p + 2, :], B[bank][:, :].rearrange("p (a b) -> p a b", a=2)[:, :, 0:P], ACT.Copy)\
                        .then_inc(E.s_gh, 1)

                def out_high(i, half, c):
                    act.wait_ge(N.used, N.tiles_done(i, body, half * GL - 1))
                    A(E.yhi[:, c * 512:(c + 1) * 512], B[2 + c][:, :], ACT.Copy).then_inc(E.s_yh, 1)

                def group(i, half):
                    for t in range(GL):
                        N.act_hi(act, i, body, half * GL + t)
                        if t < 4:
                            out_high(i, half, t)
                        for j in range(4):
                            if t == GATE_END[j] + 2:
                                act.wait_ge(N.used, N.tiles_done(i, body, half * GL + GATE_END[j]))
                                act.wait_ge(E.s_si, i * 8 + ((g0 + half) * 4 + j + 1))
                                A(E.th[:, :], B[(0, 7)[j % 2]][:, :], ACT.Tanh, scale=0.5).then_inc(E.s_th, 1)
                            if t == ACT_TR[j]:
                                act.wait_ge(E.s_at, i * 8 + ((g0 + half) * 4 + j + 1))
                                A(E.ahi[:, :], B[6][:, :], ACT.Copy).then_inc(E.s_ah, 1)
                        for p, (bank, _tiles, at) in enumerate(PICKS):
                            if t == at:
                                group_high(picked(i, half), p, bank, E.xhi[1 - half])
                for p in range(8):
                    group_high(y0 * 8, p, p % 2, E.xhi[0])
                with act.Fori(0, 2) as i:
                    for half in range(2):
                        group(i, half)
                for c in range(4):
                    out_high(2, 0, c)

        @block.vector
        def _(dve):
            with in_round(N, dve, r):
                if r == 0:
                    V.sem_inc(E.s_act, 1)
                    V.sem_inc(E.s_si, 1)
                    V.sem_inc(E.s_x, 4)

                def group_low(n, p, bank, x, xh):
                    dve.wait_ge(E.s_gh, n + (p + 1))
                    V.tensor_tensor(x[:, 2 * p:2 * p + 2, :], B[bank][:, :].rearrange("p (a b) -> p a b", a=2)[:, :, 0:P],
                                    xh[:, 2 * p:2 * p + 2, :].bitcast(F32), ALU.subtract).then_inc(E.s_gl, 1)

                def out_low(n, c):
                    dve.wait_ge(E.s_yh, n + (c + 1))
                    V.tensor_tensor(E.ylo[:, c * 512:(c + 1) * 512], B[2 + c][:, :], E.yhi[:, c * 512:(c + 1) * 512].bitcast(F32),
                                    ALU.subtract).then_inc(E.s_yl, 1)

                def add_block(n, m):
                    if m == 0:
                        dve.wait_ge(E.s_x, n * 2 + 4)
                    dve.wait_ge(E.s_sc, n + (m + 1))
                    for g, (lo, hi) in enumerate(SEG):
                        x = N.merged[:, m, lo:hi]
                        V.scalar_tensor_tensor(out=x, in0=B[(6, 7)[m % 2]][:, lo:hi], scalar=N.mods[:, 5 * KB + m, g:g + 1],
                                               in1=x, op0=ALU.mult, op1=ALU.add).then_inc(E.s_x, 1)

                def activate(i, half, j):
                    n = (g0 + half) * 4 + j
                    dve.wait_ge(E.s_act, i * 8 + (n + 1))
                    dve.wait_ge(E.s_th, i * 8 + (n + 1))
                    V.scalar_tensor_tensor(out=E.a1[:, :], in0=E.th[:, :], scalar=1.0, in1=B[(0, 7)[j % 2]][:, :],
                                           op0=ALU.add, op1=ALU.mult).then_inc(E.s_si, 1)
                    dve.wait_ge(E.s_si, i * 8 + (n + 2))
                    dve.wait_ge(N.used, N.tiles_done(i, body, half * GL + UP_END[j]))
                    V.scalar_tensor_tensor(out=E.act[:, :], in0=E.a1[:, :], scalar=E.gcur[:, j:j + 1], in1=B[1][:, :],
                                           op0=ALU.mult, op1=ALU.mult).then_inc(E.s_act, 1)

                def group(i, half):
                    for t in range(GL):
                        N.dve_lo(dve, i, body, half * GL + t)
                        if t < 4:
                            out_low((i * 2 + (y0 + half)) * 4, t)
                        if t == 5:
                            dve.wait_ge(E.s_act, i * 8 + ((g0 + half) * 4 + 1))
                            V.tensor_copy(E.gcur[:, :], E.gws[:, ds(i * 2 + half, 1), :].rearrange("p a c -> p (a c)"))\
                                .then_inc(E.s_gc, 1)
                            dve.wait_ge(E.s_gc, i * 2 + (g0 + half + 1))
                        for m in range(KB):
                            if t == SCATTER_AT[m]:
                                add_block(scattered(i, half), m)
                        for j in range(4):
                            if t == min(UP_END[j] + 2, ACT_TR[j]):
                                activate(i, half, j)
                            if t == ACT_TR[j]:
                                dve.wait_ge(E.s_ah, i * 8 + ((g0 + half) * 4 + j + 1))
                                V.tensor_tensor(E.alo[:, :], B[6][:, :], E.ahi[:, :].bitcast(F32), ALU.subtract)\
                                    .then_inc(E.s_al, 1)
                        for p, (bank, _tiles, at) in enumerate(PICKS):
                            if t == at:
                                group_low(picked(i, half), p, bank, E.xlo[1 - half], E.xhi[1 - half])
                for p in range(8):
                    group_low(y0 * 8, p, p % 2, E.xlo[0], E.xhi[0])
                with dve.Fori(0, 2) as i:
                    for half in range(2):
                        group(i, half)
                for c in range(4):
                    out_low((NG + y0) * 4, c)
                for m in range(KB):
                    add_block((NG + y0) * KB, m)

        @block.tensor
        def _(pe):
            with in_round(N, pe, r):
                def pick_block(g, k, bank, bl):
                    o = B[bank][:, bl * 256:(bl + 1) * 256]
                    for c in range(NCH):
                        tok = slice(c * P, (c + 1) * P)
                        rhs = E.pick[:, c, ds(g, 2), :].rearrange("p a s -> p (a s)")
                        nc.tensor.matmul(o, N.hhi[:, k, tok], rhs, start=(c == 0), stop=False)
                        last = nc.tensor.matmul(o, N.hlo[:, k, tok], rhs, start=False, stop=(c == NCH - 1))
                    return last

                def scatter(i, half, m):
                    n = scattered(i, half)
                    if m % 4 == 0:
                        pe.wait_ge(E.s_yl, (i * 2 + (y0 + half)) * 4 + (m // 4 + 1))
                    pe.wait_ge(E.s_x, n * 2 + (2 * m + 2))
                    o, f = B[(6, 7)[m % 2]][:, 0:T], slice(m * P, (m + 1) * P)
                    rhs = E.place[:, ds(i * 2 + half, 1), :].rearrange("p a t -> p (a t)")
                    nc.tensor.matmul(o, E.yhi[:, f], rhs, start=True, stop=False)
                    nc.tensor.matmul(o, E.ylo[:, f], rhs, start=False, stop=True).then_inc(E.s_sc, 1)

                def product(i, t, out, parts, k0, first, last):
                    s = t % R
                    pe.wait_ge(N.lo_done, i * body + (N.tile0 + t + 1))
                    for kk in range(2):
                        (xh, xl), w = parts(k0 + kk), slice(kk * 512, kk * 512 + 512)
                        nc.tensor.matmul(out, xh, N.whi[:, s, w], start=(first and kk == 0), stop=False)
                        nc.tensor.matmul(out, xl, N.whi[:, s, w], start=False, stop=False)
                        ins = nc.tensor.matmul(out, xh, N.wlo[:, s, w], start=False, stop=(last and kk == 1))
                    ins.then_inc(N.used, 1)

                def of_group(half):
                    return lambda k: (E.xhi[half][:, k, :], E.xlo[half][:, k, :])

                def of_act(k):
                    return E.ahi[:, k * P:(k + 1) * P], E.alo[:, k * P:(k + 1) * P]

                def group(i, half):
                    pe.wait_ge(E.s_gl, picked(i, half))
                    for t, (kind, j, u) in enumerate(FF_ORDER):
                        for m in range(KB):
                            if t == SCATTER_AT[m]:
                                scatter(i, half, m)
                        if t == GATE_END[0] + 9:
                            pe.wait_ge(E.s_x, scattered(i, half) * 2 + (2 * KB + 4))
                        for jj in range(4):
                            if t == ACT_TR[jj]:
                                pe.wait_ge(E.s_act, i * 8 + ((g0 + half) * 4 + jj + 2))
                                for q in range(4):
                                    last = nc.tensor.transpose(B[6][:, q * P:(q + 1) * P], E.act[:, q * P:(q + 1) * P],
                                                               N.ident[:, :])
                                last.then_inc(E.s_at, 1)
                        for p, (bank, tiles, _at) in enumerate(PICKS):
                            if t == tiles[0]:
                                pe.wait_ge(E.s_gl, picked(i, half) + p)
                            if t in tiles:
                                last = pick_block(i * 2 + (half + 1), 2 * p + tiles.index(t), bank, tiles.index(t))
                            if t == tiles[1]:
                                last.then_inc(E.s_ga, 1)
                        if u == 0 and j > 0 and kind != "down":
                            pe.wait_ge(E.s_gl, picked(i, half) + sum(at < t for _b, _t, at in PICKS))
                        if kind == "gate":
                            product(i, half * GL + t, B[(0, 7)[j % 2]][:, :], of_group(half), 2 * u, u == 0, u == 7)
                        elif kind == "up":
                            product(i, half * GL + t, B[1][:, :], of_group(half), 2 * u, u == 0, u == 7)
                        else:
                            if u == 0:
                                pe.wait_ge(E.s_al, i * 8 + ((g0 + half) * 4 + j + 1))
                            if j == 0 and u % 2 == 0:
                                pe.wait_ge(E.s_yl, (i * 2 + (y0 + half)) * 4 + (u // 2 + 1))
                            product(i, half * GL + t, B[2 + u // 2][:, :], of_act, 2 * (u % 2), j == 0 and u % 2 == 0,
                                    j == 3 and u % 2 == 1)
                for p in range(8):
                    if p >= 2:
                        pe.wait_ge(E.s_gl, y0 * 8 + p - 1)
                    for bl in range(2):
                        last = pick_block(0, 2 * p + bl, p % 2, bl)
                    last.then_inc(E.s_ga, 1)
                with pe.Fori(0, 2) as i:
                    for half in range(2):
                        group(i, half)
                for m in range(KB):
                    scatter(2, 0, m)
    N.tile0 += 2 * body


def out_phase(N):
    nc, xt = N.nc, N.merged
    s_y, s_out = N.sem("y_ready"), N.sem("y_out")
    with nc.Block() as block:
        @block.vector
        def _(dve):
            for k in range(KB):
                nc.vector.scalar_tensor_tensor(out=xt[:, k, :], in0=xt[:, k, :], scalar=N.gains[:, 2, k:k + 1],
                                               in1=N.rstd[:, :], op0=ALU.mult, op1=ALU.mult).then_inc(s_y, 1)

        @block.sync
        def _(sp):
            for b in range(4):
                sp.wait_ge(s_y, 4 * b + 4)
                sp.dma_start(N.io.y[:, 4 * b:4 * b + 4, :], xt[:, 4 * b:4 * b + 4, :]).then_inc(s_out, 16)
            sp.wait_ge(s_out, 64)


def ffn_phases(N):
    N.at = N.arena
    N.xt = N.merged
    norm_phase(N, "ffn")
    modulate_phase(N, 3, 1, "ffn_in")
    N.at = N.arena
    router_phase(N)
    E = Experts(N)
    N.src = N.io.moe
    for r in range(NCH):
        N.src0 = N.tile0
        expert_round(N, E, r)


def build(nc, io):
    N = Net(nc, io)
    ada_phase(N)
    start_credits(N)
    modulate_phase(N, 0, 0, "mix")
    ssd_in_phase(N)
    ssd_scan_phase(N)
    merge_phase(N, N.S["hi"], N.S["lo"], True, "ssd")
    attn_in_phase(N)
    attn_phase(N)
    merge_phase(N, N.S["hi"], N.S["lo"], False, "attn")
    pool_phase(N)
    merge_phase(N, N.S["hi"], N.S["lo"], False, "pool")
    N.at = N.arena
    split_merged_phase(N)
    w_out_phase(N)
    ffn_phases(N)
    N.at = N.arena
    norm_phase(N, "final")
    out_phase(N)


def blocks_a(w):
    k, n = w.shape
    return w.reshape(k // 1024, 8, P, n // P, P).transpose(3, 0, 2, 1, 4).reshape(n // P, k // 1024, P, TILE)


def blocks_b(w):
    k, n = w.shape
    return w.reshape(k // 256, 2, P, n // 512, 512).transpose(3, 0, 2, 1, 4).reshape(n // 512, k // 256, P, TILE)


def feature_major(x, blocks):
    return x.T.reshape(blocks, P, -1).transpose(1, 0, 2)


def by_block(v, blocks):
    return v.reshape(blocks, P).T


def lay_out(a):
    f = np.float32
    w_in = a["w_in"][0]
    edges = np.cumsum([0, 1024, 1536, 16, 16, 1024, 256, 256, 1024, 3 * D])
    z, xbc, dtf, dtb, q, k, v, pool, gates = [w_in[:, edges[i]:edges[i + 1]] for i in range(9)]
    q = q.reshape(D, HEADS, HD)[:, Q_HEADS].reshape(D, -1)
    w_attn = a["w_attn_out"][0].reshape(HEADS, HD, D)[Q_HEADS].reshape(-1, D)

    def merge(i, w_out):
        g, o = blocks_a(gates[:, i * D:(i + 1) * D]), blocks_a(w_out)
        return np.concatenate([g, o], axis=1).reshape(-1, P, TILE)

    flat = lambda t: t.reshape(-1, P, TILE)
    gate, up, down = [[flat(blocks_b(w[e])) for e in range(NE)]
                      for w in (a["w_gate_ff"][0], a["w_up_ff"][0], a["w_down_ff"][0])]
    ada = flat(blocks_b(a["w_ada"][0]))
    dense = np.concatenate([
        ada[:ADA_FIRST * ADA_BODY],
        flat(blocks_a(np.concatenate([xbc, z], axis=1))), merge(0, a["w_ssd_out"][0]),
        flat(blocks_a(np.concatenate([q, k, v], axis=1))), ada[ADA_FIRST * ADA_BODY:], merge(1, w_attn),
        flat(blocks_a(pool)), merge(2, a["w_pool_out"][0]),
        flat(blocks_a(a["w_out"][0]))] + [gate[0][:R]])
    order = [{"gate": gate, "up": up, "down": down}[kind][4 * g + j][u] for g in range(NG) for kind, j, u in FF_ORDER]
    x = np.concatenate([a["x_prompt"][0], a["x_sample"][0]], axis=0)
    gains = np.stack([by_block(a["norm_mix"][0], KB), by_block(a["norm_ffn"][0], KB), by_block(a["norm_final"], KB),
                      np.concatenate([by_block(a["ssd_norm"][0], 8)] * 2, axis=1)], axis=1)
    row, lane = np.arange(P)[:, None], np.arange(P)[None, :]
    tri = np.stack([row <= lane, row >= lane], axis=1).astype(f)
    h0 = np.stack([a["state_ssd_fwd"][0, 0], a["state_ssd_bwd"][0, 0]])
    h0 = h0.reshape(2, 2, 2, 4, HD, HD).transpose(2, 5, 1, 0, 3, 4).reshape(P, 2, 2, 256)
    tok = np.arange(T_LAT)
    inv_freq = np.float32(10000.0) ** (-np.arange(HD // 4, dtype=f) / (HD // 4))
    ang = np.concatenate([(tok // GRID_W).astype(f)[:, None] * inv_freq, (tok % GRID_W).astype(f)[:, None] * inv_freq], axis=1)
    ang = ang[:, (np.arange(P) % HD) // 2].T
    swap = np.zeros((P, P), f)
    even = np.arange(0, P, 2)
    swap[even + 1, even], swap[even, even + 1] = -1, 1
    sel = np.zeros((P, 10, 32), f)
    for b in range(10):
        sel[0:64, b, 2 * b], sel[64:P, b, 2 * b + 1] = 1, 1
    pool_inv = np.zeros((4, T), f)
    for g, w in enumerate(POOL_WINDOWS):
        for lo, hi in SEG:
            t, n_tok = np.arange(hi - lo), hi - lo
            pool_inv[g, lo:hi] = 1.0 / (np.clip(t + w - w // 2, 0, n_tok) - np.clip(t - w // 2, 0, n_tok))
    n = dict(
        w_router=np.concatenate([a["w_router"], np.zeros((D, P - NE), f)], axis=1).reshape(KB, P, P).transpose(1, 0, 2),
        b_router=np.broadcast_to(a["b_router"], (P, NE)), iota=np.broadcast_to(np.arange(P, dtype=f), (P, P)),
        before=np.broadcast_to(np.tri(4, k=-1, dtype=f), (P, 4, 4)),
        head_sel=sel, head_sel_t=sel.transpose(2, 1, 0), rope=np.stack([np.cos(ang), np.sin(ang)]), rope_swap=swap,
        qk_gain=np.stack([np.tile(a["q_norm"][0], 2), np.tile(a["k_norm"][0], 2)], axis=1),
        cache_k=feature_major(a["cache_k"][0, 0].reshape(T_PAST, 256), 2), cache_v=a["cache_v"][0, 0].reshape(T_PAST, 256),
        pool_inv=np.broadcast_to(pool_inv, (P, 4, T)), pool_w=a["pool_w"][0].reshape(8, P, 256).transpose(1, 0, 2),
        pool_scale=by_block(a["pool_scale"][0], 8),
        w_dt=np.concatenate([dtf, dtb], axis=1).reshape(KB, P, 32).transpose(1, 0, 2),
        conv=np.concatenate([a["conv_w"][0], a["conv_b"]]).reshape(6, 12, P).transpose(2, 1, 0),
        d_skip=by_block(np.repeat(a["d_skip"][0], HD), 8),
        dt_bias=a["dt_bias"][0].reshape(32, 1), a_log=a["a_log"][0].reshape(32), tri=tri, h0=h0,
        dense=dense, moe=np.stack(order + order[:R]), x=feature_major(x, KB),
        cond=feature_major(np.stack([a["c_ctx"], a["c"][0]]), KB),
        b_ada=by_block(a["b_ada"][0], 96), gains=gains, ident=np.eye(P, dtype=f),
    )
    return {k: np.ascontiguousarray(v, dtype=f) for k, v in n.items()}


INPUTS = ("x_prompt", "x_sample", "cache_k", "cache_v", "state_ssd_fwd", "state_ssd_bwd", "c", "c_ctx", "w_ada", "b_ada",
          "norm_mix", "norm_ffn", "w_in", "conv_w", "conv_b", "a_log", "dt_bias", "d_skip", "ssd_norm", "q_norm", "k_norm",
          "pool_w", "pool_scale", "w_ssd_out", "w_attn_out", "w_pool_out", "w_out", "w_router", "b_router", "w_gate_ff",
          "w_up_ff", "w_down_ff", "norm_final")
OUTPUTS = (("y", (P, KB, T)), ("kout", (P, 2, T_CTX)), ("vout", (P, 256)), ("states", (P, 2, 2, 256)))


def kernel(**inputs):
    import types as _types
    import concourse.bacc as _bacc
    from concourse.bass_utils import run_bass_kernel_spmd as _run

    laid = lay_out({n: np.asarray(inputs[n]) for n in INPUTS})
    nc = _bacc.Bacc("TRN2", target_bir_lowering=False, num_devices=1)
    aps, arrays = {}, {}
    for n, v in laid.items():
        arrays["in_" + n] = v
        aps[n] = nc.dram_tensor("in_" + n, v.shape, F32, kind="ExternalInput").ap()
    for n, shape in OUTPUTS:
        aps[n] = nc.dram_tensor("out_" + n, shape, F32, kind="ExternalOutput").ap()
    aps["scratch"] = nc.dram_tensor("cs_rows", (32, T), F32, kind="Internal").ap()
    build(nc, _types.SimpleNamespace(**aps))
    res = _run(nc, [arrays], core_ids=[0]).results[0]
    y, k, v, st = [np.asarray(res["out_" + n]) for n, _shape in OUTPUTS]
    y = y.transpose(2, 1, 0).reshape(1, T, D)
    k = k.transpose(2, 1, 0).reshape(1, 1, T_CTX, KV, HD)
    st = st.reshape(2, HD, 2, 2, 4, HD).transpose(3, 2, 0, 4, 5, 1).reshape(2, 1, 1, SSD_H, HD, HD)
    return (np.ascontiguousarray(y[:, :T_CTX]), np.ascontiguousarray(y[:, T_CTX:]), np.ascontiguousarray(k),
            v.reshape(1, 1, T_CTX, KV, HD), np.ascontiguousarray(st[0]), np.ascontiguousarray(st[1]))
```

```python
import contextlib

import concourse.bass as bass
from concourse import mybir
from concourse.bass import ds
import numpy as np

F32 = mybir.dt.float32
F32R = mybir.dt.float32r
I32 = mybir.dt.int32
ACT = mybir.ActivationFunctionType
ALU = mybir.AluOpType
AX = mybir.AxisListType.X

P = 128
D = 2048
KB = D // P
T_CTX, T_LAT, T_PAST = 128, 256, 128
T = T_CTX + T_LAT
SEG = ((0, T_CTX), (T_CTX, T))
EPS = 1e-6
GRID_W = 64
HEADS, KV, HD = 16, 4, 64
SSD_H, SSD_G = 16, 4
NCH = T // P
POOL_WINDOWS = (2, 4, 8, 16)
NE, NG = 16, 4
DFF = 512

TILE = 1024
R = 4
LEAD = 2
ADA_BODY = KB // 2
ADA_FIRST, ADA_CHUNKS = 2 * D // 512, 6 * D // 512
SSD_BLOCKS, ATT_BLOCKS, POOL_BLOCKS = 20, 12, 8
MERGE_TILES = 3 * KB

Q_HEADS = [h for j in range(8) for h in (8 * (j // 4) + j % 4, 8 * (j // 4) + 4 + j % 4)]


class Steps:

    def __init__(self, eng, sem):
        self.eng, self.sem, self.n, self.i, self.per = eng, sem, 0, None, 0

    def did(self, ins):
        ins.then_inc(self.sem, 1)
        self.n += 1

    def wait(self):
        self.eng.wait_ge(self.sem, self.n if self.i is None else self.i * self.per + self.n)

    def chain(self, ins):
        self.did(ins)
        self.wait()

    def enter(self, i, per):
        self.i, self.per, self.start = i, per, self.n

    def leave(self, iters):
        assert self.n - self.start == self.per, (self.sem, self.n - self.start)
        self.n, self.i = self.start + self.per * iters, None


def rsqrt_steps(dve, nc, st, v, y, t):
    st.chain(nc.vector.tensor_scalar(y.bitcast(I32), v.bitcast(I32), 1, None, ALU.logical_shift_right))
    st.chain(nc.vector.tensor_scalar(y.bitcast(I32), y.bitcast(I32), -1.0, float(0x5F3759DF), ALU.mult, ALU.add))
    for _ in range(3):
        st.chain(nc.vector.tensor_tensor(t, y, y, ALU.mult))
        st.chain(nc.vector.scalar_tensor_tensor(out=t, in0=t, scalar=-0.5, in1=v, op0=ALU.mult, op1=ALU.mult))
        st.chain(nc.vector.scalar_tensor_tensor(out=y, in0=t, scalar=1.5, in1=y, op0=ALU.add, op1=ALU.mult))


class Net:

    def __init__(self, nc, io):
        self.nc, self.io = nc, io
        self.at = (nc.sbuf_base + 63) // 32 * 32
        self.top = nc.sbuf_usable_end // 32 * 32
        sb = self.keep
        self.ident = sb("ident", [P, P], F32)
        self.ones = sb("ones", [P, P], F32)
        self.mods = sb("mods", [P, 96, 2], F32)
        self.gains = sb("gains", [P, 4, KB], F32)
        self.mod_a = sb("mod_a", [P, KB, 2], F32)
        self.half_gate = sb("half_gate", [P, KB, 2], F32)
        self.rstd = sb("rstd", [P, T], F32)
        self.rs_v = sb("rs_v", [P, T], F32)
        self.rs_t = sb("rs_t", [P, T], F32)
        self.hhi = sb("hhi", [P, KB, T], F32R)
        self.hlo = sb("hlo", [P, KB, T], F32R)
        self.merged_at = self.at
        self.merged = sb("merged", [P, KB, T], F32)
        self.raw = sb("raw", [P, R, TILE], F32)
        self.whi = sb("whi", [P, R, TILE], F32R)
        self.wlo = sb("wlo", [P, R, TILE], F32R)
        self.arena = self.at
        self.bank = [nc.alloc_psum_tensor(f"bank{i}", [P, 512], F32) for i in range(8)]
        self.landed = [nc.alloc_semaphore(f"tile_landed{i}") for i in range(R)]
        self.hi_done = nc.alloc_semaphore("tile_hi_done")
        self.lo_done = nc.alloc_semaphore("tile_lo_done")
        self.dve_steps = Steps(None, nc.alloc_semaphore("dve_steps"))
        self.used = nc.alloc_semaphore("tile_used")
        self.tile0 = 0
        self.src, self.src0 = io.dense, 0

    def keep(self, name, shape, dt):
        t = self.nc.alloc_sbuf_tensor_at(name, shape, dt, offset=self.at)
        self.at += (int(np.prod(shape[1:])) * 4 + 31) // 32 * 32
        assert self.at <= self.top, (name, self.at - self.top)
        return t

    def keep_top(self, name, shape, dt):
        self.top -= (int(np.prod(shape[1:])) * 4 + 31) // 32 * 32
        return self.nc.alloc_sbuf_tensor_at(name, shape, dt, offset=self.top)

    def steps(self, dve):
        self.dve_steps.eng = dve
        return self.dve_steps

    def sem(self, name):
        return self.nc.alloc_semaphore(name)

    def sp_start(self, sp):
        for t in range(R):
            sp.dma_start(self.raw[:, t, :], self.src[t]).then_inc(self.landed[t], 16)

    def sp_tile(self, sp, i, body, t):
        n = i * body + (self.tile0 + t)
        sp.wait_ge(self.lo_done, n + 1)
        sp.dma_start(self.raw[:, t % R, :], self.src[ds(n + (R - self.src0), 1)].rearrange("a p c -> p (a c)"))\
            .then_inc(self.landed[t % R], 16)

    def sp_tiles(self, sp, iters, body):
        with sp.Fori(0, iters) as i:
            for t in range(body):
                self.sp_tile(sp, i, body, t)

    def act_hi(self, act, i, body, t):
        s, n = (t + LEAD) % R, i * body + (self.tile0 + t + LEAD)
        act.wait_ge(self.landed[s], i * (16 * body // R) + 16 * (self.tile0 // R + (t + LEAD) // R + 1))
        act.wait_ge(self.used, n + 1)
        self.nc.scalar.activation(self.whi[:, s, :], self.raw[:, s, :], ACT.Copy).then_inc(self.hi_done, 1)

    def dve_lo(self, dve, i, body, t):
        s, n = (t + LEAD) % R, i * body + (self.tile0 + t + LEAD)
        dve.wait_ge(self.hi_done, n + 1)
        self.nc.vector.tensor_tensor(self.wlo[:, s, :], self.raw[:, s, :], self.whi[:, s, :].bitcast(F32),
                                     ALU.subtract).then_inc(self.lo_done, 1)

    def pe_tile(self, pe, i, body, t, out, xhi, xlo, k0, blocks):
        s = t % R
        pe.wait_ge(self.lo_done, i * body + (self.tile0 + t + 1))
        for kk in range(8):
            k, c = k0 + kk, slice(kk * P, kk * P + P)
            self.nc.tensor.matmul(out, self.whi[:, s, c], xhi[:, k, :], start=(k == 0), stop=False)
            self.nc.tensor.matmul(out, self.whi[:, s, c], xlo[:, k, :], start=False, stop=False)
            last = self.nc.tensor.matmul(out, self.wlo[:, s, c], xhi[:, k, :], start=False, stop=(k == blocks - 1))
        last.then_inc(self.used, 1)

    def tiles_done(self, i, body, t):
        return i * body + (self.tile0 + t + 1 + R)


def ada_phase(N):
    nc, io, body, chunks = N.nc, N.io, ADA_BODY, ADA_FIRST
    N.at = N.arena
    xt = N.keep("x_mix", [P, KB, T], F32)
    N.xt = xt
    cond = N.keep("cond", [P, KB, 2], F32)
    ctanh = N.keep("cond_tanh", [P, KB, 2], F32)
    csilu = N.keep("cond_silu", [P, KB, 2], F32)
    at, N.at = N.at, N.merged_at
    cst = N.cst = N.keep("cond_parts", [P, KB, P], F32R)
    bada = N.b_ada = N.keep("b_ada_sb", [P, 96], F32)
    N.ada_end, N.at = N.at, at
    rows = N.keep("ada_rows", [P, 512], F32)
    four = N.keep("ada_four", [P, 4, 4], F32)
    sq = N.keep("x_squares", [P, 2, 4, T], F32)
    sem = N.sem
    loaded, s_tanh, s_silu, s_chi, s_clo, s_zero = [sem("ada_" + n) for n in ("loaded", "tanh", "silu", "chi", "clo", "zero")]
    consts_in, x_in = sem("consts_in"), sem("x_in")
    s_sq, s_sqsum, s_row, s_tr, s_four, s_add = [
        sem("ada_" + n) for n in ("squares", "sqsum", "row", "tr", "four", "add")]
    N.ada_sems, N.ada0 = (s_row, s_tr, s_four, s_add), chunks
    with nc.Block() as block:
        @block.sync
        def _(sp):
            sp.dma_start(cond[:, :, :], io.cond).then_inc(loaded, 16)
            sp.dma_start(N.ident[:, :], io.ident).then_inc(consts_in, 16)
            sp.dma_start(N.gains[:, :, :], io.gains).then_inc(consts_in, 16)
            sp.dma_start(bada[:, :], io.b_ada).then_inc(consts_in, 16)
            N.sp_start(sp)
            sp.dma_start(xt[:, :, :], io.x).then_inc(x_in, 16)
            N.sp_tiles(sp, chunks, body)

        @block.gpsimd
        def _(pool):
            nc.gpsimd.memset(cst[:, :, :].bitcast(F32), 0.0).then_inc(s_zero, 1)
            nc.gpsimd.memset(N.ones[:, :], 1.0).then_inc(s_zero, 1)

        @block.scalar
        def _(act):
            nc.scalar.sem_inc(s_four, 1)
            act.wait_ge(loaded, 16)
            nc.scalar.activation(ctanh[:, :, :], cond[:, :, :], ACT.Tanh, scale=0.5).then_inc(s_tanh, 1)
            for t in range(-LEAD, 0):
                N.act_hi(act, 0, body, t)
            act.wait_ge(s_silu, 1)
            act.wait_ge(s_zero, 1)
            nc.scalar.activation(cst[:, :, 0:2], csilu[:, :, :], ACT.Copy).then_inc(s_chi, 1)
            act.wait_ge(x_in, 16)
            for b in range(4):
                if b >= 2:
                    act.wait_ge(s_sqsum, b - 1)
                nc.scalar.activation(sq[:, b % 2], xt[:, 4 * b:4 * b + 4, :], ACT.Square).then_inc(s_sq, 1)

            def chunk(i, first):
                for t in range(body):
                    N.act_hi(act, i, body, t)
                    if t == 1 and not first:
                        act.wait_ge(s_tr, i)
                        nc.scalar.activation(four[:, :, :], N.bank[6][:, :].rearrange("p (a b) -> p a b", a=4)[:, :, 0:4],
                                             ACT.Copy).then_inc(s_four, 1)
                act.wait_ge(N.used, N.tiles_done(i, body, body - 1))
                nc.scalar.activation(rows[:, :], N.bank[0][:, :], ACT.Copy).then_inc(s_row, 1)
            chunk(0, True)
            with act.Fori(1, chunks) as i:
                chunk(i, False)
            act.wait_ge(s_tr, chunks)
            nc.scalar.activation(four[:, :, :], N.bank[6][:, :].rearrange("p (a b) -> p a b", a=4)[:, :, 0:4],
                                 ACT.Copy).then_inc(s_four, 1)

        @block.vector
        def _(dve):
            st = N.steps(dve)
            dve.wait_ge(s_tanh, 1)
            st.chain(nc.vector.scalar_tensor_tensor(out=csilu[:, :, :], in0=ctanh[:, :, :], scalar=1.0, in1=cond[:, :, :],
                                                    op0=ALU.add, op1=ALU.mult))
            nc.vector.tensor_scalar(csilu[:, :, :], csilu[:, :, :], 0.5, None, ALU.mult).then_inc(s_silu, 1)
            for t in range(-LEAD, 0):
                N.dve_lo(dve, 0, body, t)
            dve.wait_ge(s_silu, 1)
            dve.wait_ge(s_chi, 1)
            nc.vector.tensor_tensor(cst[:, :, 2:4], csilu[:, :, :], cst[:, :, 0:2].bitcast(F32), ALU.subtract)\
                .then_inc(s_clo, 1)

            def chunk(i, first):
                for t in range(body):
                    N.dve_lo(dve, i, body, t)
                    if t == 3 and not first:
                        dve.wait_ge(s_four, i + 1)
                        nc.vector.tensor_tensor(N.mods[:, ds(i * 4 - 4, 4), :], four[:, :, 0:2], four[:, :, 2:4],
                                                ALU.add).then_inc(s_add, 1)
            chunk(0, True)
            dve.wait_ge(s_sqsum, 4)
            st.chain(nc.vector.tensor_scalar(N.rs_v[:, :], N.bank[7][:, 0:T], 1.0 / D, EPS, ALU.mult, ALU.add))
            rsqrt_steps(dve, nc, st, N.rs_v[:, :], N.rstd[:, :], N.rs_t[:, :])
            with dve.Fori(1, chunks) as i:
                chunk(i, False)
            dve.wait_ge(s_four, chunks + 1)
            dve.wait_ge(consts_in, 48)
            nc.vector.tensor_tensor(N.mods[:, 4 * chunks - 4:4 * chunks, :], four[:, :, 0:2], four[:, :, 2:4], ALU.add).then_inc(s_add, 1)
            dve.wait_ge(s_add, chunks)
            done = slice(0, 4 * chunks)
            st.chain(nc.vector.tensor_tensor(N.mods[:, done, :], N.mods[:, done, :],
                                             bada[:, done].unsqueeze(2).to_broadcast([P, 4 * chunks, 2]), ALU.add))

        @block.tensor
        def _(pe):
            nc.tensor.sem_inc(N.used, R)
            pe.wait_ge(s_zero, 2)
            for b in range(4):
                pe.wait_ge(s_sq, b + 1)
                for k in range(4):
                    last = nc.tensor.matmul(N.bank[7][:, 0:T], N.ones[:, :], sq[:, b % 2, k, :],
                                            start=(b + k == 0), stop=(b * 4 + k == KB - 1))
                last.then_inc(s_sqsum, 1)
            pe.wait_ge(s_clo, 1)
            pe.wait_ge(consts_in, 48)

            def transposes(i):
                pe.wait_ge(s_row, i)
                pe.wait_ge(s_four, i)
                for q in range(4):
                    last = nc.tensor.transpose(N.bank[6][:, q * P:q * P + P], rows[:, q * P:q * P + P], N.ident[:, :])
                last.then_inc(s_tr, 1)

            def chunk(i, first):
                for t in range(body):
                    pe.wait_ge(N.lo_done, i * body + (N.tile0 + t + 1))
                    if t == 0 and not first:
                        pe.wait_ge(s_row, i)
                    for kk in range(2):
                        k, c = 2 * t + kk, slice(kk * 512, kk * 512 + 512)
                        nc.tensor.matmul(N.bank[0][:, :], cst[:, k, :], N.whi[:, t % R, c], start=(k == 0), stop=False)
                        last = nc.tensor.matmul(N.bank[0][:, :], cst[:, k, :], N.wlo[:, t % R, c],
                                                start=False, stop=(k == KB - 1))
                    last.then_inc(N.used, 1)
                    if t == 1 and not first:
                        transposes(i)
            chunk(0, True)
            with pe.Fori(1, chunks) as i:
                chunk(i, False)
            transposes(chunks)
    N.tile0 += chunks * body


def among(own, pattern):
    n = {"own": 0, "ada": 0}
    order = []
    for c in pattern:
        kind = "ada" if c == "a" else "own"
        order.append((kind, n[kind]))
        n[kind] += 1
    assert n == {"own": own, "ada": ADA_BODY}
    return order


MERGE_ORDER = among(12, "ooo" "aaa" "ooo" "aaa" "ooo" "aa" "ooo")
OUT_ORDER = among(8, "oo" "aaa" "oo" "aaa" "oo" "aa" "oo")


def ada_product(N, pe, i, body, t, a):
    nc = N.nc
    pe.wait_ge(N.lo_done, i * body + (N.tile0 + t + 1))
    if a == 0:
        pe.wait_ge(N.ada_sems[0], i + N.ada0)
    for kk in range(2):
        k, c = 2 * a + kk, slice(kk * 512, kk * 512 + 512)
        nc.tensor.matmul(N.bank[7][:, :], N.cst[:, k, :], N.whi[:, t % R, c], start=(k == 0), stop=False)
        last = nc.tensor.matmul(N.bank[7][:, :], N.cst[:, k, :], N.wlo[:, t % R, c], start=False, stop=(k == KB - 1))
    last.then_inc(N.used, 1)


def ada_row(N, act, i, body, t):
    act.wait_ge(N.used, N.tiles_done(i, body, t))
    N.nc.scalar.activation(N.ada_rows[:, :], N.bank[7][:, :], ACT.Copy).then_inc(N.ada_sems[0], 1)


def ada_transposes(N, pe, i):
    s_row, s_tr, s_four, _s_add = N.ada_sems
    pe.wait_ge(s_row, i + (N.ada0 + 1))
    pe.wait_ge(s_four, i + (N.ada0 + 1))
    for q in range(4):
        last = N.nc.tensor.transpose(N.bank[6][:, q * P:q * P + P], N.ada_rows[:, q * P:q * P + P], N.ident[:, :])
    last.then_inc(s_tr, 1)


def ada_turned(N, act, i):
    _s_row, s_tr, s_four, s_add = N.ada_sems
    act.wait_ge(s_tr, i + (N.ada0 + 1))
    act.wait_ge(s_add, i + N.ada0)
    N.nc.scalar.activation(N.ada_four[:, :, :], N.bank[6][:, :].rearrange("p (a b) -> p a b", a=4)[:, :, 0:4], ACT.Copy)\
        .then_inc(s_four, 1)


def ada_add(N, dve, st, i):
    _s_row, _s_tr, s_four, s_add = N.ada_sems
    m = N.mods[:, ds(i * 4 + 4 * N.ada0, 4), :]
    dve.wait_ge(s_four, i + (N.ada0 + 2))
    st.chain(N.nc.vector.tensor_tensor(m, N.ada_four[:, :, 0:2], N.ada_four[:, :, 2:4], ALU.add))
    N.nc.vector.tensor_tensor(m, m, N.b_ada[:, ds(i * 4 + 4 * N.ada0, 4)].unsqueeze(2).to_broadcast([P, 4, 2]), ALU.add)\
        .then_inc(s_add, 1)


def modulate_phase(N, part, gain, name):
    nc = N.nc
    tmp = N.keep("mod_tmp" + name, [P, 4, T], F32)
    s_a, s_t, s_hi, s_lo = [N.sem(name + n) for n in ("_a", "_t", "_hi", "_lo")]
    with nc.Block() as block:
        @block.vector
        def _(dve):
            st = N.steps(dve)
            scale = N.mods[:, (part + 1) * KB:(part + 2) * KB, :]
            st.chain(nc.vector.scalar_tensor_tensor(
                out=N.mod_a[:, :, :], in0=scale, scalar=1.0,
                in1=N.gains[:, gain, :].unsqueeze(2).to_broadcast([P, KB, 2]), op0=ALU.add, op1=ALU.mult))

            def low(k):
                dve.wait_ge(s_hi, 2 * k + 2)
                for g, (a, b) in enumerate(SEG):
                    nc.vector.scalar_tensor_tensor(
                        out=N.hlo[:, k, a:b], in0=tmp[:, k % 4, a:b], scalar=N.mods[:, part * KB + k, g:g + 1],
                        in1=N.hhi[:, k, a:b].bitcast(F32), op0=ALU.add, op1=ALU.subtract).then_inc(s_lo, 1)
            for k in range(KB):
                if k >= 4:
                    dve.wait_ge(s_lo, 2 * k - 6)
                for g, (a, b) in enumerate(SEG):
                    nc.vector.scalar_tensor_tensor(
                        out=tmp[:, k % 4, a:b], in0=N.xt[:, k, a:b], scalar=N.mod_a[:, k, g:g + 1],
                        in1=N.rstd[:, a:b], op0=ALU.mult, op1=ALU.mult).then_inc(s_t, 1)
                if k >= 2:
                    low(k - 2)
            low(KB - 2)
            low(KB - 1)

        @block.scalar
        def _(act):
            for k in range(KB):
                act.wait_ge(s_t, 2 * k + 2)
                for g, (a, b) in enumerate(SEG):
                    nc.scalar.activation(N.hhi[:, k, a:b], tmp[:, k % 4, a:b], ACT.Identity,
                                         bias=N.mods[:, part * KB + k, g:g + 1], scale=1.0).then_inc(s_hi, 1)


def start_credits(N):
    N.evac, N.blk0 = N.sem("block_evacuated"), 0
    N.gate_read, N.out_read, N.m0 = N.sem("gate_bank_read"), N.sem("out_bank_read"), 0
    with N.nc.Block() as block:
        @block.scalar
        def _(act):
            N.nc.scalar.sem_inc(N.evac, 2)
            N.nc.scalar.sem_inc(N.gate_read, 2)

        @block.vector
        def _(dve):
            N.nc.vector.sem_inc(N.out_read, 2)


def pe_blocks(N, pe, iters):
    with pe.Fori(0, iters) as i:
        for t in range(4):
            if t % 2 == 0:
                pe.wait_ge(N.evac, i * 2 + (N.blk0 + t // 2 + 1))
            N.pe_tile(pe, i, 4, t, N.bank[t // 2][:, 0:T], N.hhi, N.hlo, 8 * (t % 2), KB)


def ssd_in_phase(N):
    nc, io = N.nc, N.io
    N.at = N.arena
    S = N.S = {}
    S["z"] = z = N.keep("ssd_z", [P, 8, T], F32)
    S["xs_at"] = N.at
    S["xs"] = xs = N.keep("ssd_xbc", [P, 12, T], F32)
    S["d"] = dskip = N.keep("d_skip_sb", [P, 8], F32)
    S["end1"] = N.at
    PADW = T + 8
    pad = N.keep("xbc_padded", [P, 2, PADW], F32)
    acc = N.keep("conv_sums", [P, 2, PADW - 4], F32)
    th = N.keep("conv_tanh", [P, 2, PADW - 4], F32)
    cw = N.keep("conv_weights", [P, 12, 6], F32)
    wdt = N.keep("w_dt_raw", [P, KB, 32], F32)
    wdh = N.keep("w_dt_hi", [P, KB, P], F32R)
    wdl = N.keep("w_dt_lo", [P, KB, P], F32R)
    sem = N.sem
    s_ld, s_zero, s_dhi, s_dlo, s_dt = [sem("sin_" + n) for n in ("loads", "zero", "dthi", "dtlo", "dt")]
    s_conv, s_fin, s_tanh, s_z, s_zt = [sem("sin_" + n) for n in ("conv", "xs", "tanh", "z", "ztanh")]
    t0 = N.tile0
    with nc.Block() as block:
        @block.sync
        def _(sp):
            sp.dma_start(wdt[:, :, :], io.w_dt).then_inc(s_ld, 16)
            sp.dma_start(cw[:, :, :], io.conv).then_inc(s_ld, 16)
            sp.dma_start(dskip[:, :], io.d_skip).then_inc(s_ld, 16)
            N.sp_tiles(sp, 6, 4)
            N.tile0 += 24
            N.sp_tiles(sp, 4, 4)
            N.tile0 = t0
            sp.wait_ge(s_ld, 48)

        @block.gpsimd
        def _(pool):
            nc.gpsimd.memset(wdh[:, :, :].bitcast(F32), 0.0).then_inc(s_zero, 1)
            nc.gpsimd.memset(wdl[:, :, :].bitcast(F32), 0.0).then_inc(s_zero, 1)
            nc.gpsimd.memset(pad[:, :, :], 0.0).then_inc(s_zero, 1)

        @block.scalar
        def _(act):
            act.wait_ge(s_ld, 48)
            act.wait_ge(s_zero, 3)
            nc.scalar.activation(wdh[:, :, 0:32], wdt[:, :, :], ACT.Copy).then_inc(s_dhi, 1)
            with act.Fori(0, 6) as i:
                for t in range(4):
                    N.act_hi(act, i, 4, t)
                    if t % 2 == 1:
                        b = t // 2
                        act.wait_ge(s_conv, i * 2 + (b + 1))
                        act.wait_ge(N.used, N.tiles_done(i, 4, t))
                        nc.scalar.activation(pad[:, b, 2:2 + T_CTX], N.bank[b][:, 0:T_CTX], ACT.Copy)
                        nc.scalar.activation(pad[:, b, 6 + T_CTX:6 + T], N.bank[b][:, T_CTX:T], ACT.Copy)\
                            .then_inc(N.evac, 1)
                    if t >= 2:
                        b = t - 2
                        act.wait_ge(s_conv, i * 2 + (b + 3))
                        nc.scalar.activation(th[:, b, :], acc[:, b, :], ACT.Tanh, scale=0.5).then_inc(s_tanh, 1)
            N.tile0 += 24
            act.wait_ge(s_fin, 4 + 24)
            with act.Fori(0, 4) as i:
                for t in range(4):
                    N.act_hi(act, i, 4, t)
                    if t % 2 == 1:
                        b = t // 2
                        act.wait_ge(s_z, i * 2 + (b + 1))
                        act.wait_ge(N.used, N.tiles_done(i, 4, t))
                        nc.scalar.activation(th[:, b, 0:T], N.bank[b][:, 0:T], ACT.Tanh, scale=0.5).then_inc(s_zt, 1)
                        nc.scalar.activation(z[:, ds(i * 2 + b, 1), :].rearrange("p a c -> p (a c)"), N.bank[b][:, 0:T],
                                             ACT.Copy).then_inc(N.evac, 1)
            N.tile0 = t0

        @block.vector
        def _(dve):
            nc.vector.sem_inc(s_conv, 2)
            nc.vector.sem_inc(s_z, 2)
            nc.vector.sem_inc(s_fin, 4)
            dve.wait_ge(s_dhi, 1)
            nc.vector.tensor_tensor(wdl[:, :, 0:32], wdt[:, :, :], wdh[:, :, 0:32].bitcast(F32), ALU.subtract)\
                .then_inc(s_dlo, 1)
            st = N.steps(dve)
            with dve.Fori(0, 6) as i:
                st.enter(i, 10)
                for t in range(4):
                    N.dve_lo(dve, i, 4, t)
                    if t % 2 == 1:
                        b = t // 2
                        dve.wait_ge(N.evac, i * 2 + (N.blk0 + b + 3))
                        dve.wait_ge(s_fin, i * 4 + (2 * b + 2))
                        w = lambda k: cw[:, ds(i * 2 + b, 1), k:k + 1].rearrange("p a c -> p (a c)")
                        st.chain(nc.vector.tensor_scalar(acc[:, b, :], pad[:, b, 0:T + 4], w(0), w(5), ALU.mult, ALU.add))
                        for k in range(1, 5):
                            ins = nc.vector.scalar_tensor_tensor(out=acc[:, b, :], in0=pad[:, b, k:k + T + 4], scalar=w(k),
                                                                 in1=acc[:, b, :], op0=ALU.mult, op1=ALU.add)
                            if k < 4:
                                st.chain(ins)
                            else:
                                ins.then_inc(s_conv, 1)
                    if t >= 2:
                        b = t - 2
                        dve.wait_ge(s_tanh, i * 2 + (b + 1))
                        st.chain(nc.vector.tensor_scalar(th[:, b, :], th[:, b, :], 0.5, 0.5, ALU.mult, ALU.add))
                        for (o, (lo, hi)) in zip((0, 4), SEG):
                            nc.vector.tensor_tensor(
                                xs[:, ds(i * 2 + b, 1), lo:hi].rearrange("p a c -> p (a c)"),
                                acc[:, b, lo + o:hi + o], th[:, b, lo + o:hi + o], ALU.mult).then_inc(s_fin, 1)
                st.leave(6)
            N.tile0 += 24
            with dve.Fori(0, 4) as i:
                for t in range(4):
                    N.dve_lo(dve, i, 4, t)
                    if t % 2 == 1:
                        b = t // 2
                        dve.wait_ge(N.evac, i * 2 + (N.blk0 + 12 + b + 3))
                        zb = z[:, ds(i * 2 + b, 1), :].rearrange("p a c -> p (a c)")
                        nc.vector.scalar_tensor_tensor(out=zb, in0=th[:, b, 0:T], scalar=1.0, in1=zb,
                                                       op0=ALU.add, op1=ALU.mult).then_inc(s_z, 1)
            N.tile0 = t0

        @block.tensor
        def _(pe):
            pe.wait_ge(s_dlo, 1)
            for k in range(KB):
                nc.tensor.matmul(N.bank[7][:, 0:T], wdh[:, k, :], N.hhi[:, k, :], start=(k == 0), stop=False)
                nc.tensor.matmul(N.bank[7][:, 0:T], wdh[:, k, :], N.hlo[:, k, :], start=False, stop=False)
                last = nc.tensor.matmul(N.bank[7][:, 0:T], wdl[:, k, :], N.hhi[:, k, :], start=False, stop=(k == KB - 1))
            last.then_inc(s_dt, 1)
            pe_blocks(N, pe, 6)
            N.tile0, N.blk0 = N.tile0 + 24, N.blk0 + 12
            pe_blocks(N, pe, 4)
            N.tile0, N.blk0 = t0, N.blk0 - 12
            pe.wait_ge(s_dt, 1)
    N.tile0 += 40
    N.blk0 += 20


def ssd_scan_phase(N):
    nc, io, S = N.nc, N.io, N.S
    z, xs, dskip = S["z"], S["xs"], S["d"]
    N.at = S["end1"]
    sem = N.sem
    xtok = N.keep("x_tok", [P, NCH, 1024], F32)
    btok = N.keep("B_tok", [P, NCH, 256], F32)
    h0 = N.keep("h0", [P, 2, 2, 256], F32)
    s1s = [N.keep("mid_state", [P, 256], F32)]
    cbm = N.keep("CB_masked", [P, 2, T], F32)
    stout = N.keep("ctx_states", [P, 2, 2, 256], F32)
    tri = N.keep("tri", [P, 2, P], F32)
    wt = N.keep("decay_w", [P, 4, 2], F32)
    dttok = N.keep("dt_tok", [P, NCH, 32], F32)
    cstok = N.keep("cs_tok", [P, NCH, 32], F32)
    aexp = N.keep("a_exp", [P, 32], F32)
    dbias = N.keep("dt_bias_sb", [32, 1], F32)
    ecs = [N.keep("C_decayed", [P, 4, T_LAT], F32)]
    xds = [N.keep("x_dt", [P, NCH, 256], F32)]
    xdds = [N.keep("x_dt_decay", [P, 2, 256], F32)]
    csb_at, N.at = N.at, N.ada_end
    s1s.append(N.keep("mid_state_odd", [P, 256], F32))
    ecs.append(N.keep("C_decayed_odd", [P, 4, T_LAT], F32))
    xds.append(N.keep("x_dt_odd", [P, NCH, 256], F32))
    xdds.append(N.keep("x_dt_decay_odd", [P, 2, 256], F32))
    assert N.at <= N.merged_at + KB * T * 4
    N.at = csb_at
    csb = N.keep("cs_rows_bc", [P, 2, 4, T], F32)
    N.at = csb_at
    dv, du, ds_, dq, dp, dr, dsp = [N.keep("dt_" + n, [32, T], F32) for n in ("v", "u", "s", "q", "p", "r", "sp")]
    rows_f, rows_b = N.rs_t, N.rs_v
    N.at = S["xs_at"]
    S["hi"] = ohi = N.keep("ssd_out_hi", [P, 8, T], F32R)
    S["lo"] = olo = N.keep("ssd_out_lo", [P, 8, T], F32R)
    (s_ld, s_v, s_abs, s_exp, s_dtr, s_tp, s_dttok, s_aexp, s_atok, s_cs, s_cstok, s_rows, s_rowst, s_x2t, s_xtok) = [
        sem("sc_" + n) for n in ("loads", "v", "abs", "exp", "dtr", "dtT", "dttok", "aexp", "atok", "cs", "cstok",
                                 "rows", "rows_stored", "xT", "xtok")]
    s_csb = [sem("sc_csb0"), sem("sc_csb1")]
    (s_cb, s_cbm, s_ec, s_wsub, s_wexp, s_xd, s_xdd, s_st, s_s1, s_stout, s_cd, s_d, s_dexp, s_m, s_y, s_gated, s_sq, s_sqs,
     s_norm, s_ohi, s_olo, s_sto) = [
        sem("sc_" + n) for n in ("cb", "cbm", "ec", "wsub", "wexp", "xd", "xdd", "st", "s1", "stout", "cd", "d", "dexp", "m",
                                 "y", "gated", "sq", "sqs", "norm", "ohi", "olo", "states_out")]
    B = N.bank
    steps = [(g, dr_) for g in range(SSD_G) for dr_ in range(2)]
    MID, END, NEXT = (1, 2), (127, 128), (2, 1)

    def ybank(g, pp):
        return B[2 + 2 * (g % 2) + pp]

    with nc.Block() as block:
        @block.sync
        def _(sp):
            sp.dma_start(dbias[:, :], io.dt_bias).then_inc(s_ld, 16)
            sp.dma_start(aexp[:, :], io.a_log.partition_broadcast(P)).then_inc(s_ld, 16)
            sp.dma_start(tri[:, :, :], io.tri).then_inc(s_ld, 16)
            sp.dma_start(h0[:, :, :, :], io.h0).then_inc(s_ld, 16)
            sp.wait_ge(s_rows, 2)
            sp.dma_start(io.scratch[0:16, :], rows_f[0:16, :]).then_inc(s_rowst, 16)
            sp.dma_start(io.scratch[16:32, :], rows_b[16:32, :]).then_inc(s_rowst, 16)
            sp.wait_ge(s_rowst, 32)
            for n, (g, d) in enumerate(steps):
                if n >= 2:
                    sp.wait_ge(s_y, n - 1)
                r0 = 16 * d + 4 * g
                sp.dma_start(csb[:, n % 2].rearrange("p a c -> p (a c)"),
                             io.scratch[r0:r0 + 4, :].rearrange("a c -> (a c)").partition_broadcast(P))\
                    .then_inc(s_csb[n % 2], 16)
            sp.wait_ge(s_stout, 8)
            sp.dma_start(io.states, stout[:, :, :, :]).then_inc(s_sto, 16)
            sp.wait_ge(s_sto, 16)
            sp.wait_ge(s_ld, 64)

        @block.tensor
        def _(pe):
            for f in range(6):
                for q in range(4):
                    last = nc.tensor.transpose(B[f][:, q * P:q * P + P], xs[:, 4 * (f % 2) + q, (f // 2) * P:(f // 2 + 1) * P],
                                               N.ident[:, :])
                last.then_inc(s_x2t, 1)
            for f in range(2):
                pe.wait_ge(s_xtok, f + 1)
                for q in range((4, 2)[f]):
                    c, b = (2 * f + q // 2), 8 + q % 2
                    last = nc.tensor.transpose(B[f][:, q * P:q * P + P], xs[:, b, c * P:(c + 1) * P], N.ident[:, :])
                last.then_inc(s_x2t, 1)
            pe.wait_ge(s_dtr, 1)
            for c in range(NCH):
                last = nc.tensor.transpose(B[6][:, c * 32:c * 32 + 32], dsp[:, c * P:(c + 1) * P], N.ident[0:32, 0:32])
            last.then_inc(s_tp, 1)
            pe.wait_ge(s_atok, 1)
            pe.wait_ge(s_ld, 64)
            pe.wait_ge(s_xtok, 8)
            for c in range(NCH):
                for d in range(2):
                    last = nc.tensor.matmul(B[6][:, 128 + c * 32 + 16 * d:128 + c * 32 + 16 * d + 16], tri[:, d, :],
                                            cstok[:, c, 16 * d:16 * d + 16], start=True, stop=True)
            last.then_inc(s_cs, 1)
            for d in range(2):
                for c in range(NCH):
                    last = nc.tensor.matmul(B[4 + d][0:32, c * P:(c + 1) * P], cstok[:, c, :], tri[:, d, :],
                                            start=True, stop=True)
                last.then_inc(s_cs, 1)
            for n, (g, d) in enumerate(steps):
                ec, xd, xdd, s1 = ecs[n % 2], xds[n % 2], xdds[n % 2], s1s[n % 2]
                pb, gg = 64 * (g % 2), g // 2
                rows = slice(pb, pb + 64)
                if d == 0:
                    if g == 0:
                        pe.wait_ge(s_rows, 2)
                    pe.wait_ge(s_cbm, 2 * g)
                    for c in range(NCH):
                        last = nc.tensor.matmul(B[0][:, c * P:(c + 1) * P], xs[rows, 8 + gg, c * P:(c + 1) * P],
                                                xs[rows, 10 + gg, c * P:(c + 1) * P], start=True, stop=True)
                    last.then_inc(s_cb, 1)
                pe.wait_ge(s_xdd, n + 1)
                pe.wait_ge(s_stout, n)
                pe.wait_ge(s_s1, n)
                nc.tensor.matmul(B[1][rows, 0:256], btok[:, 0, g * 64:g * 64 + 64], xdd[:, 0, :], start=True, stop=True)
                nc.tensor.matmul(B[6][rows, 0:256], btok[:, MID[d], g * 64:g * 64 + 64], xdd[:, 1, :], start=True,
                                 stop=True).then_inc(s_st, 1)
                pe.wait_ge(s_gated, 2 * max(g - 1, 0))
                pe.wait_ge(s_m, n + 1)
                for hh in range(4):
                    y = ybank(g, hh // 2)[64 * (hh % 2):64 * (hh % 2) + 64, :]
                    for c in range(NCH):
                        nc.tensor.matmul(y[:, c * P:(c + 1) * P], xd[:, c, hh * 64:hh * 64 + 64],
                                         csb[:, n % 2, hh, c * P:(c + 1) * P], start=(c == 0 and d == 0), stop=(c == 0 and d == 1),
                                         skip_group_check=True)
                pe.wait_ge(s_cd, n + 1)
                for hh in range(4):
                    y = ybank(g, hh // 2)[64 * (hh % 2):64 * (hh % 2) + 64, :]
                    first, nxt = MID[d], NEXT[d]
                    nc.tensor.matmul(y[:, first * P:(first + 1) * P], h0[rows, gg, d, hh * 64:hh * 64 + 64],
                                     ec[rows, hh, (first - 1) * P:first * P], start=False, stop=False, skip_group_check=True)
                    last = nc.tensor.matmul(y[:, nxt * P:(nxt + 1) * P], s1[rows, hh * 64:hh * 64 + 64],
                                            ec[rows, hh, (nxt - 1) * P:nxt * P], start=False, stop=(d == 1),
                                            skip_group_check=True)
                last.then_inc(s_y, 1)
            for b in range(8):
                pe.wait_ge(s_sq, b + 1)
                last = nc.tensor.matmul(B[0][:, 0:T], N.ones[:, :], xs[:, b, :], start=(b == 0), stop=(b == 7))
            last.then_inc(s_sqs, 1)

        @block.scalar
        def _(act):
            A = nc.scalar.activation
            act.wait_ge(s_v, 1)
            A(du[:, :], dv[:, :], ACT.Abs).then_inc(s_abs, 1)
            act.wait_ge(s_abs, 1)
            A(du[:, :], du[:, :], ACT.Exp, scale=-1.0).then_inc(s_exp, 1)
            act.wait_ge(s_ld, 64)
            A(aexp[:, :], aexp[:, :], ACT.Exp).then_inc(s_aexp, 1)
            for f in range(6):
                act.wait_ge(s_x2t, f + 1)
                A(xtok[:, f // 2, 512 * (f % 2):512 * (f % 2) + 512], B[f][:, :], ACT.Copy).then_inc(s_xtok, 1)
            act.wait_ge(s_x2t, 7)
            A(btok[:, 0:2, :], B[0][:, :], ACT.Copy).then_inc(s_xtok, 1)
            act.wait_ge(s_x2t, 8)
            A(btok[:, 2, :], B[1][:, 0:256], ACT.Copy).then_inc(s_xtok, 1)
            act.wait_ge(s_tp, 1)
            A(dttok[:, :, :], B[6][:, 0:96], ACT.Copy).then_inc(s_dttok, 1)
            act.wait_ge(s_cs, 1)
            act.wait_ge(s_cs, 3)
            A(cstok[:, :, :], B[6][:, 128:224], ACT.Copy).then_inc(s_cstok, 1)
            A(rows_f[0:32, :], B[4][0:32, 0:T], ACT.Copy).then_inc(s_rows, 1)
            A(rows_b[0:32, :], B[5][0:32, 0:T], ACT.Copy).then_inc(s_rows, 1)
            for n, (g, d) in enumerate(steps):
                ec, xd, xdd, s1 = ecs[n % 2], xds[n % 2], xdds[n % 2], s1s[n % 2]
                pb, gg = 64 * (g % 2), g // 2
                rows = slice(pb, pb + 64)
                act.wait_ge(s_csb[n % 2], 16 * (n // 2 + 1))
                if n >= 2:
                    act.wait_ge(s_y, n - 1)
                A(ec[rows, :, :], csb[rows, n % 2, :, T_CTX:T], ACT.Exp).then_inc(s_ec, 1)
                act.wait_ge(s_wsub, n + 1)
                A(wt[:, :, :], wt[:, :, :], ACT.Exp).then_inc(s_wexp, 1)
                act.wait_ge(s_d, n + 1)
                A(csb[:, n % 2], csb[:, n % 2], ACT.Exp).then_inc(s_dexp, 1)
                act.wait_ge(s_st, n + 1)
                A(stout[rows, gg, d, :], B[1][rows, 0:256], ACT.Copy).then_inc(s_stout, 1)
            for b in range(8):
                act.wait_ge(s_gated, b + 1)
                if b == 0:
                    act.wait_ge(s_gated, 8)
                A(xs[:, b, :], z[:, b, :], ACT.Square).then_inc(s_sq, 1)
            for b in range(8):
                act.wait_ge(s_norm, b + 1)
                A(ohi[:, b, :], z[:, b, :], ACT.Copy, scale=0.5).then_inc(s_ohi, 1)

        @block.vector
        def _(dve):
            V = nc.vector
            st = N.steps(dve)
            dve.wait_ge(s_ld, 64)
            V.tensor_scalar(dv[:, :], B[7][0:32, 0:T], dbias[:, 0:1], None, ALU.add).then_inc(s_v, 1)
            dve.wait_ge(s_exp, 1)
            st.chain(V.tensor_scalar(dr[:, :], du[:, :], 2.0, None, ALU.add))
            st.chain(V.reciprocal(dr[:, :], dr[:, :]))
            st.chain(V.tensor_tensor(ds_[:, :], du[:, :], dr[:, :], ALU.mult))
            st.chain(V.tensor_tensor(dq[:, :], ds_[:, :], ds_[:, :], ALU.mult))
            st.chain(V.tensor_scalar(dp[:, :], dq[:, :], 1.0 / 17.0, None, ALU.mult))
            for k in (15, 13, 11, 9, 7, 5, 3):
                st.chain(V.scalar_tensor_tensor(out=dp[:, :], in0=dp[:, :], scalar=1.0 / k, in1=dq[:, :], op0=ALU.add, op1=ALU.mult))
            st.chain(V.scalar_tensor_tensor(out=dp[:, :], in0=dp[:, :], scalar=1.0, in1=ds_[:, :], op0=ALU.add, op1=ALU.mult))
            dve.wait_ge(s_v, 1)
            st.chain(V.tensor_scalar(dv[:, :], dv[:, :], 0.0, None, ALU.max))
            V.scalar_tensor_tensor(out=dsp[:, :], in0=dp[:, :], scalar=2.0, in1=dv[:, :], op0=ALU.mult, op1=ALU.add)\
                .then_inc(s_dtr, 1)
            dve.wait_ge(s_aexp, 1)
            dve.wait_ge(s_dttok, 1)
            V.scalar_tensor_tensor(out=cstok[:, :, :], in0=dttok[:, :, :], scalar=-1.0,
                                   in1=aexp[:, :].unsqueeze(1).to_broadcast([P, NCH, 32]), op0=ALU.mult, op1=ALU.mult)\
                .then_inc(s_atok, 1)
            dve.wait_ge(s_cstok, 1)

            def gate(g):
                dve.wait_ge(s_y, 2 * g + 2)
                for pp in range(2):
                    b = 2 * g + pp
                    st.chain(V.scalar_tensor_tensor(out=xs[:, b, :], in0=xs[:, b, :], scalar=dskip[:, b:b + 1],
                                                    in1=ybank(g, pp)[:, 0:T], op0=ALU.mult, op1=ALU.add))
                    V.tensor_tensor(z[:, b, :], z[:, b, :], xs[:, b, :], ALU.mult).then_inc(s_gated, 1)
            for n, (g, d) in enumerate(steps):
                ec, xd, xdd, s1 = ecs[n % 2], xds[n % 2], xdds[n % 2], s1s[n % 2]
                pb, gg = 64 * (g % 2), g // 2
                rows = slice(pb, pb + 64)
                hs = slice(16 * d + 4 * g, 16 * d + 4 * g + 4)
                row = csb[:, n % 2]
                ends = row[:, :, 127:T:P] if d == 0 else row[:, :, 0:T:P]
                pick = slice(0, 2) if d == 0 else slice(0, 3, 2)
                if d == 0:
                    dve.wait_ge(s_cb, g + 1)
                    if n:
                        dve.wait_ge(s_m, n)
                    for dd in range(2):
                        V.tensor_tensor(cbm[:, dd, :], B[0][:, 0:T],
                                        tri[:, dd:dd + 1, :].to_broadcast([P, NCH, P]), ALU.mult).then_inc(s_cbm, 1)
                dve.wait_ge(s_csb[n % 2], 16 * (n // 2 + 1))
                if n:
                    dve.wait_ge(s_xdd, n)
                st.chain(V.tensor_tensor(wt[:, :, :], ends[:, :, pick], cstok[:, pick, hs].rearrange("p c h -> p h c"),
                                         ALU.subtract))
                V.tensor_scalar(wt[:, :, :], wt[:, :, :], 0.0, None, ALU.min).then_inc(s_wsub, 1)
                dve.wait_ge(s_ec, n + 1)
                if n >= 2:
                    dve.wait_ge(s_y, n - 1)
                V.tensor_tensor(xd[:, :, :].rearrange("p c (h q) -> p c h q", h=4),
                                xtok[:, :, g * 256:g * 256 + 256].rearrange("p c (h q) -> p c h q", h=4),
                                dttok[:, :, hs].unsqueeze(3).to_broadcast([P, NCH, 4, HD]), ALU.mult).then_inc(s_xd, 1)
                dve.wait_ge(s_wexp, n + 1)
                dve.wait_ge(s_xd, n + 1)
                V.tensor_tensor(xdd[:, :, :].rearrange("p c (h q) -> p c h q", h=4),
                                xd[:, pick, :].rearrange("p c (h q) -> p c h q", h=4),
                                wt[:, :, :].rearrange("p h c -> p c h").unsqueeze(3).to_broadcast([P, 2, 4, HD]),
                                ALU.mult).then_inc(s_xdd, 1)
                st.chain(V.tensor_tensor(row.rearrange("p h (c l) -> p h c l", c=NCH), row.rearrange("p h (c l) -> p h c l", c=NCH),
                                         cstok[:, :, hs].rearrange("p c h -> p h c").unsqueeze(3).to_broadcast([P, 4, NCH, P]),
                                         ALU.subtract))
                V.tensor_scalar(row, row, 0.0, None, ALU.min).then_inc(s_d, 1)
                st.chain(V.tensor_tensor(s1[rows, :].rearrange("p (h q) -> p h q", h=4),
                                         h0[rows, gg, d, :].rearrange("p (h q) -> p h q", h=4),
                                         ec[rows, :, END[d]:END[d] + 1].to_broadcast([64, 4, HD]), ALU.mult))
                dve.wait_ge(s_st, n + 1)
                V.tensor_tensor(s1[rows, :], s1[rows, :], B[6][rows, 0:256], ALU.add).then_inc(s_s1, 1)
                dve.wait_ge(s_s1, n + 1)
                V.tensor_tensor(ec[rows, :, :], ec[rows, :, :],
                                xs[rows, 10 + gg, T_CTX:T].unsqueeze(1).to_broadcast([64, 4, T_LAT]), ALU.mult).then_inc(s_cd, 1)
                dve.wait_ge(s_dexp, n + 1)
                V.tensor_tensor(row, row, cbm[:, d:d + 1, :].to_broadcast([P, 4, T]), ALU.mult).then_inc(s_m, 1)
                if d == 0 and g > 0:
                    gate(g - 1)
            gate(SSD_G - 1)
            dve.wait_ge(s_sqs, 1)
            st.chain(V.tensor_scalar(N.rs_v[:, :], B[0][:, 0:T], 1.0 / 4096, EPS, ALU.mult, ALU.add))
            rsqrt_steps(dve, nc, st, N.rs_v[:, :], N.rstd[:, :], N.rs_t[:, :])
            for b in range(8):
                V.scalar_tensor_tensor(out=z[:, b, :], in0=z[:, b, :], scalar=N.gains[:, 3, b:b + 1], in1=N.rstd[:, :],
                                       op0=ALU.mult, op1=ALU.mult).then_inc(s_norm, 1)
            for b in range(8):
                dve.wait_ge(s_ohi, b + 1)
                V.scalar_tensor_tensor(out=olo[:, b, :], in0=z[:, b, :], scalar=0.5, in1=ohi[:, b, :].bitcast(F32),
                                       op0=ALU.mult, op1=ALU.subtract).then_inc(s_olo, 1)


def ada_settle_phase(N):
    nc, parts, b_ada = N.nc, N.cst, N.b_ada
    N.cst = N.keep_top("cond_parts_kept", [P, KB, P], F32R)
    N.b_ada = N.keep_top("b_ada_kept", [P, 96], F32)
    N.ada_rows = N.keep_top("ada_rows_kept", [P, 512], F32)
    N.ada_four = N.keep_top("ada_four_kept", [P, 4, 4], F32)
    with nc.Block() as block:
        @block.scalar
        def _(act):
            nc.scalar.activation(N.cst[:, :, :], parts[:, :, :].bitcast(F32), ACT.Copy)

        @block.vector
        def _(dve):
            nc.vector.tensor_copy(N.b_ada[:, :], b_ada[:, :])


def merge_phase(N, ohi, olo, first, name):
    nc, body = N.nc, len(MERGE_ORDER)
    gt = N.keep("gate_tanh_" + name, [P, 2, T], F32)
    mt = N.keep("merge_tmp_" + name, [P, 2, T], F32)
    iters = MERGE_TILES // 12
    ada_end = MERGE_ORDER.index(("ada", ADA_BODY - 1))
    with nc.Block() as block:
        @block.sync
        def _(sp):
            N.sp_tiles(sp, iters, body)

        @block.scalar
        def _(act):
            with act.Fori(0, iters) as i:
                for t, (kind, o) in enumerate(MERGE_ORDER):
                    N.act_hi(act, i, body, t)
                    if kind == "own" and o % 3 == 2:
                        m = o // 3
                        act.wait_ge(N.out_read, i * 4 + (N.m0 + m + 1))
                        act.wait_ge(N.used, N.tiles_done(i, body, t - 1))
                        nc.scalar.activation(gt[:, m % 2, :], N.bank[m % 2][:, 0:T], ACT.Tanh, scale=0.5)\
                            .then_inc(N.gate_read, 1)
                    if t == ada_end + 1:
                        ada_row(N, act, i, body, ada_end)
                ada_turned(N, act, i)

        @block.vector
        def _(dve):
            st = N.steps(dve)
            with dve.Fori(0, iters) as i:
                st.enter(i, 1 if first else 5)
                for t, (kind, o) in enumerate(MERGE_ORDER):
                    N.dve_lo(dve, i, body, t)
                    if kind == "own" and o % 3 == 2:
                        m = o // 3
                        dve.wait_ge(N.gate_read, i * 4 + (N.m0 + m + 3))
                        dve.wait_ge(N.used, N.tiles_done(i, body, t))
                        acc = N.merged[:, ds(i * 4 + m, 1), :].rearrange("p a c -> p (a c)")
                        out = acc if first else mt[:, m % 2, :]
                        nc.vector.scalar_tensor_tensor(out=out, in0=gt[:, m % 2, :], scalar=1.0, in1=N.bank[2 + m % 2][:, 0:T],
                                                       op0=ALU.add, op1=ALU.mult).then_inc(N.out_read, 1)
                        if not first:
                            dve.wait_ge(N.out_read, i * 4 + (N.m0 + m + 3))
                            st.chain(nc.vector.tensor_tensor(acc, acc, mt[:, m % 2, :], ALU.add))
                ada_add(N, dve, st, i)
                st.leave(iters)

        @block.tensor
        def _(pe):
            with pe.Fori(0, iters) as i:
                for t, (kind, o) in enumerate(MERGE_ORDER):
                    if kind == "ada":
                        ada_product(N, pe, i, body, t, o)
                        continue
                    m = o // 3
                    if o % 3 == 0:
                        pe.wait_ge(N.gate_read, i * 4 + (N.m0 + m + 1))
                    if t == body - 1:
                        ada_transposes(N, pe, i)
                    if o % 3 == 2:
                        pe.wait_ge(N.out_read, i * 4 + (N.m0 + m + 1))
                        N.pe_tile(pe, i, body, t, N.bank[2 + m % 2][:, 0:T], ohi, olo, 0, 8)
                    else:
                        N.pe_tile(pe, i, body, t, N.bank[m % 2][:, 0:T], N.hhi, N.hlo, 8 * (o % 3), KB)
    N.tile0 += iters * body
    N.ada0 += iters
    N.m0 += KB


def attn_in_phase(N):
    nc = N.nc
    N.at = N.arena
    S = N.S = {}
    S["hi"] = N.keep("attn_out_hi", [P, 8, T], F32R)
    S["lo"] = N.keep("attn_out_lo", [P, 8, T], F32R)
    S["qkv"] = qkv = N.keep("qkv", [P, ATT_BLOCKS, T], F32)
    block_in_phase(N, qkv, ATT_BLOCKS)


def block_in_phase(N, out, blocks):
    nc, iters = N.nc, blocks // 2
    with nc.Block() as block:
        @block.sync
        def _(sp):
            N.sp_tiles(sp, iters, 4)

        @block.scalar
        def _(act):
            with act.Fori(0, iters) as i:
                for t in range(4):
                    N.act_hi(act, i, 4, t)
                    if t % 2 == 1:
                        b = t // 2
                        act.wait_ge(N.used, N.tiles_done(i, 4, t))
                        nc.scalar.activation(out[:, ds(i * 2 + b, 1), 0:T].rearrange("p a c -> p (a c)"),
                                             N.bank[b][:, 0:T], ACT.Copy).then_inc(N.evac, 1)

        @block.vector
        def _(dve):
            with dve.Fori(0, iters) as i:
                for t in range(4):
                    N.dve_lo(dve, i, 4, t)

        @block.tensor
        def _(pe):
            pe_blocks(N, pe, iters)
    N.tile0 += 2 * blocks
    N.blk0 += blocks


def attn_phase(N):
    nc, io, S = N.nc, N.io, N.S
    qkv, ohi, olo = S["qkv"], S["hi"], S["lo"]
    sem = N.sem
    early = N.at
    pr = N.keep("probs", [P, 4, T], F32)
    late, N.at = N.at, early
    sq = N.keep("head_squares", [P, 2, T], F32)
    sel = N.keep("head_sel", [P, 10, 32], F32)
    selt = N.keep("head_sel_t", [32, 10, P], F32)
    N.at = max(N.at, late)
    cos, sin = N.keep("rope_cos", [P, T_LAT], F32), N.keep("rope_sin", [P, T_LAT], F32)
    rot = N.keep("rope_swap", [P, P], F32)
    qkg = N.keep("qk_gain", [P, 2], F32)
    kf = N.keep("k_all", [P, 2, 512], F32)
    vt = N.keep("v_tok", [P, 4, 256], F32)
    ptl = N.keep("probs_t_lat", [P, 2, 3, T_LAT], F32)
    ptc = N.keep("probs_t_ctx", [P, 2, T_CTX], F32)
    mx, nmx, sm, rc = [N.keep("softmax_" + n, [P, 4], F32) for n in ("max", "bias", "sum", "rec")]
    s_ld, s_sq, s_sqs, s_rs, s_bc, s_nrm, s_rot, s_rope, s_vT, s_v, s_out = [
        sem("at_" + n) for n in ("loads", "sq", "sqs", "rs", "bc", "nrm", "rot", "rope", "vT", "v", "out")]
    s_sc, s_mx, s_nmx, s_exp, s_rc, s_p, s_pt, s_pte, s_pv, s_hi, s_lo = [
        sem("at_" + n) for n in ("scores", "max", "bias", "exp", "rec", "probs", "probsT", "probsT_read", "pv", "hi", "lo")]
    B = N.bank
    units = [(j, a, t) for j in range(8) for a in range(2) for t in range(3)]
    U = len(units)

    def heads_rows(a):
        return slice(64 * a, 64 * a + 64)

    def attn_hi(act, j):
        act.wait_ge(s_pv, 2 * j + 2)
        nc.scalar.activation(ohi[:, j, :], B[5 + j % 2][:, 0:T], ACT.Copy).then_inc(s_hi, 1)

    with nc.Block() as block:
        @block.sync
        def _(sp):
            for dst, src in ((sel[:, :, :], io.head_sel), (selt[:, :, :], io.head_sel_t), (cos[:, :], io.rope[0]),
                             (sin[:, :], io.rope[1]), (rot[:, :], io.rope_swap), (qkg[:, :], io.qk_gain),
                             (kf[:, :, T:512], io.cache_k), (vt[:, 3, :], io.cache_v)):
                sp.dma_start(dst, src).then_inc(s_ld, 16)
            sp.wait_ge(s_nrm, 20)
            sp.dma_start(io.kout, kf[:, :, 0:T_CTX]).then_inc(s_out, 16)
            sp.wait_ge(s_v, 2)
            sp.dma_start(io.vout, vt[:, 0, :]).then_inc(s_out, 16)
            sp.wait_ge(s_out, 32)
            sp.wait_ge(s_ld, 128)

        @block.tensor
        def _(pe):
            pe.wait_ge(s_ld, 128)
            for f in range(2):
                for q in range((4, 2)[f]):
                    c = 2 * f + q // 2
                    last = nc.tensor.transpose(B[5 + f][:, q * P:q * P + P], qkv[:, 10 + q % 2, c * P:(c + 1) * P], N.ident[:, :])
                last.then_inc(s_vT, 1)
            for b in range(10):
                pe.wait_ge(s_sq, b + 1)
                nc.tensor.matmul(B[7][0:32, 0:T], sel[:, b, :], sq[:, b % 2, :], start=(b == 0), stop=(b == 9))\
                    .then_inc(s_sqs, 1)
            pe.wait_ge(s_rs, 1)

            def rotate(b):
                pe.wait_ge(s_nrm, 2 * b + 2)
                if b >= 2:
                    pe.wait_ge(s_rope, b - 1)
                x = qkv[:, b, T_CTX:T] if b < 8 else kf[:, b - 8, T_CTX:T]
                nc.tensor.matmul(B[2 + b % 2][:, 0:T_LAT], rot[:, :], x, start=True, stop=True).then_inc(s_rot, 1)
            for b in range(10):
                if b >= 2:
                    pe.wait_ge(s_nrm, 2 * b - 2)
                nc.tensor.matmul(B[b % 2][:, 0:T], selt[:, b, :], N.rstd[0:32, :], start=True, stop=True).then_inc(s_bc, 1)
                if b >= 1:
                    rotate(b - 1)
            rotate(9)
            pe.wait_ge(s_rope, 10)
            pe.wait_ge(s_v, 2)
            for u in range(U + 5):
                if u < U:
                    j, a, t = units[u]
                    kb, r = j // 4, heads_rows(a)
                    if u >= 3:
                        pe.wait_ge(s_exp, u - 2)
                    keys = kf[r, kb, 0:T_CTX] if t == 0 else kf[r, kb, T_CTX:512]
                    nc.tensor.matmul(B[u % 3][:, 0:(T_CTX if t == 0 else T)], qkv[r, j, t * P:(t + 1) * P], keys,
                                     start=True, stop=True).then_inc(s_sc, 1)
                w = u - 2
                if 0 <= w < U:
                    pe.wait_ge(s_p, w + 1)
                    if w >= 2:
                        pe.wait_ge(s_pte, w - 1)
                    for q in range(1 if units[w][2] == 0 else 3):
                        last = nc.tensor.transpose(B[3 + w % 2][:, q * P:q * P + P], pr[:, w % 4, q * P:q * P + P], N.ident[:, :])
                    last.then_inc(s_pt, 1)
                w = u - 4
                if 0 <= w < U and units[w][2] == 2:
                    j, a, _t = units[w]
                    pe.wait_ge(s_pte, w + 1)
                    if j >= 2 and a == 0:
                        pe.wait_ge(s_lo, j - 1)
                    o, vc = B[5 + j % 2][heads_rows(a), :], (j // 4) * P + 64 * a
                    nc.tensor.matmul(o[:, 0:T_CTX], vt[:, 0, vc:vc + 64], ptc[:, a, :], start=True, stop=True)
                    for q in range(3):
                        last = nc.tensor.matmul(o[:, T_CTX:T], vt[:, 1 + q, vc:vc + 64], ptl[:, a, q, :],
                                                start=(q == 0), stop=(q == 2))
                    last.then_inc(s_pv, 1)

        @block.scalar
        def _(act):
            A = nc.scalar.activation
            for b in range(10):
                if b >= 2:
                    act.wait_ge(s_sqs, b - 1)
                A(sq[:, b % 2, :], qkv[:, b, :], ACT.Square).then_inc(s_sq, 1)
                if b == 3:
                    act.wait_ge(s_vT, 2)
                    A(vt[:, 0:2, :], B[5][:, :], ACT.Copy).then_inc(s_v, 1)
                    A(vt[:, 2, :], B[6][:, 0:256], ACT.Copy).then_inc(s_v, 1)
            for u in range(U + 3):
                if u < U:
                    act.wait_ge(s_nmx, u + 1)
                    if u >= 4:
                        act.wait_ge(s_pt, u - 3)
                    n = T_CTX if units[u][2] == 0 else T
                    A(pr[:, u % 4, 0:n], B[u % 3][:, 0:n], ACT.Exp, bias=nmx[:, u % 4:u % 4 + 1], scale=HD ** -0.5,
                      accum_out=sm[:, u % 4:u % 4 + 1]).then_inc(s_exp, 1)
                w = u - 3
                if 0 <= w < U:
                    j, a, t = units[w]
                    act.wait_ge(s_pt, w + 1)
                    if w // 3 >= 2:
                        act.wait_ge(s_pv, w // 3 - 1)
                    if t == 0:
                        A(ptc[:, a, :], B[3 + w % 2][:, 0:P], ACT.Copy).then_inc(s_pte, 1)
                    else:
                        A(ptl[:, a, :, (t - 1) * P:t * P], B[3 + w % 2][:, 0:T], ACT.Copy).then_inc(s_pte, 1)
                w = u - 9
                if w >= 0 and w % 6 == 0 and w // 6 < 7:
                    attn_hi(act, w // 6)
            attn_hi(act, 7)

        @block.vector
        def _(dve):
            V = nc.vector
            st = N.steps(dve)
            dve.wait_ge(s_sqs, 10)
            st.chain(V.tensor_scalar(N.rs_v[0:32, :], B[7][0:32, 0:T], 1.0 / HD, EPS, ALU.mult, ALU.add))
            rsqrt_steps(dve, nc, st, N.rs_v[0:32, :], N.rstd[0:32, :], N.rs_t[0:32, :])
            nc.vector.sem_inc(s_rs, 1)
            dve.wait_ge(s_ld, 128)

            def rope(b):
                x = qkv[:, b, T_CTX:T] if b < 8 else kf[:, b - 8, T_CTX:T]
                dve.wait_ge(s_rot, b + 1)
                st.chain(V.tensor_tensor(N.rs_t[:, 0:T_LAT], B[2 + b % 2][:, 0:T_LAT], sin[:, :], ALU.mult))
                st.chain(V.tensor_tensor(x, x, cos[:, :], ALU.mult))
                V.tensor_tensor(x, x, N.rs_t[:, 0:T_LAT], ALU.add).then_inc(s_rope, 1)
                dve.wait_ge(s_rope, b + 1)
            for b in range(10):
                dve.wait_ge(s_bc, b + 1)
                for (lo, hi) in SEG:
                    x = qkv[:, b, lo:hi] if b < 8 else kf[:, b - 8, lo:hi]
                    V.scalar_tensor_tensor(out=x, in0=qkv[:, b, lo:hi], scalar=qkg[:, b // 8:b // 8 + 1], in1=B[b % 2][:, lo:hi],
                                           op0=ALU.mult, op1=ALU.mult).then_inc(s_nrm, 1)
                if b >= 1:
                    rope(b - 1)
            rope(9)

            def low(j):
                dve.wait_ge(s_hi, j + 1)
                V.tensor_tensor(olo[:, j, :], B[5 + j % 2][:, 0:T], ohi[:, j, :].bitcast(F32), ALU.subtract).then_inc(s_lo, 1)
            for u in range(U + 1):
                if u < U:
                    n = T_CTX if units[u][2] == 0 else T
                    c = slice(u % 4, u % 4 + 1)
                    dve.wait_ge(s_sc, u + 1)
                    V.reduce_max(mx[:, c], B[u % 3][:, 0:n], AX).then_inc(s_mx, 1)
                    dve.wait_ge(s_mx, u + 1)
                    if u >= 4:
                        dve.wait_ge(s_exp, u - 3)
                    V.tensor_scalar(nmx[:, c], mx[:, c], -(HD ** -0.5), None, ALU.mult).then_inc(s_nmx, 1)
                w = u - 1
                if w >= 0:
                    n = T_CTX if units[w][2] == 0 else T
                    c = slice(w % 4, w % 4 + 1)
                    dve.wait_ge(s_exp, w + 1)
                    V.reciprocal(rc[:, c], sm[:, c]).then_inc(s_rc, 1)
                    dve.wait_ge(s_rc, w + 1)
                    V.tensor_scalar(pr[:, w % 4, 0:n], pr[:, w % 4, 0:n], rc[:, c], None, ALU.mult).then_inc(s_p, 1)
                w = u - 10
                if w >= 0 and w % 6 == 0 and w // 6 < 7:
                    low(w // 6)
            low(7)
    N.at = early


def pool_phase(N):
    nc, io = N.nc, N.io
    N.at = N.arena
    S = N.S = {}
    S["hi"] = ohi = N.keep("pool_out_hi", [P, 8, T], F32R)
    S["lo"] = olo = N.keep("pool_out_lo", [P, 8, T], F32R)
    outputs_end = N.at
    W = 8 + T_CTX + 8 + T_LAT + 8
    pin = N.keep("pool_in", [P, 8, T], F32)
    pad = N.keep("pool_padded", [P, 2, W], F32)
    s2 = N.keep("pool_sums", [P, 2, 2, W], F32)
    inv = N.keep("pool_inv_count", [P, 4, T], F32)
    pw = N.keep("pool_w_sb", [P, 8, 256], F32)
    psc = N.keep("pool_scale_sb", [P, 8], F32)
    dif = N.keep("pool_diff", [P, 2, 2, T], F32)
    block_in_phase(N, pin, POOL_BLOCKS)
    sem = N.sem
    s_ld, s_pad, s_dif, s_mm, s_f, s_hi, s_lo, s_zero = [
        sem("po_" + n) for n in ("loads", "pad", "diff", "mm", "scaled", "hi", "lo", "zero")]
    at = (8, 8 + T_CTX + 8)

    def high(g):
        for e in range(2):
            nc.scalar.wait_ge(s_mm, 2 * g + e + 1)
            nc.scalar.activation(ohi[:, 2 * g + e, :], N.bank[2 * (g % 2) + e][:, 0:T], ACT.Copy,
                                 scale=psc[:, 2 * g + e:2 * g + e + 1]).then_inc(s_hi, 1)

    with nc.Block() as block:
        @block.sync
        def _(sp):
            for dst, src in ((inv[:, :, :], io.pool_inv), (pw[:, :, :], io.pool_w), (psc[:, :], io.pool_scale)):
                sp.dma_start(dst, src).then_inc(s_ld, 16)
            sp.wait_ge(s_ld, 48)

        @block.gpsimd
        def _(pool):
            nc.gpsimd.memset(pad[:, :, :], 0.0).then_inc(s_zero, 1)

        @block.scalar
        def _(act):
            act.wait_ge(s_zero, 1)
            for g in range(4):
                if g >= 1:
                    act.wait_ge(s_dif, 2 * g)
                for (lo, hi), o in zip(SEG, at):
                    nc.scalar.activation(pad[:, :, o:o + hi - lo], pin[:, 2 * g:2 * g + 2, lo:hi], ACT.Copy).then_inc(s_pad, 1)
                if g >= 1:
                    high(g - 1)
            high(3)

        @block.vector
        def _(dve):
            V = nc.vector
            st = N.steps(dve)
            dve.wait_ge(s_ld, 48)

            def low(g):
                for e in range(2):
                    b = 2 * g + e
                    dve.wait_ge(s_hi, b + 1)
                    V.scalar_tensor_tensor(out=olo[:, b, :], in0=N.bank[2 * (g % 2) + e][:, 0:T], scalar=psc[:, b:b + 1],
                                           in1=ohi[:, b, :].bitcast(F32), op0=ALU.mult, op1=ALU.subtract).then_inc(s_lo, 1)
            for g, win in enumerate(POOL_WINDOWS):
                dve.wait_ge(s_pad, 2 * g + 2)
                src, n, w = pad[:, :, :], W, 1
                while w < win:
                    dst = s2[:, (w.bit_length() - 1) % 2]
                    n -= w
                    st.chain(V.tensor_tensor(dst[:, :, 0:n], src[:, :, 0:n], src[:, :, w:w + n], ALU.add))
                    src, w = dst, 2 * w
                if g >= 2:
                    dve.wait_ge(s_mm, 2 * g - 2)
                for (lo, hi), o in zip(SEG, at):
                    st.chain(V.tensor_tensor(dif[:, g % 2, :, lo:hi], src[:, :, o - win // 2:o - win // 2 + hi - lo],
                                             inv[:, g:g + 1, lo:hi].to_broadcast([P, 2, hi - lo]), ALU.mult))
                for (lo, hi), o in zip(SEG, at):
                    V.tensor_tensor(dif[:, g % 2, :, lo:hi], dif[:, g % 2, :, lo:hi], pad[:, :, o:o + hi - lo], ALU.subtract)\
                        .then_inc(s_dif, 1)
                if g >= 1:
                    low(g - 1)
            low(3)

        @block.tensor
        def _(pe):
            pe.wait_ge(s_ld, 48)
            for g in range(4):
                pe.wait_ge(s_dif, 2 * g + 2)
                if g >= 2:
                    pe.wait_ge(s_lo, 2 * g - 2)
                for e in range(2):
                    for k in range(2):
                        last = nc.tensor.matmul(N.bank[2 * (g % 2) + e][:, 0:T], pw[:, 2 * g + k, e * P:(e + 1) * P],
                                                dif[:, g % 2, k, :], start=(k == 0), stop=(k == 1))
                    last.then_inc(s_mm, 1)
    N.at = outputs_end


def split_merged_phase(N):
    nc = N.nc
    s_hi, s_lo, x_in = N.sem("merged_hi"), N.sem("merged_lo"), N.sem("x_again")
    with nc.Block() as block:
        @block.scalar
        def _(act):
            for b in range(4):
                nc.scalar.activation(N.hhi[:, 4 * b:4 * b + 4, :], N.merged[:, 4 * b:4 * b + 4, :], ACT.Copy, scale=0.5)\
                    .then_inc(s_hi, 1)

        @block.vector
        def _(dve):
            for b in range(4):
                q = slice(4 * b, 4 * b + 4)
                dve.wait_ge(s_hi, b + 1)
                nc.vector.scalar_tensor_tensor(out=N.hlo[:, q, :], in0=N.merged[:, q, :], scalar=0.5,
                                               in1=N.hhi[:, q, :].bitcast(F32), op0=ALU.mult, op1=ALU.subtract)\
                    .then_inc(s_lo, 1)

        @block.sync
        def _(sp):
            for b in range(4):
                sp.wait_ge(s_lo, b + 1)
                sp.dma_start(N.merged[:, 4 * b:4 * b + 4, :], N.io.x[:, 4 * b:4 * b + 4, :]).then_inc(x_in, 16)
            sp.wait_ge(x_in, 64)


def w_out_phase(N):
    nc, xt = N.nc, N.merged
    body, iters = len(OUT_ORDER), KB // 4
    ada_end = OUT_ORDER.index(("ada", ADA_BODY - 1))
    gcol = N.keep("gate1_four", [P, 4, 2], F32)
    s_x, s_g = N.sem("x_updated"), N.sem("gate1_here")
    with nc.Block() as block:
        @block.sync
        def _(sp):
            N.sp_tiles(sp, iters, body)

        @block.scalar
        def _(act):
            with act.Fori(0, iters) as i:
                for t in range(body):
                    N.act_hi(act, i, body, t)
                    if t == ada_end + 1:
                        ada_row(N, act, i, body, ada_end)
                ada_turned(N, act, i)

        @block.vector
        def _(dve):
            nc.vector.sem_inc(s_x, 4)
            st = N.steps(dve)
            with dve.Fori(0, iters) as i:
                st.enter(i, 1)
                dve.wait_ge(s_x, i * 8 + 4)
                nc.vector.tensor_copy(gcol[:, :, :], N.mods[:, ds(i * 4 + 2 * KB, 4), :]).then_inc(s_g, 1)
                dve.wait_ge(s_g, i + 1)
                for t, (kind, o) in enumerate(OUT_ORDER):
                    N.dve_lo(dve, i, body, t)
                    if kind == "own" and o % 2 == 1:
                        b = o // 2
                        dve.wait_ge(N.used, N.tiles_done(i, body, t))
                        for g, (lo, hi) in enumerate(SEG):
                            x = xt[:, ds(i * 4 + b, 1), lo:hi].rearrange("p a c -> p (a c)")
                            nc.vector.scalar_tensor_tensor(out=x, in0=N.bank[b % 2][:, lo:hi], scalar=gcol[:, b, g:g + 1],
                                                           in1=x, op0=ALU.mult, op1=ALU.add).then_inc(s_x, 1)
                ada_add(N, dve, st, i)
                st.leave(iters)

        @block.tensor
        def _(pe):
            with pe.Fori(0, iters) as i:
                for t, (kind, o) in enumerate(OUT_ORDER):
                    if kind == "ada":
                        ada_product(N, pe, i, body, t, o)
                        continue
                    if o % 2 == 0:
                        pe.wait_ge(s_x, i * 8 + (o + 2))
                    if t == body - 1:
                        ada_transposes(N, pe, i)
                    N.pe_tile(pe, i, body, t, N.bank[o // 2 % 2][:, 0:T], N.hhi, N.hlo, 8 * (o % 2), KB)
    N.tile0 += iters * body
    N.ada0 += iters
    N.top = nc.sbuf_usable_end // 32 * 32


def norm_phase(N, name):
    nc, xt = N.nc, N.merged
    sq = N.keep("squares_" + name, [P, 2, 4, T], F32)
    s_sq, s_sum = [N.sem(name + n) for n in ("_squares", "_sums")]
    with nc.Block() as block:
        @block.scalar
        def _(act):
            for b in range(4):
                if b >= 2:
                    act.wait_ge(s_sum, b - 1)
                nc.scalar.activation(sq[:, b % 2], xt[:, 4 * b:4 * b + 4, :], ACT.Square).then_inc(s_sq, 1)

        @block.tensor
        def _(pe):
            for b in range(4):
                pe.wait_ge(s_sq, b + 1)
                for k in range(4):
                    last = nc.tensor.matmul(N.bank[7][:, 0:T], N.ones[:, :], sq[:, b % 2, k, :],
                                            start=(b + k == 0), stop=(b * 4 + k == KB - 1))
                last.then_inc(s_sum, 1)

        @block.vector
        def _(dve):
            st = N.steps(dve)
            dve.wait_ge(s_sum, 4)
            st.chain(nc.vector.tensor_scalar(N.rs_v[:, :], N.bank[7][:, 0:T], 1.0 / D, EPS, ALU.mult, ALU.add))
            rsqrt_steps(dve, nc, st, N.rs_v[:, :], N.rstd[:, :], N.rs_t[:, :])


def rank_steps(st, nc, v, ahead, after, before, rank):
    q = v.shape[1]
    shape = [P, q, 4, 4]
    vi, vj = v.unsqueeze(2).to_broadcast(shape), v.unsqueeze(3).to_broadcast(shape)
    st.did(nc.vector.tensor_tensor(ahead, vi, vj, ALU.is_gt))
    st.chain(nc.vector.tensor_tensor(after, vi, vj, ALU.is_ge))
    st.chain(nc.vector.tensor_tensor(after, after, ahead, ALU.subtract))
    st.chain(nc.vector.tensor_tensor(after, after, before.unsqueeze(1).to_broadcast(shape), ALU.mult))
    st.chain(nc.vector.tensor_tensor(ahead, ahead, after, ALU.add))
    st.chain(nc.vector.reduce_sum(rank, ahead, AX))


def router_phase(N):
    nc, io, sem = N.nc, N.io, N.sem
    N.gate_w = N.keep("half_gate_weights", [P, NCH, NE], F32)
    N.slot = N.keep("slot_in_group", [P, NCH, NG], F32)
    N.most = N.keep("most_in_group", [P, 1], I32)
    N.iota = N.keep("slot_numbers", [P, P], F32)
    mark = N.at
    wr = N.keep("w_router_sb", [P, KB, P], F32)
    wrh = N.keep("w_router_hi", [P, KB, P], F32R)
    wrl = N.keep("w_router_lo", [P, KB, P], F32R)
    lt = N.keep("logits_t", [P, T], F32)
    br = N.keep("b_router_sb", [P, NE], F32)
    before = N.keep("index_before", [P, 4, 4], F32)
    tri = N.keep("tri_upto", [P, P], F32)
    ex, sc, bi, wt = [N.keep("router_" + n, [P, NCH * NE], F32) for n in ("exp", "scores", "biased", "weights")]
    ah, af = N.keep("rank_ahead", [P, 12, 4, 4], F32), N.keep("rank_equal", [P, 12, 4, 4], F32)
    rk, sel = N.keep("rank_in_group", [P, 12, 4], F32), N.keep("selected", [P, 12, 4], F32)
    gs, gr, gb = [N.keep("group_" + n, [P, NCH, NG], F32) for n in ("score", "rank", "best")]
    den = N.keep("weight_sum", [P, NCH], F32)
    cm = N.keep("most_f", [P, 1], F32)
    s_ld, s_wh, s_wl, s_lg, s_lt, s_tr, s_ex, s_gb, s_cs = [
        sem("rt_" + n) for n in ("loads", "w_hi", "w_lo", "logits", "logits_sb", "by_token", "exp", "best", "cumsum")]
    s_ht, s_hh, s_hl = sem("h_by_token"), sem("h_by_token_hi"), sem("h_by_token_lo")
    B = N.bank
    with nc.Block() as block:
        @block.sync
        def _(sp):
            for dst, src in ((wr[:, :, :], io.w_router), (br[:, :], io.b_router), (before[:, :, :], io.before),
                             (tri[:, :], io.tri[:, 0, :]), (N.iota[:, :], io.iota)):
                sp.dma_start(dst, src).then_inc(s_ld, 16)
            sp.wait_ge(s_ld, 80)

        @block.scalar
        def _(act):
            act.wait_ge(s_ld, 80)
            nc.scalar.activation(wrh[:, :, :], wr[:, :, :], ACT.Copy).then_inc(s_wh, 1)
            act.wait_ge(s_lg, 1)
            nc.scalar.activation(lt[:, :], B[0][:, 0:T], ACT.Copy).then_inc(s_lt, 1)
            act.wait_ge(s_tr, 1)
            for c in range(NCH):
                nc.scalar.activation(ex[:, c * NE:(c + 1) * NE], B[1][:, c * P:c * P + NE], ACT.Exp, scale=-1.0)\
                    .then_inc(s_ex, 1)
            for k in range(KB):
                act.wait_ge(s_ht, k + 1)
                nc.scalar.activation(N.hhi[:, k, :], B[4 + k % 4][:, 0:T], ACT.Copy).then_inc(s_hh, 1)

        @block.tensor
        def _(pe):
            pe.wait_ge(s_wl, 1)
            for k in range(KB):
                nc.tensor.matmul(B[0][:, 0:T], wrh[:, k, :], N.hhi[:, k, :], start=(k == 0), stop=False)
                nc.tensor.matmul(B[0][:, 0:T], wrh[:, k, :], N.hlo[:, k, :], start=False, stop=False)
                last = nc.tensor.matmul(B[0][:, 0:T], wrl[:, k, :], N.hhi[:, k, :], start=False, stop=(k == KB - 1))
            last.then_inc(s_lg, 1)
            pe.wait_ge(s_lt, 1)
            for c in range(NCH):
                last = nc.tensor.transpose(B[1][:, c * P:(c + 1) * P], lt[:, c * P:(c + 1) * P], N.ident[:, :])
            last.then_inc(s_tr, 1)
            for k in range(KB):
                if k >= 4:
                    pe.wait_ge(s_hl, k - 3)
                for c in range(NCH):
                    o, t = B[4 + k % 4][:, c * P:(c + 1) * P], slice(c * P, (c + 1) * P)
                    nc.tensor.matmul(o, N.hhi[:, k, t].bitcast(F32), N.ident[:, :], start=True, stop=False)
                    last = nc.tensor.matmul(o, N.hlo[:, k, t].bitcast(F32), N.ident[:, :], start=False, stop=True)
                last.then_inc(s_ht, 1)
            pe.wait_ge(s_gb, 1)
            for c in range(NCH):
                for b in range(c + 1):
                    nc.tensor.matmul(B[2][:, c * NG:(c + 1) * NG], (tri if b == c else N.ones)[:, :], gb[:, b, :],
                                     start=(b == 0), stop=(b == c))
            for b in range(NCH):
                last = nc.tensor.matmul(B[3][:, 0:NG], N.ones[:, :], gb[:, b, :], start=(b == 0), stop=(b == NCH - 1))
            last.then_inc(s_cs, 1)

        @block.vector
        def _(dve):
            V = nc.vector
            st = N.steps(dve)
            dve.wait_ge(s_ld, 80)
            dve.wait_ge(s_wh, 1)
            V.tensor_tensor(wrl[:, :, :], wr[:, :, :], wrh[:, :, :].bitcast(F32), ALU.subtract).then_inc(s_wl, 1)

            def lows(k0, k1):
                for k in range(k0, k1):
                    dve.wait_ge(s_hh, k + 1)
                    V.tensor_tensor(N.hlo[:, k, :], B[4 + k % 4][:, 0:T], N.hhi[:, k, :].bitcast(F32), ALU.subtract)\
                        .then_inc(s_hl, 1)
            dve.wait_ge(s_ex, NCH)
            st.chain(V.tensor_scalar(ex[:, :], ex[:, :], 1.0, None, ALU.add))
            st.chain(V.reciprocal(sc[:, :], ex[:, :]))
            lows(0, 2)
            st.chain(V.tensor_tensor(bi[:, :].rearrange("p (c e) -> p c e", c=NCH), sc[:, :].rearrange("p (c e) -> p c e", c=NCH),
                                     br[:, :].unsqueeze(1).to_broadcast([P, NCH, NE]), ALU.add))
            b4 = bi[:, :].rearrange("p (q j) -> p q j", j=4)
            rank_steps(st, nc, b4, ah[:, :, :, :], af[:, :, :, :], before[:, :, :], rk[:, :, :])
            lows(2, 5)
            st.chain(V.tensor_scalar(sel[:, :, :], rk[:, :, :], 1.5, None, ALU.is_lt))
            st.chain(V.tensor_tensor(rk[:, :, :], sel[:, :, :], b4, ALU.mult))
            st.chain(V.reduce_sum(gs[:, :, :].rearrange("p c g -> p (c g)"), rk[:, :, :], AX))
            lows(5, 7)
            rank_steps(st, nc, gs[:, :, :], ah[:, 0:NCH], af[:, 0:NCH], before[:, :, :], gr[:, :, :])
            lows(7, 10)
            V.tensor_scalar(gb[:, :, :], gr[:, :, :], 0.5, None, ALU.is_lt).then_inc(s_gb, 1)
            dve.wait_ge(s_gb, 1)
            st.chain(V.tensor_tensor(sel[:, :, :], sel[:, :, :],
                                     gb[:, :, :].rearrange("p c g -> p (c g)").unsqueeze(2).to_broadcast([P, 12, 4]), ALU.mult))
            lows(10, 12)
            w3 = wt[:, :].rearrange("p (c e) -> p c e", c=NCH)
            st.chain(V.tensor_tensor(wt[:, :], sel[:, :, :].rearrange("p q j -> p (q j)"), sc[:, :], ALU.mult))
            st.chain(V.reduce_sum(den[:, :], w3, AX))
            st.chain(V.reciprocal(den[:, :], den[:, :]))
            st.chain(V.tensor_scalar(den[:, :], den[:, :], 0.5, None, ALU.mult))
            st.chain(V.tensor_tensor(N.gate_w[:, :, :], w3, den[:, :].unsqueeze(2).to_broadcast([P, NCH, NE]), ALU.mult))
            lows(12, KB)
            dve.wait_ge(s_cs, 1)
            st.chain(V.tensor_tensor(N.slot[:, :, :].rearrange("p c g -> p (c g)"), B[2][:, 0:12],
                                     gb[:, :, :].rearrange("p c g -> p (c g)"), ALU.mult))
            st.chain(V.tensor_scalar(N.slot[:, :, :], N.slot[:, :, :], -1.0, None, ALU.add))
            st.chain(V.reduce_max(cm[:, :], B[3][:, 0:NG], AX))
            st.chain(V.tensor_copy(N.most[:, :], cm[:, :]))
    N.at = mark


FF_ORDER = [(kind, j, u) for kind, j in (
    ("gate", 0), ("up", 0), ("gate", 1), ("down", 0), ("up", 1), ("gate", 2), ("down", 1), ("up", 2), ("gate", 3),
    ("up", 3), ("down", 2), ("down", 3)) for u in range(8)]
GATE_END = [FF_ORDER.index(("gate", j, 7)) for j in range(4)]
UP_END = [FF_ORDER.index(("up", j, 7)) for j in range(4)]
ACT_TR = [min(UP_END[j] + 5, FF_ORDER.index(("down", j, 0))) for j in range(4)]
SCATTER_AT = [2, 4, 6, 8, 10, 12, 14, 16, 18, 25, 27, 29, 31, 33, 36, 39]
PICKS = [(1, (24, 25), 26), (0, (27, 28), 29), (0, (31, 33), 34), (0, (35, 36), 37),
         (1, (48, 49), 50), (7, (51, 52), 53), (7, (55, 57), 58), (7, (60, 61), 62)]


class Experts:

    def __init__(self, N):
        sb, sem = N.keep, N.sem
        self.pick = sb("pick", [P, NCH, NG + 2, P], F32R)
        self.place = sb("place", [P, NG + 1, T], F32R)
        self.sr = sb("slot_this_round", [P, NCH, NG], F32)
        self.gws = sb("slot_weights", [P, NG, 4], F32)
        self.gcur = sb("slot_weights_now", [P, 4], F32)
        self.xhi = [sb(f"group_hi{h}", [P, KB, P], F32R) for h in range(2)]
        self.xlo = [sb(f"group_lo{h}", [P, KB, P], F32R) for h in range(2)]
        self.th = sb("ff_tanh", [P, 512], F32)
        self.a1 = sb("ff_silu", [P, 512], F32)
        self.act = sb("ff_act", [P, 512], F32)
        self.ahi = [sb(f"ff_act_hi{h}", [P, 512], F32R) for h in range(2)]
        self.alo = [sb(f"ff_act_lo{h}", [P, 512], F32R) for h in range(2)]
        self.yhi, self.ylo = sb("ff_out_hi", [P, D], F32R), sb("ff_out_lo", [P, D], F32R)
        names = ("picked", "place_tr", "place", "weights", "weights_sb", "steps", "gathered", "group_hi", "group_lo", "tanh",
                 "silu", "act", "act_tr", "act_hi", "act_lo", "y_hi", "y_lo", "scattered", "x_added", "gate_now")
        (self.s_pick, self.s_ptr, self.s_pl, self.s_w, self.s_ws, self.st_sem, self.s_ga, self.s_gh, self.s_gl, self.s_th,
         self.s_si, self.s_act, self.s_at, self.s_ah, self.s_al, self.s_yh, self.s_yl, self.s_sc, self.s_x,
         self.s_gc) = [sem("ff_" + n) for n in names]


def in_round(N, eng, r):
    if r == 0:
        return contextlib.nullcontext()
    return eng.If(eng.value_load(N.most[0:1, 0:1], min_val=0, max_val=T) > P * r)


def expert_round(N, E, r):
    nc, B, body = N.nc, N.bank, NG // 2 * len(FF_ORDER)
    A, V = nc.scalar.activation, nc.vector
    with nc.Block() as block:
        @block.vector
        def _(dve):
            with in_round(N, dve, r):
                st = Steps(dve, E.st_sem)
                st.n = r
                st.chain(V.tensor_scalar(E.sr[:, :, :], N.slot[:, :, :], float(-P * r), None, ALU.add))
                for c in range(NCH):
                    for g in range(NG):
                        V.tensor_scalar(E.pick[:, c, g, :], N.iota[:, :], E.sr[:, c, g:g + 1], None, ALU.is_equal)\
                            .then_inc(E.s_pick, 1)
                dve.wait_ge(E.s_w, r + 1)
                for g in range(NG):
                    V.tensor_copy(E.gws[:, g, :], B[4][:, g * NE + 4 * g:g * NE + 4 * g + 4]).then_inc(E.s_ws, 1)

        @block.gpsimd
        def _(pool):
            if r == 0:
                nc.gpsimd.memset(E.pick[:, :, NG:NG + 2, :].bitcast(F32), 0.0)
                nc.gpsimd.memset(E.place[:, 0:1, :].bitcast(F32), 0.0)

        @block.tensor
        def _(pe):
            with in_round(N, pe, r):
                pe.wait_ge(E.s_pick, 12 * (r + 1))
                for g in range(NG):
                    for c in range(NCH):
                        last = nc.tensor.transpose(B[g][:, c * P:(c + 1) * P], E.pick[:, c, g, :].bitcast(F32), N.ident[:, :])
                    last.then_inc(E.s_ptr, 1)
                for g in range(NG):
                    for c in range(NCH):
                        last = nc.tensor.matmul(B[4][:, g * NE:(g + 1) * NE], E.pick[:, c, g, :].bitcast(F32), N.gate_w[:, c, :],
                                                start=(c == 0), stop=(c == NCH - 1))
                last.then_inc(E.s_w, 1)

        @block.scalar
        def _(act):
            with in_round(N, act, r):
                for g in range(NG):
                    act.wait_ge(E.s_ptr, NG * r + g + 1)
                    A(E.place[:, g + 1, :], B[g][:, 0:T], ACT.Copy).then_inc(E.s_pl, 1)

    g0, y0 = NG * r, (NG + 1) * r
    GL = len(FF_ORDER)

    def picked(i, half):
        return (i * 2 + (y0 + half + 1)) * 8

    def scattered(i, half):
        return (i * 2 + (y0 + half)) * KB

    with nc.Block() as block:
        @block.sync
        def _(sp):
            with in_round(N, sp, r):
                N.sp_tiles(sp, 2, body)
                for s in range(R):
                    sp.wait_ge(N.landed[s], 16 * (N.tile0 // R + 2 * body // R + 1))

        @block.scalar
        def _(act):
            with in_round(N, act, r):
                def group_high(n, p, bank, x):
                    act.wait_ge(E.s_ga, n + (p + 1))
                    A(x[:, 2 * p:2 * p + 2, :], B[bank][:, :].rearrange("p (a b) -> p a b", a=2)[:, :, 0:P], ACT.Copy)\
                        .then_inc(E.s_gh, 1)

                def out_high(i, half, c):
                    act.wait_ge(N.used, N.tiles_done(i, body, half * GL - 1))
                    A(E.yhi[:, c * 512:(c + 1) * 512], B[2 + c][:, :], ACT.Copy).then_inc(E.s_yh, 1)

                def group(i, half):
                    for t in range(GL):
                        N.act_hi(act, i, body, half * GL + t)
                        if t < 4:
                            out_high(i, half, t)
                        for j in range(4):
                            if t == GATE_END[j] + 2:
                                act.wait_ge(N.used, N.tiles_done(i, body, half * GL + GATE_END[j]))
                                act.wait_ge(E.s_si, i * 8 + ((g0 + half) * 4 + j + 1))
                                A(E.th[:, :], B[(0, 7)[j % 2]][:, :], ACT.Tanh, scale=0.5).then_inc(E.s_th, 1)
                            if t == ACT_TR[j]:
                                act.wait_ge(E.s_at, i * 8 + ((g0 + half) * 4 + j + 1))
                                A(E.ahi[j % 2][:, :], B[6][:, :], ACT.Copy).then_inc(E.s_ah, 1)
                        for p, (bank, _tiles, at) in enumerate(PICKS):
                            if t == at:
                                group_high(picked(i, half), p, bank, E.xhi[1 - half])
                for p in range(8):
                    group_high(y0 * 8, p, p % 2, E.xhi[0])
                with act.Fori(0, 2) as i:
                    for half in range(2):
                        group(i, half)
                for c in range(4):
                    out_high(2, 0, c)

        @block.vector
        def _(dve):
            with in_round(N, dve, r):
                if r == 0:
                    V.sem_inc(E.s_act, 1)
                    V.sem_inc(E.s_si, 1)
                    V.sem_inc(E.s_x, 2)

                def group_low(n, p, bank, x, xh):
                    dve.wait_ge(E.s_gh, n + (p + 1))
                    V.tensor_tensor(x[:, 2 * p:2 * p + 2, :], B[bank][:, :].rearrange("p (a b) -> p a b", a=2)[:, :, 0:P],
                                    xh[:, 2 * p:2 * p + 2, :].bitcast(F32), ALU.subtract).then_inc(E.s_gl, 1)

                def out_low(n, c):
                    dve.wait_ge(E.s_yh, n + (c + 1))
                    V.tensor_tensor(E.ylo[:, c * 512:(c + 1) * 512], B[2 + c][:, :], E.yhi[:, c * 512:(c + 1) * 512].bitcast(F32),
                                    ALU.subtract).then_inc(E.s_yl, 1)

                def add_block(n, m, bank=6):
                    if m == 0:
                        dve.wait_ge(E.s_x, n * 2 + 2)
                    dve.wait_ge(E.s_sc, n + (m + 1))
                    for g, (lo, hi) in enumerate(SEG):
                        x = N.merged[:, m, lo:hi]
                        V.scalar_tensor_tensor(out=x, in0=B[bank][:, lo:hi], scalar=N.mods[:, 5 * KB + m, g:g + 1],
                                               in1=x, op0=ALU.mult, op1=ALU.add).then_inc(E.s_x, 1)

                def activate(i, half, j):
                    n = (g0 + half) * 4 + j
                    dve.wait_ge(E.s_act, i * 8 + (n + 1))
                    dve.wait_ge(E.s_th, i * 8 + (n + 1))
                    V.scalar_tensor_tensor(out=E.a1[:, :], in0=E.th[:, :], scalar=1.0, in1=B[(0, 7)[j % 2]][:, :],
                                           op0=ALU.add, op1=ALU.mult).then_inc(E.s_si, 1)
                    dve.wait_ge(E.s_si, i * 8 + (n + 2))
                    dve.wait_ge(N.used, N.tiles_done(i, body, half * GL + UP_END[j]))
                    V.scalar_tensor_tensor(out=E.act[:, :], in0=E.a1[:, :], scalar=E.gcur[:, j:j + 1], in1=B[1][:, :],
                                           op0=ALU.mult, op1=ALU.mult).then_inc(E.s_act, 1)

                def group(i, half):
                    for t in range(GL):
                        N.dve_lo(dve, i, body, half * GL + t)
                        if t < 4:
                            out_low((i * 2 + (y0 + half)) * 4, t)
                        if t == 5:
                            dve.wait_ge(E.s_act, i * 8 + ((g0 + half) * 4 + 1))
                            V.tensor_copy(E.gcur[:, :], E.gws[:, ds(i * 2 + half, 1), :].rearrange("p a c -> p (a c)"))\
                                .then_inc(E.s_gc, 1)
                            dve.wait_ge(E.s_gc, i * 2 + (g0 + half + 1))
                        for m in range(KB):
                            if t == SCATTER_AT[m]:
                                add_block(scattered(i, half), m)
                        for j in range(4):
                            if t == min(UP_END[j] + 2, ACT_TR[j]):
                                activate(i, half, j)
                            if t == ACT_TR[j]:
                                dve.wait_ge(E.s_ah, i * 8 + ((g0 + half) * 4 + j + 1))
                                V.tensor_tensor(E.alo[j % 2][:, :], B[6][:, :], E.ahi[j % 2][:, :].bitcast(F32), ALU.subtract)\
                                    .then_inc(E.s_al, 1)
                        for p, (bank, _tiles, at) in enumerate(PICKS):
                            if t == at:
                                group_low(picked(i, half), p, bank, E.xlo[1 - half], E.xhi[1 - half])
                for p in range(8):
                    group_low(y0 * 8, p, p % 2, E.xlo[0], E.xhi[0])
                with dve.Fori(0, 2) as i:
                    for half in range(2):
                        group(i, half)
                for c in range(4):
                    out_low((NG + y0) * 4, c)
                for m in range(KB):
                    add_block((NG + y0) * KB, m, (6, 7)[m % 2])

        @block.tensor
        def _(pe):
            with in_round(N, pe, r):
                def pick_block(g, k, bank, bl):
                    o = B[bank][:, bl * 256:(bl + 1) * 256]
                    for c in range(NCH):
                        tok = slice(c * P, (c + 1) * P)
                        rhs = E.pick[:, c, ds(g, 2), :].rearrange("p a s -> p (a s)")
                        nc.tensor.matmul(o, N.hhi[:, k, tok], rhs, start=(c == 0), stop=False)
                        last = nc.tensor.matmul(o, N.hlo[:, k, tok], rhs, start=False, stop=(c == NCH - 1))
                    return last

                def scatter(i, half, m, banks=(6,)):
                    n = scattered(i, half)
                    if m % 4 == 0:
                        pe.wait_ge(E.s_yl, (i * 2 + (y0 + half)) * 4 + (m // 4 + 1))
                    pe.wait_ge(E.s_x, n * 2 + (2 * m + 4 - 2 * len(banks)))
                    o, f = B[banks[m % len(banks)]][:, 0:T], slice(m * P, (m + 1) * P)
                    rhs = E.place[:, ds(i * 2 + half, 1), :].rearrange("p a t -> p (a t)")
                    nc.tensor.matmul(o, E.yhi[:, f], rhs, start=True, stop=False)
                    nc.tensor.matmul(o, E.ylo[:, f], rhs, start=False, stop=True).then_inc(E.s_sc, 1)

                def product(i, t, out, parts, k0, first, last):
                    s = t % R
                    pe.wait_ge(N.lo_done, i * body + (N.tile0 + t + 1))
                    for kk in range(2):
                        (xh, xl), w = parts(k0 + kk), slice(kk * 512, kk * 512 + 512)
                        nc.tensor.matmul(out, xh, N.whi[:, s, w], start=(first and kk == 0), stop=False)
                        nc.tensor.matmul(out, xl, N.whi[:, s, w], start=False, stop=False)
                        ins = nc.tensor.matmul(out, xh, N.wlo[:, s, w], start=False, stop=(last and kk == 1))
                    ins.then_inc(N.used, 1)

                def of_group(half):
                    return lambda k: (E.xhi[half][:, k, :], E.xlo[half][:, k, :])

                def of_act(j):
                    return lambda k: (E.ahi[j % 2][:, k * P:(k + 1) * P], E.alo[j % 2][:, k * P:(k + 1) * P])

                def group(i, half):
                    pe.wait_ge(E.s_gl, picked(i, half))
                    for t, (kind, j, u) in enumerate(FF_ORDER):
                        for m in range(KB):
                            if t == SCATTER_AT[m]:
                                scatter(i, half, m)
                        for jj in range(4):
                            if t == ACT_TR[jj]:
                                pe.wait_ge(E.s_x, scattered(i, half) * 2 + (2 * sum(at < t for at in SCATTER_AT) + 2))
                                pe.wait_ge(E.s_act, i * 8 + ((g0 + half) * 4 + jj + 2))
                                for q in range(4):
                                    last = nc.tensor.transpose(B[6][:, q * P:(q + 1) * P], E.act[:, q * P:(q + 1) * P],
                                                               N.ident[:, :])
                                last.then_inc(E.s_at, 1)
                        for p, (bank, tiles, _at) in enumerate(PICKS):
                            if t == tiles[0]:
                                pe.wait_ge(E.s_gl, picked(i, half) + p)
                            if t in tiles:
                                last = pick_block(i * 2 + (half + 1), 2 * p + tiles.index(t), bank, tiles.index(t))
                            if t == tiles[1]:
                                last.then_inc(E.s_ga, 1)
                        if u == 0 and j > 0 and kind != "down":
                            pe.wait_ge(E.s_gl, picked(i, half) + sum(at < t for _b, _t, at in PICKS))
                        if kind == "gate":
                            product(i, half * GL + t, B[(0, 7)[j % 2]][:, :], of_group(half), 2 * u, u == 0, u == 7)
                        elif kind == "up":
                            product(i, half * GL + t, B[1][:, :], of_group(half), 2 * u, u == 0, u == 7)
                        else:
                            if u == 0:
                                pe.wait_ge(E.s_al, i * 8 + ((g0 + half) * 4 + j + 1))
                            if j == 0 and u % 2 == 0:
                                pe.wait_ge(E.s_yl, (i * 2 + (y0 + half)) * 4 + (u // 2 + 1))
                            product(i, half * GL + t, B[2 + u // 2][:, :], of_act(j), 2 * (u % 2), j == 0 and u % 2 == 0,
                                    j == 3 and u % 2 == 1)
                for p in range(8):
                    if p >= 2:
                        pe.wait_ge(E.s_gl, y0 * 8 + p - 1)
                    for bl in range(2):
                        last = pick_block(0, 2 * p + bl, p % 2, bl)
                    last.then_inc(E.s_ga, 1)
                with pe.Fori(0, 2) as i:
                    for half in range(2):
                        group(i, half)
                for m in range(KB):
                    scatter(2, 0, m, (6, 7))
    N.tile0 += 2 * body


def out_phase(N):
    nc, xt = N.nc, N.merged
    s_y, s_out = N.sem("y_ready"), N.sem("y_out")
    with nc.Block() as block:
        @block.vector
        def _(dve):
            for k in range(KB):
                nc.vector.scalar_tensor_tensor(out=xt[:, k, :], in0=xt[:, k, :], scalar=N.gains[:, 2, k:k + 1],
                                               in1=N.rstd[:, :], op0=ALU.mult, op1=ALU.mult).then_inc(s_y, 1)

        @block.sync
        def _(sp):
            for b in range(4):
                sp.wait_ge(s_y, 4 * b + 4)
                sp.dma_start(N.io.y[:, 4 * b:4 * b + 4, :], xt[:, 4 * b:4 * b + 4, :]).then_inc(s_out, 16)
            sp.wait_ge(s_out, 64)


def ffn_phases(N):
    N.at = N.arena
    N.xt = N.merged
    norm_phase(N, "ffn")
    modulate_phase(N, 3, 1, "ffn_in")
    N.at = N.arena
    router_phase(N)
    E = Experts(N)
    N.src = N.io.moe
    for r in range(NCH):
        N.src0 = N.tile0
        expert_round(N, E, r)


def build(nc, io):
    N = Net(nc, io)
    ada_phase(N)
    start_credits(N)
    modulate_phase(N, 0, 0, "mix")
    ssd_in_phase(N)
    ssd_scan_phase(N)
    ada_settle_phase(N)
    merge_phase(N, N.S["hi"], N.S["lo"], True, "ssd")
    attn_in_phase(N)
    attn_phase(N)
    merge_phase(N, N.S["hi"], N.S["lo"], False, "attn")
    pool_phase(N)
    merge_phase(N, N.S["hi"], N.S["lo"], False, "pool")
    N.at = N.arena
    split_merged_phase(N)
    w_out_phase(N)
    ffn_phases(N)
    N.at = N.arena
    norm_phase(N, "final")
    out_phase(N)


def blocks_a(w):
    k, n = w.shape
    return w.reshape(k // 1024, 8, P, n // P, P).transpose(3, 0, 2, 1, 4).reshape(n // P, k // 1024, P, TILE)


def blocks_b(w):
    k, n = w.shape
    return w.reshape(k // 256, 2, P, n // 512, 512).transpose(3, 0, 2, 1, 4).reshape(n // 512, k // 256, P, TILE)


def feature_major(x, blocks):
    return x.T.reshape(blocks, P, -1).transpose(1, 0, 2)


def by_block(v, blocks):
    return v.reshape(blocks, P).T


def lay_out(a):
    f = np.float32
    w_in = a["w_in"][0]
    edges = np.cumsum([0, 1024, 1536, 16, 16, 1024, 256, 256, 1024, 3 * D])
    z, xbc, dtf, dtb, q, k, v, pool, gates = [w_in[:, edges[i]:edges[i + 1]] for i in range(9)]
    q = q.reshape(D, HEADS, HD)[:, Q_HEADS].reshape(D, -1)
    w_attn = a["w_attn_out"][0].reshape(HEADS, HD, D)[Q_HEADS].reshape(-1, D)

    def flat(t):
        return t.reshape(-1, P, TILE)

    ada = flat(blocks_b(a["w_ada"][0]))

    def beside(order, own, chunk):
        n = sum(kind == "own" for kind, _ in order)
        own = own.reshape(-1, n, P, TILE)
        ada_c = ada.reshape(-1, ADA_BODY, P, TILE)[chunk:chunk + len(own)]
        return np.stack([(own if kind == "own" else ada_c)[:, j] for kind, j in order], axis=1).reshape(-1, P, TILE)

    def merge(i, w_out):
        g, o = blocks_a(gates[:, i * D:(i + 1) * D]), blocks_a(w_out)
        return beside(MERGE_ORDER, np.concatenate([g, o], axis=1), ADA_FIRST + 4 * i)

    gate, up, down = [[flat(blocks_b(w[e])) for e in range(NE)]
                      for w in (a["w_gate_ff"][0], a["w_up_ff"][0], a["w_down_ff"][0])]
    dense = np.concatenate([
        ada[:ADA_FIRST * ADA_BODY],
        flat(blocks_a(np.concatenate([xbc, z], axis=1))), merge(0, a["w_ssd_out"][0]),
        flat(blocks_a(np.concatenate([q, k, v], axis=1))), merge(1, w_attn),
        flat(blocks_a(pool)), merge(2, a["w_pool_out"][0]),
        beside(OUT_ORDER, blocks_a(a["w_out"][0]), ADA_FIRST + 12)] + [gate[0][:R]])
    order = [{"gate": gate, "up": up, "down": down}[kind][4 * g + j][u] for g in range(NG) for kind, j, u in FF_ORDER]
    x = np.concatenate([a["x_prompt"][0], a["x_sample"][0]], axis=0)
    gains = np.stack([by_block(a["norm_mix"][0], KB), by_block(a["norm_ffn"][0], KB), by_block(a["norm_final"], KB),
                      np.concatenate([by_block(a["ssd_norm"][0], 8)] * 2, axis=1)], axis=1)
    row, lane = np.arange(P)[:, None], np.arange(P)[None, :]
    tri = np.stack([row <= lane, row >= lane], axis=1).astype(f)
    h0 = np.stack([a["state_ssd_fwd"][0, 0], a["state_ssd_bwd"][0, 0]])
    h0 = h0.reshape(2, 2, 2, 4, HD, HD).transpose(2, 5, 1, 0, 3, 4).reshape(P, 2, 2, 256)
    tok = np.arange(T_LAT)
    inv_freq = np.float32(10000.0) ** (-np.arange(HD // 4, dtype=f) / (HD // 4))
    ang = np.concatenate([(tok // GRID_W).astype(f)[:, None] * inv_freq, (tok % GRID_W).astype(f)[:, None] * inv_freq], axis=1)
    ang = ang[:, (np.arange(P) % HD) // 2].T
    swap = np.zeros((P, P), f)
    even = np.arange(0, P, 2)
    swap[even + 1, even], swap[even, even + 1] = -1, 1
    sel = np.zeros((P, 10, 32), f)
    for b in range(10):
        sel[0:64, b, 2 * b], sel[64:P, b, 2 * b + 1] = 1, 1
    pool_inv = np.zeros((4, T), f)
    for g, w in enumerate(POOL_WINDOWS):
        for lo, hi in SEG:
            t, n_tok = np.arange(hi - lo), hi - lo
            pool_inv[g, lo:hi] = 1.0 / (np.clip(t + w - w // 2, 0, n_tok) - np.clip(t - w // 2, 0, n_tok))
    n = dict(
        w_router=np.concatenate([a["w_router"], np.zeros((D, P - NE), f)], axis=1).reshape(KB, P, P).transpose(1, 0, 2),
        b_router=np.broadcast_to(a["b_router"], (P, NE)), iota=np.broadcast_to(np.arange(P, dtype=f), (P, P)),
        before=np.broadcast_to(np.tri(4, k=-1, dtype=f), (P, 4, 4)),
        head_sel=sel, head_sel_t=sel.transpose(2, 1, 0), rope=np.stack([np.cos(ang), np.sin(ang)]), rope_swap=swap,
        qk_gain=np.stack([np.tile(a["q_norm"][0], 2), np.tile(a["k_norm"][0], 2)], axis=1),
        cache_k=feature_major(a["cache_k"][0, 0].reshape(T_PAST, 256), 2), cache_v=a["cache_v"][0, 0].reshape(T_PAST, 256),
        pool_inv=np.broadcast_to(pool_inv, (P, 4, T)), pool_w=a["pool_w"][0].reshape(8, P, 256).transpose(1, 0, 2),
        pool_scale=by_block(a["pool_scale"][0], 8),
        w_dt=np.concatenate([dtf, dtb], axis=1).reshape(KB, P, 32).transpose(1, 0, 2),
        conv=np.concatenate([a["conv_w"][0], a["conv_b"]]).reshape(6, 12, P).transpose(2, 1, 0),
        d_skip=by_block(np.repeat(a["d_skip"][0], HD), 8),
        dt_bias=a["dt_bias"][0].reshape(32, 1), a_log=a["a_log"][0].reshape(32), tri=tri, h0=h0,
        dense=dense, moe=np.stack(order + order[:R]), x=feature_major(x, KB),
        cond=feature_major(np.stack([a["c_ctx"], a["c"][0]]), KB),
        b_ada=by_block(a["b_ada"][0], 96), gains=gains, ident=np.eye(P, dtype=f),
    )
    return {k: np.ascontiguousarray(v, dtype=f) for k, v in n.items()}


INPUTS = ("x_prompt", "x_sample", "cache_k", "cache_v", "state_ssd_fwd", "state_ssd_bwd", "c", "c_ctx", "w_ada", "b_ada",
          "norm_mix", "norm_ffn", "w_in", "conv_w", "conv_b", "a_log", "dt_bias", "d_skip", "ssd_norm", "q_norm", "k_norm",
          "pool_w", "pool_scale", "w_ssd_out", "w_attn_out", "w_pool_out", "w_out", "w_router", "b_router", "w_gate_ff",
          "w_up_ff", "w_down_ff", "norm_final")
OUTPUTS = (("y", (P, KB, T)), ("kout", (P, 2, T_CTX)), ("vout", (P, 256)), ("states", (P, 2, 2, 256)))


def kernel(**inputs):
    import types as _types
    import concourse.bacc as _bacc
    from concourse.bass_utils import run_bass_kernel_spmd as _run

    laid = lay_out({n: np.asarray(inputs[n]) for n in INPUTS})
    nc = _bacc.Bacc("TRN2", target_bir_lowering=False, num_devices=1)
    aps, arrays = {}, {}
    for n, v in laid.items():
        arrays["in_" + n] = v
        aps[n] = nc.dram_tensor("in_" + n, v.shape, F32, kind="ExternalInput").ap()
    for n, shape in OUTPUTS:
        aps[n] = nc.dram_tensor("out_" + n, shape, F32, kind="ExternalOutput").ap()
    aps["scratch"] = nc.dram_tensor("cs_rows", (32, T), F32, kind="Internal").ap()
    build(nc, _types.SimpleNamespace(**aps))
    res = _run(nc, [arrays], core_ids=[0]).results[0]
    y, k, v, st = [np.asarray(res["out_" + n]) for n, _shape in OUTPUTS]
    y = y.transpose(2, 1, 0).reshape(1, T, D)
    k = k.transpose(2, 1, 0).reshape(1, 1, T_CTX, KV, HD)
    st = st.reshape(2, HD, 2, 2, 4, HD).transpose(3, 2, 0, 4, 5, 1).reshape(2, 1, 1, SSD_H, HD, HD)
    return (np.ascontiguousarray(y[:, :T_CTX]), np.ascontiguousarray(y[:, T_CTX:]), np.ascontiguousarray(k),
            v.reshape(1, 1, T_CTX, KV, HD), np.ascontiguousarray(st[0]), np.ascontiguousarray(st[1]))
```
